# Optimizing a Trainium2 kernel written in Bass

```python
import jax
import jax.numpy as jnp
from jax import lax

D_MODEL = 2048
BATCH = 1
SEQ = 512
DEPTH = 2
DEC_BATCH = 8
DEC_SEQ = 4
PAST_LEN = 2048
PAGE_SIZE = 128

N_META = 16
N_A_LAYERS = DEPTH // 2
N_B_LAYERS = DEPTH - N_A_LAYERS
GLA_HEADS = 4
GLA_KEY_DIM = D_MODEL // 2
GLA_VAL_DIM = D_MODEL
GLA_DK = GLA_KEY_DIM // GLA_HEADS
GLA_DV = GLA_VAL_DIM // GLA_HEADS
GATE_RANK = 16
GATE_LOGIT_NORM = 16.0
GLA_CHUNK = 64
GLA_IN_WIDTH = 2 * GLA_KEY_DIM + 2 * GLA_VAL_DIM + GATE_RANK
HEAD_DIM = 64
N_Q_HEADS = D_MODEL // HEAD_DIM
N_KV_HEADS = 8
GROUP = N_Q_HEADS // N_KV_HEADS
Q_WIDTH = N_Q_HEADS * HEAD_DIM
KV_WIDTH = N_KV_HEADS * HEAD_DIM
WINDOW = 128
BLOCK = 128
RMS_EPS = 1e-6
NEG_INF = -1e30

kernel_name = 'yoco_gla_swa_sink_step'

def rmsnorm(x, g):
    xf = x.astype(jnp.float32)
    y = xf * lax.rsqrt(jnp.mean(xf * xf, axis=-1, keepdims=True) + RMS_EPS)
    return (y * g.astype(jnp.float32)).astype(x.dtype)

def gla_recurrence(q, k, v, g, s0, chunk):
    B, L, H, _ = q.shape
    DV = v.shape[-1]
    pad = (-L) % chunk
    if pad:
        widths = ((0, 0), (pad, 0), (0, 0), (0, 0))
        q, k, v, g = (jnp.pad(t, widths) for t in (q, k, v, g))
    n = (L + pad) // chunk

    def to_chunks(t):
        return t.reshape(B, n, chunk, H, t.shape[-1]).transpose(1, 0, 3, 2, 4)

    tri = jnp.tril(jnp.ones((chunk, chunk), dtype=bool))

    def step(S, inp):
        qc, kc, vc, gc = inp
        b = jnp.cumsum(gc, axis=2)
        diff = b[:, :, :, None, :] - b[:, :, None, :, :]
        decay = jnp.where(tri[:, :, None], jnp.exp(jnp.minimum(diff, 0.0)), 0.0)
        att = jnp.einsum('bhid,bhjd,bhijd->bhij', qc, kc, decay)
        o = (jnp.einsum('bhij,bhjv->bhiv', att, vc)
             + jnp.einsum('bhid,bhdv->bhiv', qc * jnp.exp(b), S))
        b_last = b[:, :, -1:, :]
        S_new = (S * jnp.exp(b_last[:, :, 0, :])[..., None]
                 + jnp.einsum('bhjd,bhjv->bhdv', kc * jnp.exp(b_last - b), vc))
        return S_new.astype(S.dtype), o.astype(vc.dtype)

    S_fin, o = lax.scan(step, s0, (to_chunks(q), to_chunks(k), to_chunks(v), to_chunks(g)))
    o = o.transpose(1, 0, 3, 2, 4).reshape(B, L + pad, H, DV)[:, pad:]
    return o, S_fin

def gla_layer(x, s0, norm_w, w_in, w_gk2, b_gk2, onorm, w_out, chunk):
    B, L, _ = x.shape
    h = rmsnorm(x, norm_w)
    proj = h @ w_in
    q, k, v, gate, glr = jnp.split(
        proj, [GLA_KEY_DIM, 2 * GLA_KEY_DIM, 2 * GLA_KEY_DIM + GLA_VAL_DIM,
               2 * GLA_KEY_DIM + 2 * GLA_VAL_DIM], axis=-1)
    g = (jax.nn.log_sigmoid((glr @ w_gk2 + b_gk2).astype(jnp.float32))
         / GATE_LOGIT_NORM).astype(x.dtype)
    q = q.reshape(B, L, GLA_HEADS, GLA_DK) * (GLA_DK ** -0.5)
    k = k.reshape(B, L, GLA_HEADS, GLA_DK)
    v = v.reshape(B, L, GLA_HEADS, GLA_DV)
    g = g.reshape(B, L, GLA_HEADS, GLA_DK)
    o, S = gla_recurrence(q, k, v, g, s0, chunk)
    o = rmsnorm(o, onorm).reshape(B, L, GLA_VAL_DIM) * jax.nn.silu(gate)
    return x + o @ w_out, S

def shared_kv(x, norm_kv, w_kv):
    B, L, _ = x.shape
    kv = rmsnorm(x, norm_kv) @ w_kv
    k, v = jnp.split(kv, [KV_WIDTH], axis=-1)
    return (k.reshape(B, L, N_KV_HEADS, HEAD_DIM), v.reshape(B, L, N_KV_HEADS, HEAD_DIM))

def window_mask(qpos, kpos):
    return (kpos >= 0) & (kpos <= qpos) & (qpos - kpos < WINDOW)

def sink_softmax(s, sinks):
    col = jnp.broadcast_to(
        sinks.reshape(N_KV_HEADS, GROUP, 1).astype(jnp.float32), s.shape[:-1])[..., None]
    return jax.nn.softmax(jnp.concatenate([s, col], axis=-1), axis=-1)[..., :-1]

def swa_banded(q, k, v, sinks):
    B, L = q.shape[:2]
    pad = (-L) % BLOCK
    widths = ((0, 0), (pad, 0), (0, 0), (0, 0))
    q, k, v = (jnp.pad(t, widths) for t in (q, k, v))
    Lp = L + pad
    nb = Lp // BLOCK
    qb = q.reshape(B, nb, BLOCK, N_KV_HEADS, GROUP, HEAD_DIM)
    kb = k.reshape(B, nb, BLOCK, N_KV_HEADS, HEAD_DIM)
    vb = v.reshape(B, nb, BLOCK, N_KV_HEADS, HEAD_DIM)

    def with_prev(t):
        prev = jnp.concatenate([jnp.zeros_like(t[:, :1]), t[:, :-1]], axis=1)
        return jnp.concatenate([prev, t], axis=2)

    kc, vc = with_prev(kb), with_prev(vb)
    pos = jnp.arange(Lp, dtype=jnp.int32).reshape(nb, BLOCK) - pad
    kpos = jnp.concatenate([pos - BLOCK, pos], axis=1)
    mask = window_mask(pos[:, :, None], kpos[:, None, :])
    s = jnp.einsum('bnqhgd,bnkhd->bnhgqk', qb, kc).astype(jnp.float32) * (HEAD_DIM ** -0.5)
    s = jnp.where(mask[None, :, None, None], s, NEG_INF)
    p = sink_softmax(s, sinks).astype(v.dtype)
    o = jnp.einsum('bnhgqk,bnkhd->bnqhgd', p, vc)
    return o.reshape(B, Lp, N_Q_HEADS, HEAD_DIM)[:, pad:]

def swa_decode(q, k_all, v_all, sinks):
    Bd, T = q.shape[:2]
    Wc = k_all.shape[1] - T
    qg = q.reshape(Bd, T, N_KV_HEADS, GROUP, HEAD_DIM)
    qpos = PAST_LEN + jnp.arange(T, dtype=jnp.int32)
    kpos = jnp.concatenate([PAST_LEN - Wc + jnp.arange(Wc, dtype=jnp.int32), qpos])
    mask = window_mask(qpos[:, None], kpos[None, :])
    s = jnp.einsum('bqhgd,bkhd->bhgqk', qg, k_all).astype(jnp.float32) * (HEAD_DIM ** -0.5)
    s = jnp.where(mask, s, NEG_INF)
    p = sink_softmax(s, sinks).astype(v_all.dtype)
    o = jnp.einsum('bhgqk,bkhd->bqhgd', p, v_all)
    return o.reshape(Bd, T, N_Q_HEADS, HEAD_DIM)

def swa_layer(x, k, v, norm_w, w_in, sinks, w_out, attend):
    B, L, _ = x.shape
    h = rmsnorm(x, norm_w)
    q, gate = jnp.split(h @ w_in, [Q_WIDTH], axis=-1)
    o = attend(q.reshape(B, L, N_Q_HEADS, HEAD_DIM), k, v, sinks).reshape(B, L, Q_WIDTH)
    return x + (o * jax.nn.silu(gate)) @ w_out

def trunk(x, gla_s0, gla_chunk, attend, norm_a, w_in_a, w_gk2_a, b_gk2_a, onorm_a,
          w_out_a, norm_kv, w_kv, norm_b, w_in_b, sinks_b, w_out_b, norm_f):
    finals = []
    k_sh = None
    v_sh = None
    for layer in range(DEPTH):
        if layer < N_A_LAYERS:
            i = layer
            x, s = gla_layer(x, gla_s0[i], norm_a[i], w_in_a[i], w_gk2_a[i], b_gk2_a[i],
                             onorm_a[i], w_out_a[i], gla_chunk)
            finals.append(s)
            if layer == N_A_LAYERS - 1:
                k_sh, v_sh = shared_kv(x, norm_kv, w_kv)
        else:
            j = layer - N_A_LAYERS
            x = swa_layer(x, k_sh, v_sh, norm_b[j], w_in_b[j], sinks_b[j], w_out_b[j], attend)
    return rmsnorm(x, norm_f), jnp.stack(finals), k_sh, v_sh

def setup_inputs(seed: int = 0) -> dict:
    key = jax.random.key(seed)
    ks = jax.random.split(key, 20)

    def nrm(k, shape, scale):
        return jax.random.normal(k, shape, jnp.float32) * scale

    win = min(WINDOW, PAST_LEN)
    return {
        'x_prompt': nrm(ks[0], (BATCH, SEQ, D_MODEL), 1.0),
        'x_sample': nrm(ks[1], (DEC_BATCH, DEC_SEQ, D_MODEL), 1.0),
        'state_gla': nrm(ks[2], (N_A_LAYERS, DEC_BATCH, GLA_HEADS, GLA_DK, GLA_DV), 1.0),
        'cache_k_win': nrm(ks[3], (DEC_BATCH, win, N_KV_HEADS, HEAD_DIM), 1.0),
        'cache_v_win': nrm(ks[4], (DEC_BATCH, win, N_KV_HEADS, HEAD_DIM), 1.0),
        'meta_tokens': nrm(ks[5], (N_META, D_MODEL), 1.0),
        'norm_a': 1.0 + nrm(ks[6], (N_A_LAYERS, D_MODEL), 0.02),
        'w_in_a': nrm(ks[7], (N_A_LAYERS, D_MODEL, GLA_IN_WIDTH), D_MODEL ** -0.5),
        'w_gk2_a': nrm(ks[8], (N_A_LAYERS, GATE_RANK, GLA_KEY_DIM), GATE_RANK ** -0.5),
        'b_gk2_a': nrm(ks[9], (N_A_LAYERS, GLA_KEY_DIM), 0.02),
        'onorm_a': 1.0 + nrm(ks[10], (N_A_LAYERS, GLA_DV), 0.02),
        'w_out_a': nrm(ks[11], (N_A_LAYERS, GLA_VAL_DIM, D_MODEL), GLA_VAL_DIM ** -0.5),
        'norm_kv': 1.0 + nrm(ks[12], (D_MODEL,), 0.02),
        'w_kv': nrm(ks[13], (D_MODEL, 2 * KV_WIDTH), D_MODEL ** -0.5),
        'norm_b': 1.0 + nrm(ks[14], (N_B_LAYERS, D_MODEL), 0.02),
        'w_in_b': nrm(ks[15], (N_B_LAYERS, D_MODEL, 2 * Q_WIDTH), D_MODEL ** -0.5),
        'sinks_b': nrm(ks[16], (N_B_LAYERS, N_Q_HEADS), 1.0),
        'w_out_b': nrm(ks[17], (N_B_LAYERS, Q_WIDTH, D_MODEL), Q_WIDTH ** -0.5),
        'norm_f': 1.0 + nrm(ks[18], (D_MODEL,), 0.02),
    }

def reference(x_prompt, x_sample, state_gla, cache_k_win, cache_v_win, meta_tokens,
              norm_a, w_in_a, w_gk2_a, b_gk2_a, onorm_a, w_out_a, norm_kv, w_kv,
              norm_b, w_in_b, sinks_b, w_out_b, norm_f):
    win = cache_k_win.shape[1]
    B = x_prompt.shape[0]
    meta = jnp.broadcast_to(meta_tokens[None].astype(x_prompt.dtype), (B, N_META, D_MODEL))
    xp = jnp.concatenate([meta, x_prompt], axis=1)
    s0_p = jnp.zeros((N_A_LAYERS, B, GLA_HEADS, GLA_DK, GLA_DV), x_prompt.dtype)
    yp, sgla_p, k_p, v_p = trunk(
        xp, s0_p, GLA_CHUNK, swa_banded, norm_a, w_in_a, w_gk2_a, b_gk2_a, onorm_a,
        w_out_a, norm_kv, w_kv, norm_b, w_in_b, sinks_b, w_out_b, norm_f)
    y_prompt = yp[:, N_META:]
    k_win_p = k_p[:, -win:]
    v_win_p = v_p[:, -win:]

    def attend_sample(q, k, v, sinks):
        return swa_decode(q, jnp.concatenate([cache_k_win, k], axis=1),
                          jnp.concatenate([cache_v_win, v], axis=1), sinks)

    y_sample, sgla_s, k_s, v_s = trunk(
        x_sample, state_gla, x_sample.shape[1], attend_sample, norm_a, w_in_a, w_gk2_a,
        b_gk2_a, onorm_a, w_out_a, norm_kv, w_kv, norm_b, w_in_b, sinks_b, w_out_b, norm_f)
    k_win_s = jnp.concatenate([cache_k_win, k_s], axis=1)[:, -win:]
    v_win_s = jnp.concatenate([cache_v_win, v_s], axis=1)[:, -win:]
    return (y_prompt, y_sample, sgla_p, sgla_s, k_win_p, v_win_p, k_win_s, v_win_s)


_drawn_inputs = setup_inputs


def setup_inputs(seed=0):
    import zlib

    import numpy as np

    out = dict(_drawn_inputs(seed))
    spreads = {}
    factors = {'b_gk2_a': 6.489,
     'onorm_a': 5.239,
     'norm_kv': 2.926,
     'norm_b': 8.0,
     'sinks_b': 64.0,
     'norm_f': 8.055}
    for name, (base, spread) in spreads.items():
        noise = np.random.default_rng([zlib.crc32(name.encode()), seed]).standard_normal(out[name].shape)
        drawn = base * np.exp(spread * noise) if base else spread * noise
        out[name] = jnp.asarray(drawn.astype(out[name].dtype))
    for name, factor in factors.items():
        out[name] = (out[name] * factor).astype(out[name].dtype)
    return out
```

```python
import numpy as np
import concourse.bass as bass
from concourse import mybir
from contextlib import ExitStack

FP32 = mybir.dt.float32
I32 = mybir.dt.int32
ALU = mybir.AluOpType
ACT = mybir.ActivationFunctionType
AX = mybir.AxisListType

P = 128
DM = 2048
NK = DM // P
SEQ, META, DB, DT = 512, 16, 8, 4
SMP = DB * DT
EXT = SMP + META
TOK = SEQ + EXT
HALF = TOK // 2
NT = SEQ // P
HEADS, DK, DV = 4, 256, 512
KT, VT = DK // P, DV // P
RANK = 16
GN = 16.0
KV = 8
GRP = 4
HD = 64
EPS = 1e-6
NEG = -1e30
LEVELS = [64, 32, 16, 8, 4, 2, 1]
NL = len(LEVELS) + 1
NLX = 5
WR = 4
SR = 4
USES = 14
OUT_A = USES * HEADS
KVP = OUT_A + NK
SWA = KVP + 8
OUT_B = SWA + 4 * KV
W_OUT_A = 12 * HEADS
W_KV = W_OUT_A + NK
W_SWA = W_KV + 8
W_OUT_B = W_SWA + 4 * KV


def consts_array():
    parts, where, at = [], {}, 0

    def put(name, a):
        nonlocal at
        full = np.zeros((P, a.shape[1]), np.float32)
        full[:a.shape[0]] = a
        parts.append(full)
        where[name] = (at, at + a.shape[1])
        at += a.shape[1]

    i = np.arange(P)
    put("ident", np.eye(P))
    for h in LEVELS:
        put(f"level{h}", (i[:, None] // (2 * h) == i[None] // (2 * h)) & (i[:, None] % (2 * h) < h)
            & (i[None] % (2 * h) >= h))
    put("level0", np.eye(P))
    e = np.arange(EXT)
    for h in LEVELS[-4:]:
        m = (e[:, None] // (2 * h) == e[None] // (2 * h)) & (e[:, None] % (2 * h) < h) & (e[None] % (2 * h) >= h)
        if 2 * h > DT:
            m &= (e[:, None] >= SMP) & (e[None] >= SMP)
        put(f"ext{h}", m)
    put("ext0", np.eye(EXT))
    put("causal", i[None] <= i[:, None])
    put("causalT", i[:, None] <= i[None])
    put("prevT", i[:, None] > i[None])
    m = np.arange(META)
    put("meta_neg", np.where(m[None] > m[:, None], NEG, 0.0))
    keep = np.ones((P, TOK))
    keep[:, 0:SEQ:P] = 0
    keep[:, SEQ:SEQ + SMP:DT] = 0
    keep[:, SEQ + SMP] = 0
    put("keep", keep)
    row_t, row_s = i % DT, i // (GRP * DT)
    u = np.arange(DT)
    put("new_ok", u[None] <= row_t[:, None])
    put("old_ok", u[None] > row_t[:, None])
    c = np.arange(SMP)
    put("new_block", (c[None] // DT == row_s[:, None]) & (c[None] % DT <= row_t[:, None]))
    put("seq_of", (c[:, None] // DT == np.arange(DB)[None]))
    return np.ascontiguousarray(np.concatenate(parts, 1).astype(np.float32)), where


class Tally:

    def __init__(self, sem, base=0):
        self.sem, self.base, self.n = sem, base, 0

    def inc(self, ins):
        ins.then_inc(self.sem, 1)
        self.n += 1

    @property
    def value(self):
        return self.base + self.n

    def link(self, eng, ins):
        self.inc(ins)
        eng.wait_ge(self.sem, self.value)


def yoco_kernel(nc, I, OUTS):
    ctx = ExitStack()
    _, where = consts_array()
    with ctx:
        def sb(name, shape, dt=FP32):
            return ctx.enter_context(nc.sbuf_tensor(name, shape, dt))

        def sem(name):
            return ctx.enter_context(nc.semaphore(name))

        def sems(name, n):
            return [sem(f"{name}{k}") for k in range(n)]

        H = sb("H", [P, NK, TOK])
        O = sb("O", [P, NK, TOK])
        W = sb("W", [P, WR, NK, P])
        CST = sb("CST", [P, max(b for _, b in where.values())])
        ones = sb("ones", [P, P])
        RB = sb("RB", [P, TOK])
        GV = sb("GV", [P, 76])
        SK = sb("SK", [P, 4 * KV])
        SKR = sb("SKR", [P, KV])
        small = sb("small", [P, 96])
        acc = sb("acc", [P, TOK])

        def C(name, p0=0, p1=P):
            a, b = where[name]
            return CST[p0:p1, a:b]

        ident = C("ident")
        G_A, G_KV, G_B, G_F, B_GK, G_O = 0, 16, 32, 48, 64, 72

        AR = sb("AR", [P, 22700])
        top = [0]

        def take(shape):
            n = int(np.prod(shape))
            v = AR[:, top[0]:top[0] + n]
            top[0] += n
            assert top[0] <= 22700, top
            if len(shape) == 2:
                v = v.rearrange("p (a b) -> p a b", a=shape[0])
            if len(shape) == 3:
                v = v.rearrange("p (a b c) -> p a b c", a=shape[0], b=shape[1])
            return v

        XR = take([5, DM])
        junk = take([DM])
        xt = take([2, TOK])
        NV = take([P])
        diag = take([5, P])
        sx = take([P])
        top[0] = 0
        Dd = take([2, KT * TOK])
        Dd = [Dd[:, n, :].rearrange("p (a b) -> p a b", a=KT) for n in range(2)]
        Tt = take([2, KT * TOK])
        Tt = [Tt[:, n, :].rearrange("p (a b) -> p a b", a=KT) for n in range(2)]
        qT, kT, bT = take([KT, TOK]), take([KT, TOK]), take([KT, TOK])
        kd, qe = Dd[1], Tt[1]
        kdT, kdX = take([NT, DK]), take([DK])
        Vn, Vx, Vs = take([NT, DV]), take([DV]), take([DV])
        TH = take([2, TOK])
        att, attx = take([NT, P]), take([EXT])
        S = take([KT, DV])
        S0 = take([SR, KT, DV])
        o_sb = take([2, VT * P])
        sq = take([VT * P])
        rr, ra, rv, rl = take([P]), take([P]), take([P]), take([P])
        kdm = take([2, DK])
        glr = take([TOK])
        gk2 = take([DK])
        wglr = take([NK, RANK])
        el = take([KT, NT + DB + 1])
        top[0] = 10240
        xs = take([4, TOK])
        sqa = take([2, TOK])
        x2 = take([2, TOK])
        xg = take([2, TOK])
        top[0] = 0
        YR = take([5, DM])
        top[0] = 0
        kdup = take([KV, TOK])
        Wn, Wx, Wm = take([NT, KV * HD]), take([KV * HD]), take([KV * HD])
        THb = take([2, TOK])
        qB = take([2, TOK])
        Cc, Pp = take([2, GRP * P]), take([2, GRP * P])
        PTc, PTp = take([2, GRP * P]), take([2, GRP * P])
        on = take([2, GRP * HD])
        Kc, Vc = take([1, DB * HD]), take([1, DB * HD])
        kcat = take([DB, P + DT])
        kg, vg, vxg, vmg = take([TOK]), take([NT, HD]), take([HD]), take([HD])
        qN = take([2, TOK])
        sm = take([2, 32])
        Qz, Pz = take([DB, P]), take([DB, P])
        Pn, PnT = take([SMP]), take([P])
        kwin, kwx = take([KV * HD]), take([KV * HD])

        PP = [ctx.enter_context(nc.psum_tensor(f"PP{n}", [P, 2, 512], FP32)) for n in range(2)]
        BS = ctx.enter_context(nc.psum_tensor("BS", [P, 2, 512], FP32))
        B0, B1 = BS[:, 0, :], BS[:, 1, :]
        B2, B3 = [ctx.enter_context(nc.psum_tensor(f"B{n}", [P, 512], FP32)) for n in (2, 3)]

        x0T = nc.dram_tensor("x0T", (NK, P, TOK), FP32, kind="Internal").ap()
        x1T = nc.dram_tensor("x1T", (NK, P, TOK), FP32, kind="Internal").ap()

        cst_in, x_in, vec_in = sem("cst_in"), sems("x_in", 5), sem("vec_in")
        w_in = sems("w_in", WR)
        wglr_in, gk2_in = sem("wglr_in"), sem("gk2_in")
        proj_done, pp_free = sem("proj_done"), sems("pp_free", 2)
        setup, sink_rows, passed, stage_step = sem("setup"), sem("sink_rows"), sem("passed"), sem("stage_step")
        vecs_done, vecs_kept = sem("vecs_done"), sem("vecs_kept")
        row_ss, rs_act, rs_dve = sem("row_ss"), sem("rs_act"), sem("rs_dve")
        diag_ready, bc_done, rb_ready = sem("diag_ready"), sem("bc_done"), sem("rb_ready")
        h_ready, x0_out, glr_done, glr_kept = sem("h_ready"), sems("x0_out", 2), sem("glr_done"), sem("glr_kept")
        th_ready, vtr_done, vn_kept = sem("th_ready"), sem("vtr_done"), sem("vn_kept")
        g_act, decay_exp = sem("g_act"), sem("decay_exp")
        d_ready, e_ready, t_ready = sem("d_ready"), sem("e_ready"), sem("t_ready")
        scores_done, scores_kept, attx_ready = sem("scores_done"), sem("scores_kept"), sem("attx_ready")
        kde_ready, kd_ready, qe_ready = sem("kde_ready"), sem("kd_ready"), sem("qe_ready")
        kdtr_done, kdt_ready = sem("kdtr_done"), sem("kdt_ready")
        o_done, o_kept, u_done, s_ready = sem("o_done"), sem("o_kept"), sem("u_done"), sem("s_ready")
        sq_ready, ss_done, r_act, r_dve, o_gated = (sem("sq_ready"), sem("ss_done"), sem("r_act"), sem("r_dve"),
                                                    sem("o_gated"))
        state_out = sem("state_out")
        s0_in, s0_out = sems("s0_in", SR), sems("s0_out", SR)
        extbase, vs_ready, kdm_ready = sem("extbase"), sem("vs_ready"), sem("kdm_ready")
        smp_u, smp_new = sem("smp_u"), sem("smp_new")
        xs_in, sq_a, acc_done, x1_out, acc_zero = (sems("xs_in", 4), sem("sq_a"), sem("acc_done"), sems("x1_out", 4),
                                                   sem("acc_zero"))
        ms_done, n_act, n_dve = sem("ms_done"), sem("n_act"), sem("n_dve")
        kw_done, kw_kept, win_out, vm_in = sem("kw_done"), sem("kw_kept"), sem("win_out"), sem("vm_in")
        thb_ready = sem("thb_ready")
        sc_done, comb, comb_ok, sm_dve, sm_act = sem("sc_done"), sem("comb"), sem("comb_ok"), sem("sm_dve"), sem("sm_act")
        p_ready, pt_done, pt_kept, pv_done, on_ready = (sem("p_ready"), sem("pt_done"), sem("pt_kept"), sem("pv_done"),
                                                        sem("on_ready"))
        ot_done, b_gated = sem("ot_done"), sem("b_gated")
        kc_in, kct_done, kcat_ready, qz_ready, c_fill = (sems("kc_in", 2), sem("kct_done"), sem("kcat_ready"),
                                                         sem("qz_ready"), sem("c_fill"))
        staged, q_copied, o_stat = sem("staged"), sem("q_copied"), sem("o_stat")
        b_step, den_ready, y_scaled_v = sem("b_step"), sem("den_ready"), sem("y_scaled_v")
        xg_ready, yt_done, y_kept, y_scaled, y_out = (sem("xg_ready"), sem("yt_done"),
                                                                sem("y_kept"), sem("y_scaled"), sem("y_out"))

        ds = bass.ds
        COLS = [slice(t * P, (t + 1) * P) for t in range(NT)] + [slice(SEQ, TOK)]
        WID = [P] * NT + [EXT]

        def halves(ap):
            return ap.rearrange("p (c n) -> p c n", c=2)

        def PV(k):
            return PP[k % 2][:, :, 0:HALF]

        def tile(buf, n):
            return buf[:, n, :] if isinstance(n, int) else buf[:, ds(n, 1), :].rearrange("p a n -> p (a n)")

        def bank4(b, w=P):
            return b[:, 0:4 * w].rearrange("p (a n) -> p a n", a=4)

        def own_scores(n=P, w=P):
            return BS[0:n].rearrange("p b (h x) -> p h b x", h=2)[:, :, :, 0:w]

        def old_scores(a=0):
            return BS[:].rearrange("p b (h x) -> p h b x", h=2)[:, :, :, P + a:2 * P]

        def by_head(ap, w=P):
            return ap.rearrange("p (h b n) -> p h b n", h=2, b=2)[:, :, :, 0:w]

        def over(ap, n, axis=1):
            shape = list(ap.shape)
            shape.insert(axis, n)
            return ap.unsqueeze(axis).broadcast_to(shape)

        def alone(eng):
            eng.sem_inc(passed, 1)

        ss_c, ms_c, lg_c, rs_c, nt_c = (small[:, 40 + 5 * k:45 + 5 * k] for k in range(5))
        eps_c = small[:, 65:66]

        block = ctx.enter_context(nc.Block())

        @block.sync
        def _(sp):
            sp.dma_start(CST[:], I["consts"]).then_inc(cst_in, 16)
            for t in range(NT):
                sp.dma_start(XR[:, t, :], I["x_prompt"][0, t * P:(t + 1) * P, :]).then_inc(x_in[t], 16)
            sp.dma_start(XR[0:SMP, NT, :], I["x_sample"].rearrange("b t d -> (b t) d")).then_inc(x_in[NT], 16)
            sp.dma_start(XR[SMP:EXT, NT, :], I["meta_tokens"]).then_inc(x_in[NT], 16)
            rows = ((G_A, "norm_a", NK), (G_B, "norm_b", NK), (B_GK, "b_gk2_a", KT * HEADS), (G_O, "onorm_a", VT))
            for at, name, n in rows:
                sp.dma_start(NV[at:at + n, :], I[name].rearrange("a (n p) -> (a n) p", p=P)).then_inc(vec_in, 16)
            for at, name in ((G_KV, "norm_kv"), (G_F, "norm_f")):
                sp.dma_start(NV[at:at + NK, :], I[name].rearrange("(n p) -> n p", p=P)).then_inc(vec_in, 16)
            sp.dma_start(small[0:1, 0:32], I["sinks_b"]).then_inc(vec_in, 16)
            sp.dma_start(small[0:KV, 32:36], I["sinks_b"].rearrange("a (g r) -> (a g) r", r=GRP)).then_inc(vec_in, 16)
            w_in_a = I["w_in_a"][0].rearrange("(k p) n -> p k n", p=P)
            sp.dma_start(wglr, w_in_a[:, :, 6144:6144 + RANK]).then_inc(wglr_in, 16)

            def weights(j, src, col, freed):
                if freed is not None:
                    sp.wait_ge(proj_done, NK + freed)
                alone(sp)
                sp.dma_start(W[:, j % WR, :, :], src[:, :, ds(col, P)]).then_inc(w_in[j % WR], 16)

            def head_weights(h):
                kinds = [4096 + h * DV, 4096 + h * DV + P, 4096 + h * DV + 2 * P, 4096 + h * DV + 3 * P,
                         2048 + h * DV, 2048 + h * DV + P, 2048 + h * DV + 2 * P, 2048 + h * DV + 3 * P,
                         1024 + h * DK, 1024 + h * DK + P, h * DK, h * DK + P]
                for j, col in enumerate(kinds):
                    first = isinstance(h, int) and j < WR
                    weights(j, w_in_a, col, None if first else USES * h + (j - 3))

            head_weights(0)
            with sp.Fori(1, HEADS) as h:
                head_weights(h)
            w_out_a = I["w_out_a"][0].rearrange("(k p) n -> p k n", p=P)
            with sp.Fori(0, NK // 4) as i:
                for j in range(4):
                    weights(j, w_out_a, (4 * i + j) * P, OUT_A + 4 * i + j - 3)
            w_kv = I["w_kv"].rearrange("(k p) n -> p k n", p=P)
            for j in range(8):
                weights(j, w_kv, j * P, KVP + j - 3)
            w_in_b = I["w_in_b"][0].rearrange("(k p) n -> p k n", p=P)
            with sp.Fori(0, KV) as g:
                for j, col in enumerate((2048, 2048 + P, 0, P)):
                    weights(j, w_in_b, g * (GRP * HD) + col, SWA + 4 * g + j - 3)
            w_out_b = I["w_out_b"][0].rearrange("(k p) n -> p k n", p=P)
            with sp.Fori(0, NK // 4) as i:
                for j in range(4):
                    weights(j, w_out_b, (4 * i + j) * P, OUT_B + 4 * i + j - 3)

        @block.tensor
        def _(pe):
            mm = nc.tensor.matmul

            def transpose(out, in_):
                k = in_.shape[0]
                b = in_.start_partition() if callable(in_.start_partition) else in_.start_partition
                return nc.tensor.transpose(out, in_, CST[b:b + k, b:b + k])

            pe.wait_ge(cst_in, 16)
            pe.wait_ge(vec_in, 128)
            pe.wait_ge(setup, 1)
            transpose(B2[:, 0:76], NV[0:76, :])
            mm(B3[:, 0:32], ones[0:1, :], small[0:1, 0:32], start=True, stop=True)
            pe.wait_ge(sink_rows, 1)
            mm(B3[:, 32:40], sx[0:KV, :], ident[0:KV, 0:KV], start=True, stop=True).then_inc(vecs_done, 1)

            def x_tile(n):
                if n >= 2:
                    pe.wait_ge(pp_free[n % 2], n // 2)
                for t in range(NT):
                    if n == 0:
                        pe.wait_ge(x_in[t], 16)
                    transpose(PP[n % 2][:, 0, COLS[t]], XR[:, t, n * P:(n + 1) * P])
                if n == 0:
                    pe.wait_ge(x_in[NT], 32)
                transpose(PP[n % 2][:, 1, 0:EXT], XR[0:EXT, NT, n * P:(n + 1) * P]).then_inc(proj_done, 0 + 1)

            x_tile(0)
            x_tile(1)
            pe.wait_ge(diag_ready, 5)
            for t in range(NT):
                mm(B0[:, COLS[t]], ones[:], diag[:, t, :], start=True, stop=True)
            mm(B1[:, 0:EXT], ones[0:EXT, :], diag[0:EXT, NT, 0:EXT], start=True, stop=True).then_inc(bc_done, 1)
            for n in range(2, NK):
                x_tile(n)
            pe.wait_ge(wglr_in, 16)
            pe.wait_ge(vecs_kept, 2)
            for k in range(NK):
                pe.wait_ge(h_ready, k + 1)
                for c, b in enumerate((B2, B3)):
                    last = mm(b[0:RANK, 0:HALF], wglr[:, k, :], H[:, k, c * HALF:(c + 1) * HALF], start=(k == 0),
                              stop=(k == NK - 1))
            last.then_inc(glr_done, 1)

            def project(lap, jw, half, j, src, fresh=None):
                pe.wait_ge(w_in[jw % WR], 16 * (lap + jw // WR + 1))
                pe.wait_ge(pp_free[j % 2], 8 + half + j // 2)
                for k in range(NK):
                    if fresh is not None:
                        pe.wait_ge(h_ready, fresh + k + 1)
                    for c in range(2):
                        last = mm(PP[j % 2][:, c, 0:HALF], W[:, jw % WR, k, :], src[:, k, c * HALF:(c + 1) * HALF],
                                  start=(k == 0), stop=(k == NK - 1))
                last.then_inc(proj_done, 1)

            def head_unit(h, jw):
                project(3 * h, jw, 7 * h, jw if jw < 8 else jw + 2, H)

            def decay(h, kt):
                pe.wait_ge(pp_free[kt], 8 + 7 * h + 4)
                if kt == 0:
                    pe.wait_ge(gk2_in, 16 * (h + 1))
                    pe.wait_ge(glr_kept, 1)
                for c in range(2):
                    last = mm(PP[kt][:, c, 0:HALF], gk2[0:RANK, kt * P:(kt + 1) * P],
                              glr[0:RANK, c * HALF:(c + 1) * HALF], start=True, stop=True)
                last.then_inc(proj_done, 1)

            def v_rows(h, j, after=None):
                pe.wait_ge(pp_free[j % 2], 8 + 7 * h + (4 + j) // 2 + 1)
                if j == 0 and after is not None:
                    pe.wait_ge(o_gated, 5 * after + 4)
                    pe.wait_ge(s_ready, 10 * after + 10)
                elif j:
                    pe.wait_ge(vn_kept, 4 * h + j)
                for t in range(NT):
                    transpose(B1[:, COLS[t]], TH[:, j % 2, COLS[t]])
                transpose(B3[0:EXT, 0:P], TH[:, j % 2, SEQ:TOK]).then_inc(vtr_done, 1)

            def scores(i, l):
                a = b = Tt[l % 2]
                if l < NL - 1:
                    pe.wait_ge(t_ready, (NL - 1) * i + l + 1)
                else:
                    a, b = kT, qT
                if l >= 2:
                    pe.wait_ge(scores_kept, NL * i + l - 1)
                bank = (B0, B1)[l % 2]
                for t in range(NT):
                    for kt in range(KT):
                        last = mm(bank[:, COLS[t]], a[:, kt, COLS[t]], b[:, kt, COLS[t]], start=(kt == 0),
                                  stop=(kt == KT - 1))
                x = l - (NL - NLX)
                if x >= 0:
                    for kt in range(KT):
                        last = mm(B2[0:EXT, x * EXT:(x + 1) * EXT], a[:, kt, SEQ:TOK], b[:, kt, SEQ:TOK],
                                  start=(kt == 0), stop=(kt == KT - 1))
                last.then_inc(scores_done, 1)

            def kd_rows(i):
                pe.wait_ge(kd_ready, i + 1)
                for kt, bank in enumerate((B3, B0)):
                    if kt:
                        pe.wait_ge(scores_kept, NL * i + NL - 1)
                    for t in range(NT):
                        last = transpose(bank[:, COLS[t]], kd[:, kt, COLS[t]])
                    last.then_inc(kdtr_done, 1)
                pe.wait_ge(scores_kept, NL * i + NL)
                alone(pe)
                for kt in range(KT):
                    last = transpose(B1[0:EXT, kt * P:(kt + 1) * P], kd[:, kt, SEQ:TOK])
                last.then_inc(kdtr_done, 1)

            def update(i, t):
                for kt, bank in enumerate((B2, B3)):
                    if t < 0:
                        last = mm(bank[:], kdX[SMP:EXT, kt * P:(kt + 1) * P], Vx[SMP:EXT, :], start=True, stop=True)
                    else:
                        last = mm(bank[:], kdT[:, t, kt * P:(kt + 1) * P], Vn[:, t, :], start=True, stop=True)
                    last.then_inc(u_done, 1)

            def meta_update(i):
                pe.wait_ge(kdt_ready, 3 * i + 3)
                pe.wait_ge(vn_kept, 4 * i + 4)
                pe.wait_ge(attx_ready, NLX * i + NLX)
                alone(pe)
                update(i, -1)

            def sumsq(i, t):
                pe.wait_ge(sq_ready, 5 * i + t + 1)
                if t:
                    pe.wait_ge(o_gated, 5 * i + t)
                w = WID[t]
                for v in range(VT):
                    last = mm(B1[:, 0:w], ones[:], sq[:, v * w:(v + 1) * w], start=(v == 0), stop=(v == VT - 1))
                last.then_inc(ss_done, 1)

            def tile_step(i, t):
                pe.wait_ge(s_ready, 10 * i + 2 * (t + 1))
                if t == 0:
                    pe.wait_ge(qe_ready, i + 1)
                else:
                    pe.wait_ge(o_kept, 5 * i + t)
                for v in range(VT):
                    out = B0[:, v * P:(v + 1) * P]
                    mm(out, Vn[:, t, v * P:(v + 1) * P], att[:, t, :], start=True, stop=False)
                    for kt in range(KT):
                        last = mm(out, S[:, kt, v * P:(v + 1) * P], qe[:, kt, COLS[t]], start=False, stop=(kt == KT - 1))
                last.then_inc(o_done, 1)
                if t:
                    sumsq(i, t - 1)
                update(i, t)

            def ext_base(i):
                pe.wait_ge(o_kept, 5 * i + 4)
                for v in range(VT):
                    last = mm(B0[:, v * EXT:(v + 1) * EXT], Vx[0:EXT, v * P:(v + 1) * P], attx[0:EXT, :],
                              start=(v == 0), stop=False, skip_group_check=True)
                last.then_inc(extbase, 1)

            def seq_state(i, s, kt):
                if kt == 0:
                    pe.wait_ge(s0_in[s % SR], 16 * (2 * i + s // SR + 1))
                    for v in range(VT):
                        for k2 in range(KT):
                            a = v * EXT + DT * s
                            last = mm(B0[:, a:a + DT], S0[:, s % SR, k2, v * P:(v + 1) * P],
                                      qe[:, k2, SEQ + DT * s:SEQ + DT * (s + 1)], start=False,
                                      stop=(s == DB - 1 and v == VT - 1 and k2 == KT - 1), skip_group_check=True)
                    if s == DB - 1:
                        last.then_inc(o_done, 1)
                    pe.wait_ge(kdm_ready, DB * i + s + 1)
                    if s == 0:
                        pe.wait_ge(vs_ready, i + 1)
                        pe.wait_ge(s_ready, 10 * i + 10)
                    else:
                        pe.wait_ge(smp_new, 2 * DB * i + 2 * s)
                else:
                    pe.wait_ge(smp_new, 2 * DB * i + 2 * s + 1)
                mm(B2[:], kdm[0:SMP, s % 2, kt * P:(kt + 1) * P], Vs[0:SMP, :], start=True, stop=True).then_inc(smp_u, 1)

            def head_step(i, h):
                rec, proj = i is not None, h is not None

                def unit(j):
                    if proj:
                        head_unit(h, j)

                unit(0)
                for l in (0, 1, 2):
                    rec and scores(i, l)
                unit(1)
                for l in (3, 4, 5):
                    rec and scores(i, l)
                unit(2)
                if rec:
                    scores(i, 6)
                    scores(i, 7)
                    kd_rows(i)
                    meta_update(i)
                unit(3)
                if rec:
                    for t in range(NT):
                        tile_step(i, t)
                    sumsq(i, NT - 1)
                    ext_base(i)
                for s in range(DB):
                    rec and seq_state(i, s, 0)
                    if proj:
                        if s == 4:
                            v_rows(h, 3)
                            decay(h, 0)
                            decay(h, 1)
                        head_unit(h, 4 + s)
                    rec and seq_state(i, s, 1)
                    if proj and 1 <= s <= 3:
                        v_rows(h, s - 1, i)
                rec and sumsq(i, NT)

            head_step(None, 0)
            with pe.Fori(0, HEADS - 1) as i:
                head_step(i, i + 1)
            head_step(HEADS - 1, None)

            def out_proj(lap, use):
                with pe.Fori(0, NK // 4) as i:
                    for j in range(4):
                        project(lap + i, j, use // 2 + 2 * i, j, O)

            def mean_square():
                for c, b in enumerate((B0, B1)):
                    last = mm(b[:, 0:HALF], ones[:], acc[:, c * HALF:(c + 1) * HALF], start=True, stop=True)
                last.then_inc(ms_done, 1)

            pe.wait_ge(o_gated, 5 * HEADS)
            out_proj(W_OUT_A // 4, OUT_A)
            pe.wait_ge(acc_done, NK)
            mean_square()

            for j in range(8):
                project(W_KV // 4, j, KVP // 2, j, O, fresh=NK if j == 0 else None)
                if j >= 5:
                    kv_rows = j - 5
                    v_rows_kv = kv_rows
                    pe.wait_ge(pp_free[v_rows_kv % 2], 8 + KVP // 2 + (4 + v_rows_kv) // 2 + 1)
                    if v_rows_kv:
                        pe.wait_ge(vn_kept, 4 * HEADS + v_rows_kv)
                    else:
                        pe.wait_ge(rb_ready, 2)
                    for t in range(NT):
                        transpose(B1[:, COLS[t]], THb[:, v_rows_kv % 2, COLS[t]])
                    transpose(B3[0:EXT, 0:P], THb[:, v_rows_kv % 2, SEQ:TOK]).then_inc(vtr_done, 1)
            pe.wait_ge(pp_free[1], 8 + KVP // 2 + 4)
            pe.wait_ge(vn_kept, 4 * HEADS + 3)
            for t in range(NT):
                transpose(B1[:, COLS[t]], THb[:, 1, COLS[t]])
            transpose(B3[0:EXT, 0:P], THb[:, 1, SEQ:TOK]).then_inc(vtr_done, 1)
            for g in range(KV):
                last = transpose(B2[:, g * HD:(g + 1) * HD], kdup[0:HD, g, SEQ - P:SEQ])
            last.then_inc(kw_done, 1)
            for g in range(KV):
                last = transpose(B0[0:SMP, g * HD:(g + 1) * HD], kdup[0:HD, g, SEQ:SEQ + SMP])
            last.then_inc(kw_done, 1)
            pe.wait_ge(kw_kept, 2)
            pe.wait_ge(vn_kept, 4 * HEADS + 4)

            def batch_scores(i, k):
                if k == 0:
                    pe.wait_ge(staged, i + 1)
                    pe.wait_ge(q_copied, i + 1)
                elif k < 5:
                    pe.wait_ge(comb_ok, 6 * i + k)
                alone(pe)
                for r in range(GRP):
                    a = HD * (r % 2)
                    q = qB[a:a + HD, r // 2, :]
                    key = kg[a:a + HD, :]
                    bank, c = (B0, B1)[r % 2], 2 * P * (r // 2)
                    if k < 4:
                        mm(bank[:, c:c + P], q[:, COLS[k]], key[:, COLS[k]], start=True, stop=True)
                        if k:
                            last = mm(bank[:, c + P:c + 2 * P], q[:, COLS[k]], key[:, COLS[k - 1]], start=True, stop=True)
                        else:
                            last = mm(bank[:, c + 2 * P - META:c + 2 * P], q[:, COLS[0]], key[:, SEQ + SMP:TOK],
                                      start=True, stop=True)
                    elif k == 4:
                        last = mm(bank[0:META, c:c + META], q[:, SEQ + SMP:TOK], key[:, SEQ + SMP:TOK],
                                  start=True, stop=True)
                if k == 5:
                    pe.wait_ge(kcat_ready, 2 * i + 2)
                    pe.wait_ge(qz_ready, 4 * i + 4)
                    for s in range(DB):
                        last = mm(B0[:, 0:P + DT], Qz[0:HD, s, :], kcat[0:HD, s, :], start=(s == 0), stop=(s == DB - 1))
                last.then_inc(sc_done, 1)

            def cache_keys(i):
                pe.wait_ge(kc_in[0], 16 * (i + 1))
                pe.wait_ge(comb_ok, 6 * i + 5)
                alone(pe)
                for s in range(DB):
                    last = transpose((B0, B1)[s // 4][0:HD, (s % 4) * P:(s % 4 + 1) * P], Kc[:, 0, s * HD:(s + 1) * HD])
                last.then_inc(kct_done, 1)

            def batch_pt(i, k):
                pe.wait_ge(p_ready, 6 * i + k + 1)
                alone(pe)
                if k < 4:
                    for r in range(GRP):
                        last = transpose(B2[:, r * P:(r + 1) * P], Pp[:, k % 2, r * P:(r + 1) * P])
                elif k == 4:
                    for r in range(GRP):
                        last = transpose(B2[0:META, r * META:(r + 1) * META], Pp[0:META, 0, r * META:(r + 1) * META])
                else:
                    pe.wait_ge(o_stat, 2 * i + 2)
                    alone(pe)
                    transpose(B2[:, 0:P], Pp[:, 1, 0:P])
                    last = transpose(B2[0:SMP, P:2 * P], Pn[:, 0:SMP])
                last.then_inc(pt_done, 1)

            def batch_pv(i, k):
                pe.wait_ge(pt_kept, 6 * i + k + 1)
                if k:
                    pe.wait_ge(b_gated, 9 * i + k)
                if k == 5:
                    pe.wait_ge(kc_in[1], 16 * (i + 1))
                alone(pe)
                if k < 4:
                    for r in range(GRP):
                        out = B3[:, r * HD:(r + 1) * HD]
                        mm(out, PTc[:, k % 2, r * P:(r + 1) * P], vg[:, k, :], start=True, stop=False)
                        if k:
                            last = mm(out, PTp[:, k % 2, r * P:(r + 1) * P], vg[:, k - 1, :], start=False, stop=True)
                        else:
                            last = mm(out, PTp[96:P, 0, r * P:(r + 1) * P], vmg[96:P, :], start=False, stop=True)
                elif k == 4:
                    for r in range(GRP):
                        last = mm(B3[0:META, r * HD:(r + 1) * HD], PTc[SMP:EXT, 0, r * META:(r + 1) * META],
                                  vxg[SMP:EXT, :], start=True, stop=True)
                else:
                    mm(B3[:, 0:HD], PnT[0:SMP, :], vxg[0:SMP, :], start=True, stop=False)
                    for s in range(DB):
                        last = mm(B3[:, 0:HD], Pz[:, s, :], Vc[:, 0, s * HD:(s + 1) * HD], start=False, stop=(s == DB - 1))
                last.then_inc(pv_done, 1)

            def batch_ot(i, k):
                pe.wait_ge(on_ready, 6 * i + k + 1)
                alone(pe)
                if k < 5:
                    n = P if k < 4 else META
                    for u in range(2):
                        last = transpose(B3[:, u * n:(u + 1) * n], on[0:n, k % 2, u * P:(u + 1) * P])
                else:
                    last = transpose(B3[0:HD, 0:P], on[:, 1, 0:HD])
                last.then_inc(ot_done, 1)

            def group_step(i, g):
                att_, proj = i is not None, g is not None

                def unit(j):
                    if proj:
                        project(W_SWA // 4 + g, j, SWA // 2 + 2 * g, j, H, fresh=2 * NK if isinstance(g, int) and j == 0 else None)

                def step(k):
                    if not att_:
                        return
                    if k == 4:
                        cache_keys(i)
                    if k < 5:
                        batch_scores(i, k + 1)
                    if k:
                        batch_ot(i, k - 1)
                    batch_pt(i, k)
                    batch_pv(i, k)

                unit(0)
                if att_:
                    batch_scores(i, 0)
                unit(1)
                step(0)
                step(1)
                unit(2)
                step(2)
                step(3)
                unit(3)
                step(4)
                step(5)
                att_ and batch_ot(i, 5)

            group_step(None, 0)
            with pe.Fori(0, KV - 1) as i:
                group_step(i, i + 1)
            group_step(KV - 1, None)

            def y_rows(i, j):
                n4 = 4 * i + j
                pe.wait_ge(xg_ready, n4 + 1)
                a, b = ((B0, B2), (B1, B3))[j % 2]
                if j >= 2:
                    pe.wait_ge(y_kept, 2 * (n4 - 1))
                for t in range(NT):
                    transpose(a[:, COLS[t]], xg[:, j % 2, COLS[t]])
                transpose(b[0:EXT, 0:P], xg[:, j % 2, SEQ:TOK]).then_inc(yt_done, 1)

            pe.wait_ge(b_gated, 9 * KV)
            with pe.Fori(0, NK // 4) as i:
                for j in range(4):
                    project(W_OUT_B // 4 + i, j, OUT_B // 2 + 2 * i, j, O)
                    if j:
                        y_rows(i, j - 1)
                y_rows(i, 3)
                pe.wait_ge(y_kept, 8 * i + 8)
            pe.wait_ge(acc_done, 2 * NK)
            for t in range(NT + 1):
                n = WID[t]
                last = mm(B0[0:n, 2 * t:2 * t + 2], acc[:, COLS[t]], ones[:, 0:2], start=True, stop=True)
            last.then_inc(ms_done, 1)

        @block.scalar
        def _(act):
            A = nc.scalar.activation
            act.wait_ge(setup, 1)
            for t in range(NT + 1):
                n = WID[t]
                act.wait_ge(x_in[t], 16 if t < NT else 32)
                if t:
                    act.wait_ge(row_ss, t)
                A(junk[0:n, :], XR[0:n, t, :], ACT.Square, accum_out=ss_c[0:n, t:t + 1]).then_inc(row_ss, 1)
            act.wait_ge(rs_dve, 1)
            A(lg_c, ms_c, ACT.Ln).then_inc(rs_act, 1)
            act.wait_ge(rs_act, 1)
            A(rs_c, lg_c, ACT.Exp, scale=-0.5).then_inc(rs_act, 1)
            act.wait_ge(vecs_done, 1)
            A(SK[:], B3[:, 0:32], ACT.Copy, scale=-1.0).then_inc(vecs_kept, 1)
            A(SKR[:], B3[:, 32:40], ACT.Copy, scale=-1.0).then_inc(vecs_kept, 1)
            for n in range(NK):
                act.wait_ge(proj_done, n + 1)
                if n >= 2:
                    act.wait_ge(h_ready, n - 1)
                    act.wait_ge(x0_out[n % 2], 16 * (n // 2))
                nc.scalar.copy(xt[:, n % 2, 0:SEQ], PP[n % 2][:, 0, :])
                nc.scalar.copy(xt[:, n % 2, SEQ:TOK], PP[n % 2][:, 1, 0:EXT]).then_inc(pp_free[n % 2], 1)
            act.wait_ge(glr_done, 1)
            for b in range(2):
                act.wait_ge(x0_out[b], 8 * NK)
            nc.scalar.copy(glr[0:RANK, 0:HALF], B2[0:RANK, 0:HALF]).then_inc(g_act, 1)
            nc.scalar.copy(glr[0:RANK, HALF:TOK], B3[0:RANK, 0:HALF]).then_inc(glr_kept, 1)
            G0 = 1

            def gate(h, j, th, half, done, after=None):
                act.wait_ge(proj_done, NK + done)
                if after is not None:
                    act.wait_ge(*after)
                A(halves(th[:, j % 2, :]), PV(j), ACT.Tanh, scale=0.5).then_inc(th_ready, 1)

            def head_gate(h, j):
                if j >= 2:
                    gate(h, j, TH, 7 * h, USES * h + j + 1, (pp_free[j % 2], 8 + 7 * h + j // 2))
                elif isinstance(h, int):
                    gate(h, j, TH, 7 * h, USES * h + j + 1)
                else:
                    gate(h, j, TH, 7 * h, USES * h + j + 1, (vtr_done, 4 * h))

            def v_tile(h, j):
                act.wait_ge(proj_done, NK + USES * h + 5 + j)
                if j >= 2:
                    act.wait_ge(vtr_done, 4 * h + j - 1)
                else:
                    act.wait_ge(pp_free[j % 2], 8 + 7 * h + (j + 2) // 2 + 1)
                nc.scalar.copy(halves(TH[:, j % 2, :]), PV(j)).then_inc(pp_free[j % 2], 1)

            def decay_gate(h):
                for kt in range(KT):
                    act.wait_ge(proj_done, NK + USES * h + 9 + kt)
                    if kt == 0:
                        act.wait_ge(vn_kept, 4 * h + 1)
                    bias = GV[:, ds(B_GK + 2 * h + kt, 1)]
                    A(halves(Dd[0][:, kt, :]), PV(kt), ACT.Identity, bias=bias).then_inc(g_act, 1)
                    A(halves(Dd[1][:, kt, :]), PV(kt), ACT.Abs, bias=bias).then_inc(pp_free[kt], 1)
                for kt in range(KT):
                    act.wait_ge(pp_free[kt], 8 + 7 * h + 5)
                    A(Dd[1][:, kt, :], Dd[1][:, kt, :], ACT.Exp, scale=-1.0).then_inc(g_act, 1)
                for kt in range(KT):
                    act.wait_ge(g_act, G0 + 6 * h + 3 + kt)
                    A(Dd[1][:, kt, :], Dd[1][:, kt, :], ACT.Ln, bias=1.0).then_inc(g_act, 1)

            def q_tile(h, j):
                act.wait_ge(proj_done, NK + USES * h + 13 + j)
                if j == 0:
                    act.wait_ge(pp_free[0], 8 + 7 * h + 6)
                A(halves(qT[:, j, :]), PV(j), ACT.Copy, scale=DK ** -0.5).then_inc(pp_free[j % 2], 1)

            def level_decay(i, l):
                act.wait_ge(d_ready, (NL - 1) * i + l + 1)
                h = LEVELS[l]
                w = SEQ if l < NL - NLX else TOK
                v = Dd[l % 2][:, :, 0:w].rearrange("p k (b c) -> p k b c", c=2 * h)
                A(v[:, :, :, h:2 * h], v[:, :, :, h:2 * h], ACT.Exp, scale=1.0 / GN).then_inc(e_ready, 1)
                A(v[:, :, :, 0:h], v[:, :, :, 0:h], ACT.Exp, scale=-1.0 / GN).then_inc(e_ready, 1)

            def end_decay(i):
                act.wait_ge(kde_ready, 3 * i + 3)
                A(kd, kd, ACT.Exp, scale=-1.0 / GN).then_inc(decay_exp, 1)
                act.wait_ge(scores_done, NL * i + 6)
                A(qe, bT, ACT.Exp, scale=1.0 / GN).then_inc(decay_exp, 1)
                A(el[:, :, 0:NT], bT[:, :, P - 1:SEQ:P], ACT.Exp, scale=1.0 / GN).then_inc(decay_exp, 1)
                A(el[:, :, NT:NT + DB], bT[:, :, SEQ + DT - 1:SEQ + SMP:DT], ACT.Exp, scale=1.0 / GN).then_inc(decay_exp, 1)

            def kd_keep(i):
                act.wait_ge(kdtr_done, 3 * i + 1)
                nc.scalar.copy(kdT[:, :, 0:P], bank4(B3)).then_inc(kdt_ready, 1)
                act.wait_ge(kdtr_done, 3 * i + 2)
                nc.scalar.copy(kdT[:, :, P:DK], bank4(B0)).then_inc(kdt_ready, 1)
                act.wait_ge(kdtr_done, 3 * i + 3)
                nc.scalar.copy(kdX[0:EXT, :], B1[0:EXT, 0:DK]).then_inc(kdt_ready, 1)

            def o_keep(i, t):
                act.wait_ge(o_done, 5 * i + t + 1)
                if t >= 2:
                    act.wait_ge(o_gated, 5 * i + t - 1)
                n = VT * WID[t]
                nc.scalar.copy(o_sb[:, t % 2, 0:n], B0[:, 0:n]).then_inc(o_kept, 1)

            def head_norm(i, t):
                act.wait_ge(ss_done, 5 * i + t + 1)
                w = WID[t]
                A(rl[:, 0:w], B1[:, 0:w], ACT.Ln, bias=eps_c, scale=1.0 / DV).then_inc(r_act, 1)
                act.wait_ge(r_act, 10 * i + 2 * t + 1)
                A(rr[:, 0:w], rl[:, 0:w], ACT.Exp, scale=-0.5).then_inc(r_act, 1)

            def head_step(i, h):
                rec, proj = i is not None, h is not None
                if rec:
                    for l in range(4):
                        level_decay(i, l)
                proj and head_gate(h, 0)
                if rec:
                    for l in range(4, 7):
                        level_decay(i, l)
                proj and head_gate(h, 1)
                rec and end_decay(i)
                proj and head_gate(h, 2)
                rec and kd_keep(i)
                proj and head_gate(h, 3)
                if rec:
                    for t in range(NT):
                        o_keep(i, t)
                        if t:
                            head_norm(i, t - 1)
                    head_norm(i, NT - 1)
                if proj:
                    for j in range(VT):
                        v_tile(h, j)
                    decay_gate(h)
                    q_tile(h, 0)
                    q_tile(h, 1)
                if rec:
                    o_keep(i, NT)
                    head_norm(i, NT)

            head_step(None, 0)
            with act.Fori(0, HEADS - 1) as i:
                head_step(i, i + 1)
            head_step(HEADS - 1, None)

            def squares(half, base):
                with act.Fori(0, NK // 4) as i:
                    for j in range(4):
                        act.wait_ge(pp_free[j % 2], 8 + half + 2 * i + j // 2 + 1)
                        if j >= 2:
                            act.wait_ge(acc_done, base + 4 * i + j - 1)
                        A(sqa[:, j % 2, :], tile(H, 4 * i + j), ACT.Square).then_inc(sq_a, 1)
                    act.wait_ge(acc_done, base + 4 * i + 4)

            squares(OUT_A // 2, 0)

            def root(n):
                for c, b in enumerate((B0, B1)):
                    s = slice(c * HALF, (c + 1) * HALF)
                    act.wait_ge(n_dve, n + c + 1)
                    A(RB[:, s], acc[:, s], ACT.Ln).then_inc(n_act, 1)
                    act.wait_ge(n_act, 2 * (n + c) + 1)
                    A(RB[:, s], RB[:, s], ACT.Exp, scale=-0.5).then_inc(n_act, 1)

            root(0)
            for j in range(4):
                act.wait_ge(proj_done, NK + KVP + j + 1)
                nc.scalar.copy(halves(kdup[0:HD, 2 * j, :]), PV(j)[0:HD]).then_inc(th_ready, 1)
                nc.scalar.copy(halves(kdup[HD:P, 2 * j, :]), PV(j)[0:HD]).then_inc(th_ready, 1)
            TK = 4 * HEADS + 8
            for j in range(4):
                act.wait_ge(proj_done, NK + KVP + 5 + j)
                if j >= 2:
                    act.wait_ge(vtr_done, 4 * HEADS + j - 1)
                nc.scalar.copy(halves(THb[:, j % 2, :]), PV(j)).then_inc(pp_free[j % 2], 1)
            act.wait_ge(kw_done, 1)
            nc.scalar.copy(kwin, B2[:]).then_inc(kw_kept, 1)
            act.wait_ge(kw_done, 2)
            nc.scalar.copy(kwx[0:SMP, :], B0[0:SMP, :]).then_inc(kw_kept, 1)

            def group_gate(g, j):
                act.wait_ge(proj_done, NK + SWA + 4 * g + j + 1)
                if isinstance(g, int):
                    if j == 0:
                        act.wait_ge(vtr_done, 4 * HEADS + 4)
                else:
                    act.wait_ge(pp_free[j % 2], 8 + SWA // 2 + 2 * g - 1)
                A(halves(THb[:, j % 2, :]), PV(j), ACT.Tanh, scale=0.5).then_inc(thb_ready, 1)

            def group_q(g, j):
                act.wait_ge(proj_done, NK + SWA + 4 * g + 3 + j)
                if not isinstance(g, int):
                    act.wait_ge(q_copied, g)
                nc.scalar.copy(halves(qN[:, j, :]), PV(j)).then_inc(pp_free[j % 2], 1)

            def batch_comb(i, k):
                if k == 4:
                    return
                act.wait_ge(sc_done, 6 * i + k + 1)
                if k == 0:
                    act.wait_ge(c_fill, i + 1)
                    nc.scalar.copy(by_head(Cc[:, 0, :])[:, :, :, P - META:P], old_scores(P - META)).then_inc(comb, 1)
                elif k < 4:
                    if k >= 2:
                        act.wait_ge(p_ready, 6 * i + k - 1)
                    nc.scalar.copy(by_head(Cc[:, k % 2, :]), old_scores()).then_inc(comb, 1)
                else:
                    act.wait_ge(p_ready, 6 * i + 4)
                    nc.scalar.copy(Cc[:, 1, 0:P], B0[:, 0:P]).then_inc(comb, 1)

            def batch_exp(i, k):
                b = k % 2
                act.wait_ge(sm_dve, 18 * i + 3 * k + 3)
                if k >= 2:
                    act.wait_ge(pt_done, 6 * i + k - 1)
                n, w, heads = ((P, P, GRP), (META, META, GRP), (P, P, 1))[max(k - 3, 0)]
                for r in range(heads):
                    A(Pp[0:n, b, r * w:(r + 1) * w], Cc[0:n, b, r * w:(r + 1) * w], ACT.Exp, scale=HD ** -0.5,
                      bias=sm[0:n, b, 4 + r:5 + r], accum_out=sm[0:n, b, 16 + r:17 + r]).then_inc(sm_act, 1)
                A(sm[0:n, b, 12:12 + heads], sm[0:n, b, 8:8 + heads], ACT.Exp).then_inc(p_ready, 1)

            def group_step(i, g):
                att_, proj = i is not None, g is not None

                def batch(k):
                    if att_:
                        if k == 5:
                            act.wait_ge(kct_done, i + 1)
                            for c, b in enumerate((B0, B1)):
                                nc.scalar.copy(kcat[0:HD, 4 * c:4 * c + 4, 0:P], bank4(b)[0:HD]).then_inc(kcat_ready, 1)
                        batch_comb(i, k)
                        batch_exp(i, k)

                proj and group_gate(g, 0)
                batch(0)
                proj and group_gate(g, 1)
                batch(1)
                batch(2)
                proj and group_q(g, 0)
                batch(3)
                batch(4)
                proj and group_q(g, 1)
                batch(5)

            group_step(None, 0)
            with act.Fori(0, KV - 1) as i:
                group_step(i, i + 1)
            group_step(KV - 1, None)

            with act.Fori(0, NK // 4) as i:
                for j in range(4):
                    act.wait_ge(pp_free[j % 2], 8 + OUT_B // 2 + 2 * i + j // 2 + 1)
                    if j >= 2:
                        act.wait_ge(acc_done, NK + 4 * i + j - 1)
                        act.wait_ge(yt_done, 4 * i + j - 1)
                    A(sqa[:, j % 2, :], x2[:, j % 2, :], ACT.Square).then_inc(sq_a, 1)
                    A(xg[:, j % 2, :], x2[:, j % 2, :], ACT.Copy, scale=GV[:, ds(G_F + 4 * i + j, 1)]).then_inc(xg_ready, 1)
                act.wait_ge(acc_done, NK + 4 * i + 4)
                act.wait_ge(yt_done, 4 * i + 4)
            act.wait_ge(n_dve, 3)
            A(lg_c, ms_c, ACT.Ln).then_inc(n_act, 1)
            act.wait_ge(n_act, 5)
            A(rs_c, lg_c, ACT.Exp, scale=-0.5).then_inc(n_act, 1)
            for t in (1, 3):
                act.wait_ge(n_dve, 7)
                A(YR[:, t, :], YR[:, t, :], ACT.Copy, scale=rs_c[:, t:t + 1]).then_inc(y_scaled, 1)

        @block.vector
        def _(dve):
            V = nc.vector
            TT, TS, STT = V.tensor_tensor, V.tensor_scalar, V.scalar_tensor_tensor

            V.memset(ones[:], 1.0)
            V.memset(eps_c, EPS)
            V.memset(small[:, 40:65], 1.0).then_inc(setup, 1)
            dve.wait_ge(setup, 1)

            def newton(y, x, tmp, tally):
                tally.link(dve, TT(tmp, y, y, ALU.mult))
                tally.link(dve, TT(tmp, tmp, x, ALU.mult))
                tally.link(dve, TS(tmp, tmp, -0.5, 1.5, ALU.mult, ALU.add))
                tally.link(dve, TT(y, y, tmp, ALU.mult))

            dve.wait_ge(vec_in, 128)
            V.tensor_copy(sx[0:KV, :].rearrange("p (s r t) -> p s r t", r=GRP, t=DT),
                          small[0:KV, 32:36].unsqueeze(1).unsqueeze(3).broadcast_to([KV, DB, GRP, DT])).then_inc(sink_rows, 1)

            dve.wait_ge(row_ss, NT + 1)
            c = Tally(rs_dve)
            c.link(dve, TS(ms_c, ss_c, 1.0 / DM, EPS, ALU.mult, ALU.add))
            dve.wait_ge(rs_act, 2)
            newton(rs_c, ms_c, nt_c, c)
            dve.wait_ge(cst_in, 16)
            for t in range(NT + 1):
                TS(diag[:, t, :], ident, rs_c[:, t:t + 1], None, ALU.mult).then_inc(diag_ready, 1)
            dve.wait_ge(vecs_done, 1)
            c.link(dve, V.tensor_copy(GV[:], B2[:, 0:76]))
            c.link(dve, TS(GV[:, G_O:G_O + VT], GV[:, G_O:G_O + VT], 0.5, None, ALU.mult))
            dve.wait_ge(bc_done, 1)
            V.tensor_copy(RB[:, 0:SEQ], B0[:])
            V.tensor_copy(RB[:, SEQ:TOK], B1[:, 0:EXT]).then_inc(rb_ready, 1)
            dve.wait_ge(rb_ready, 1)
            for n in range(NK):
                dve.wait_ge(pp_free[n % 2], n // 2 + 1)
                STT(out=H[:, n, :], in0=xt[:, n % 2, :], scalar=GV[:, G_A + n:G_A + n + 1], in1=RB[:], op0=ALU.mult,
                    op1=ALU.mult).then_inc(h_ready, 1)
            for b in range(2):
                dve.wait_ge(x0_out[b], 8 * NK)
            dve.wait_ge(h_ready, NK)
            V.memset(att[:, :, :].rearrange("p t n -> p (t n)"), 0.0)
            V.memset(attx, 0.0).then_inc(setup, 1)
            dve.wait_ge(setup, 2)

            def gate(O_tile, th, j, ready):
                dve.wait_ge(*ready)
                STT(out=halves(O_tile), in0=halves(th[:, j % 2, :]), scalar=1.0, in1=PV(j), op0=ALU.add,
                    op1=ALU.mult).then_inc(pp_free[j % 2], 1)

            def head_gate(h, j):
                gate(tile(O, VT * h + j), TH, j, (th_ready, 4 * h + j + 1))

            def v_keep(base, j, rows, ext, after=None):
                dve.wait_ge(vtr_done, base + j + 1)
                if j == 0 and after is not None:
                    dve.wait_ge(extbase, after + 1)
                    dve.wait_ge(vs_ready, after + 1)
                V.tensor_copy(rows[:, :, j * P:(j + 1) * P], bank4(B1))
                V.tensor_copy(ext[0:EXT, j * P:(j + 1) * P], B3[0:EXT, 0:P]).then_inc(vn_kept, 1)

            def decay_sum(h, kt):
                dve.wait_ge(g_act, 1 + 6 * h + 5 + kt)
                STT(out=Dd[0][:, kt, :], in0=Dd[0][:, kt, :], scalar=0.0, in1=Dd[1][:, kt, :], op0=ALU.min,
                    op1=ALU.subtract).then_inc(b_step, 1)
                dve.wait_ge(b_step, 4 * h + 2 * kt + 1)
                V.tensor_tensor_scan(bT[:, kt, :], C("keep"), Dd[0][:, kt, :], 0.0, ALU.mult, ALU.add).then_inc(b_step, 1)

            def k_tile(h, j):
                dve.wait_ge(proj_done, NK + USES * h + 11 + j)
                V.tensor_copy(halves(kT[:, j, :]), PV(j)).then_inc(pp_free[j % 2], 1)

            def blocks(buf, l):
                w = SEQ if l < NL - NLX else TOK
                return buf[:, :, 0:w].rearrange("p k (b c) -> p k b c", c=2 * LEVELS[l])

            def distance(i, l):
                if l == 0:
                    dve.wait_ge(b_step, 4 * i + 4)
                if l >= 2:
                    dve.wait_ge(t_ready, (NL - 1) * i + l - 1)
                b, h = blocks(bT, l), LEVELS[l]
                ref = b[:, :, :, h - 1:h].broadcast_to(list(b.shape))
                TT(blocks(Dd[l % 2], l), b, ref, ALU.subtract).then_inc(d_ready, 1)

            def level_qk(i, l):
                dve.wait_ge(e_ready, 2 * (NL - 1) * i + 2 * l + 2)
                if l == 0:
                    for b in range(2):
                        dve.wait_ge(pp_free[b], 8 + 7 * i + 7)
                if l >= 2:
                    dve.wait_ge(scores_done, NL * i + l - 1)
                h = LEVELS[l]
                T_, D_, q, k = (blocks(x, l) for x in (Tt[l % 2], Dd[l % 2], qT, kT))
                TT(T_[:, :, :, h:2 * h], q[:, :, :, h:2 * h], D_[:, :, :, h:2 * h], ALU.mult)
                TT(T_[:, :, :, 0:h], k[:, :, :, 0:h], D_[:, :, :, 0:h], ALU.mult).then_inc(t_ready, 1)

            def take_scores(i, l):
                dve.wait_ge(scores_done, NL * i + l + 1)
                if l:
                    dve.wait_ge(scores_kept, NL * i + l)
                else:
                    dve.wait_ge(t_ready, (NL - 1) * i + 1)
                name = f"level{LEVELS[l] if l < NL - 1 else 0}"
                alone(dve)
                V.copy_predicated(att, over(C(name).bitcast(I32), NT), bank4((B0, B1)[l % 2])).then_inc(scores_kept, 1)

            def take_ext(i):
                for x in range(NLX):
                    if x:
                        dve.wait_ge(attx_ready, NLX * i + x)
                    name = f"ext{(LEVELS[-4:] + [0])[x]}"
                    alone(dve)
                    V.copy_predicated(attx[0:EXT, :], C(name, 0, EXT).bitcast(I32),
                                      B2[0:EXT, x * EXT:(x + 1) * EXT]).then_inc(attx_ready, 1)

            def end_distance(i):
                dve.wait_ge(t_ready, (NL - 1) * i + 6)
                for a, b, n in ((0, SEQ, P), (SEQ, SEQ + SMP, DT), (SEQ + SMP, TOK, META)):
                    v = bT[:, :, a:b].rearrange("p k (b c) -> p k b c", c=n)
                    last = v[:, :, :, n - 1:n].broadcast_to(list(v.shape))
                    TT(kd[:, :, a:b].rearrange("p k (b c) -> p k b c", c=n), v, last, ALU.subtract).then_inc(kde_ready, 1)

            def end_qk(i):
                dve.wait_ge(decay_exp, 4 * i + 1)
                TT(kd, kd, kT, ALU.mult).then_inc(kd_ready, 1)
                dve.wait_ge(decay_exp, 4 * i + 2)
                TT(qe, qe, qT, ALU.mult).then_inc(qe_ready, 1)

            def meta_state(i):
                for kt, bank in enumerate((B2, B3)):
                    dve.wait_ge(u_done, 10 * i + kt + 1)
                    V.tensor_copy(S[:, kt, :], bank[:]).then_inc(s_ready, 1)

            def state(i, t):
                if t == 0:
                    dve.wait_ge(decay_exp, 4 * i + 4)
                for kt, bank in enumerate((B2, B3)):
                    dve.wait_ge(u_done, 10 * i + 2 * (t + 1) + kt + 1)
                    dve.wait_ge(s_ready, 10 * i + 2 * t + kt + 1)
                    STT(out=S[:, kt, :], in0=S[:, kt, :], scalar=el[:, kt, t:t + 1], in1=bank[:], op0=ALU.mult,
                        op1=ALU.add).then_inc(s_ready, 1)

            def head_norm(i, t):
                w = WID[t]
                c = Tally(r_dve, 30 * i + 6 * t)
                dve.wait_ge(r_act, 10 * i + 2 * t + 2)
                if t == 0:
                    for b in range(2):
                        dve.wait_ge(pp_free[b], 8 + 7 * i + 2)
                c.link(dve, TS(rv[:, 0:w], B1[:, 0:w], 1.0 / DV, EPS, ALU.mult, ALU.add))
                newton(rr[:, 0:w], rv[:, 0:w], ra[:, 0:w], c)
                x = sq[:, 0:VT * w].rearrange("p (v n) -> p v n", v=VT)
                c.link(dve, TT(x, o_sb[:, t % 2, 0:VT * w].rearrange("p (v n) -> p v n", v=VT), over(rr[:, 0:w], VT),
                               ALU.mult))
                for v in range(VT):
                    o = tile(O, VT * i + v)[:, COLS[t]]
                    last = STT(out=o, in0=x[:, v, :], scalar=GV[:, G_O + v:G_O + v + 1], in1=o, op0=ALU.mult, op1=ALU.mult)
                last.then_inc(o_gated, 1)

            def seq_state(i, s, kt):
                dve.wait_ge(smp_u, 2 * DB * i + 2 * s + kt + 1)
                x = S0[:, s % SR, kt, :]
                STT(out=x, in0=x, scalar=el[:, kt, NT + s:NT + s + 1], in1=B2[:], op0=ALU.mult,
                    op1=ALU.add).then_inc(smp_new, 1)

            def head_step(i, h):
                rec, proj = i is not None, h is not None
                if rec:
                    distance(i, 0)
                    distance(i, 1)
                    level_qk(i, 0)
                    distance(i, 2)
                    level_qk(i, 1)
                    distance(i, 3)
                proj and head_gate(h, 0)
                if rec:
                    for l in (2, 3, 4):
                        take_scores(i, l - 2)
                        level_qk(i, l)
                        if l + 2 < NL - 1:
                            distance(i, l + 2)
                proj and head_gate(h, 1)
                if rec:
                    take_scores(i, 3)
                    level_qk(i, 5)
                    take_scores(i, 4)
                    level_qk(i, 6)
                    end_distance(i)
                    end_qk(i)
                proj and head_gate(h, 2)
                if rec:
                    take_scores(i, 5)
                    take_scores(i, 6)
                    take_scores(i, 7)
                    take_ext(i)
                    meta_state(i)
                proj and head_gate(h, 3)
                if rec:
                    for t in range(NT):
                        state(i, t)
                        if t:
                            head_norm(i, t - 1)
                    head_norm(i, NT - 1)
                for s in range(DB):
                    rec and seq_state(i, s, 0)
                    if proj:
                        if s == 4:
                            v_keep(4 * h, 3, Vn, Vx)
                            decay_sum(h, 0)
                            decay_sum(h, 1)
                        if s in (4, 5):
                            k_tile(h, s - 4)
                    rec and seq_state(i, s, 1)
                    if proj and 1 <= s <= 3:
                        v_keep(4 * h, s - 1, Vn, Vx, i)
                if rec:
                    head_norm(i, NT)
                    dve.wait_ge(state_out, 16 * (i + 1))

            head_step(None, 0)
            with dve.Fori(0, HEADS - 1) as i:
                head_step(i, i + 1)
            head_step(HEADS - 1, None)

            with dve.Fori(0, NK // 4) as i:
                for j in range(4):
                    dve.wait_ge(proj_done, NK + OUT_A + 4 * i + j + 1)
                    dve.wait_ge(xs_in[j], 16 * (i + 1))
                    TT(halves(tile(H, 4 * i + j)), PV(j), halves(xs[:, j, :]), ALU.add).then_inc(pp_free[j % 2], 1)
            dve.wait_ge(ms_done, 1)
            cn = Tally(n_dve)
            for c_, b in enumerate((B0, B1)):
                cn.link(dve, TS(acc[:, c_ * HALF:(c_ + 1) * HALF], b[:, 0:HALF], 1.0 / DM, EPS, ALU.mult, ALU.add))
            cr = Tally(rs_dve, c.value)
            dve.wait_ge(n_act, 4)
            newton(RB[:], acc[:], x2[:, 0, :], cr)
            V.tensor_copy(small[:, 90:91], eps_c).then_inc(rb_ready, 1)

            def normed(dst, g, n):
                STT(out=dst[:, n, :], in0=H[:, n, :], scalar=GV[:, g + n:g + n + 1], in1=RB[:], op0=ALU.mult,
                    op1=ALU.mult).then_inc(h_ready, 1)

            for b in range(2):
                dve.wait_ge(pp_free[b], 8 + KVP // 2)
            for n in range(NK):
                normed(O, G_KV, n)
            for q in range(4):
                dve.wait_ge(x1_out[q], 4 * 16)
            dve.wait_ge(h_ready, 2 * NK)
            for n in range(NK):
                normed(H, G_B, n)
            for j in range(4):
                dve.wait_ge(th_ready, 4 * HEADS + 2 * j + 2)
                V.tensor_copy(halves(kdup[0:HD, 2 * j + 1, :]), PV(j)[HD:P])
                V.tensor_copy(halves(kdup[HD:P, 2 * j + 1, :]), PV(j)[HD:P]).then_inc(pp_free[j % 2], 1)
            dve.wait_ge(h_ready, 3 * NK)
            V.memset(Wm[96:P, :], 0.0).then_inc(setup, 1)
            V.memset(Qz[0:HD].rearrange("p s n -> p (s n)"), 0.0)
            V.memset(Pz.rearrange("p s n -> p (s n)"), 0.0).then_inc(setup, 1)
            for j in range(4):
                v_keep(4 * HEADS, j, Wn, Wx)
            dve.wait_ge(setup, 4)

            def z_blocks(buf):
                full = buf.rearrange("p s n -> p (s n)")
                return full

            def spread_q(i):
                dve.wait_ge(q_copied, i + 1)
                for r in range(GRP):
                    a = HD * (r % 2)
                    src = qB[a:a + HD, r // 2, SEQ:SEQ + SMP].rearrange("p (s t) -> p s t", t=DT)
                    V.tensor_copy(diag_view(Qz, DT * r, DT)[0:HD], src).then_inc(qz_ready, 1)

            def diag_view(buf, off, n):
                flat = buf.rearrange("p s n -> p (s n)")
                w = GRP * DT
                a = flat[:, 0:(P + w) * (DB - 1) + w]
                pad = flat[:, 0:DB * P]
                v = bass.AP(tensor=a.tensor, offset=a.offset + off, ap=[list(a.ap[0]), [P + w, DB], [1, n]])
                return v

            def batch_max(i, k):
                b = k % 2
                if k < 4:
                    dve.wait_ge(comb, 5 * i + k + 1)
                    x = bank4(Cc[:, b, :])
                    alone(dve)
                    V.copy_predicated(by_head(Cc[:, b, :]), over(over(C("causal").bitcast(I32), 2), 2),
                                      own_scores()).then_inc(comb_ok, 1)
                    n, g = P, GRP
                elif k == 4:
                    dve.wait_ge(sc_done, 6 * i + 5)
                    dve.wait_ge(p_ready, 6 * i + 3)
                    n, g = META, GRP
                    x = bank4(Cc[0:META, 0, :], META)
                    TT(x.rearrange("p (h b) n -> p h b n", h=2), own_scores(META, META),
                       over(over(C("meta_neg", 0, META), 2), 2), ALU.add).then_inc(comb_ok, 1)
                else:
                    dve.wait_ge(comb, 5 * i + 5)
                    n, g = P, 1
                    alone(dve)
                    V.copy_predicated(Cc[:, 1, 0:DT], C("new_ok").bitcast(I32), B0[:, P:P + DT]).then_inc(comb_ok, 1)
                    x = Cc[:, 1, 0:P].unsqueeze(1)
                dve.wait_ge(comb_ok, 6 * i + k + 1)
                nsink = SK[0:n, ds(GRP * i, GRP)] if k < 5 else SKR[:, ds(i, 1)]
                t = Tally(sm_dve, 18 * i + 3 * k)
                m, nm, d = (sm[0:n, b, 4 * q:4 * q + g] for q in range(3))
                t.link(dve, V.tensor_reduce(m, x, AX.X, ALU.max, negate=True))
                t.link(dve, STT(out=nm, in0=m, scalar=HD ** -0.5, in1=nsink, op0=ALU.mult, op1=ALU.min))
                t.link(dve, TT(d, nm, nsink, ALU.subtract))

            def batch_keep(i, k):
                b = k % 2
                dve.wait_ge(p_ready, 6 * i + k + 1)
                n, g = ((P, GRP), (META, GRP), (P, 1))[max(k - 3, 0)]
                es, rs, den, rinv = (sm[0:n, b, 4 * q:4 * q + g] for q in (3, 4, 5, 6))
                if k >= 2:
                    dve.wait_ge(on_ready, 6 * i + k - 1)
                t = Tally(den_ready, 12 * i + 2 * k)
                t.link(dve, TT(den, es, rs, ALU.add))
                t.link(dve, V.reciprocal(rinv, den))
                if k == 5:
                    TT(Pn.rearrange("p (s u) -> p s u", u=DT), over(Pp[:, 1, 0:DT], DB),
                       C("new_block").rearrange("p (s u) -> p s u", u=DT), ALU.mult).then_inc(o_stat, 1)
                    dve.wait_ge(o_stat, 2 * i + 1)
                    TT(Pp[:, 1, 0:DT], Pp[:, 1, 0:DT], C("old_ok"), ALU.mult).then_inc(o_stat, 1)
                dve.wait_ge(pt_done, 6 * i + k + 1)
                if k >= 2:
                    dve.wait_ge(pv_done, 6 * i + k - 1)
                if k < 4:
                    TT(bank4(PTc[:, b, :]), bank4(B2), over(C("causalT"), GRP), ALU.mult)
                    last = TT(bank4(PTp[:, b, :]), bank4(B2), over(C("prevT"), GRP), ALU.mult)
                elif k == 4:
                    last = V.tensor_copy(PTc[SMP:EXT, 0, 0:GRP * META], B2[0:META, 0:GRP * META])
                else:
                    V.tensor_copy(diag_view(Pz, 0, GRP * DT), B2[:, 0:P].rearrange("p (s n) -> p s n", s=DB))
                    last = V.tensor_copy(PnT[0:SMP, :], B2[0:SMP, P:2 * P])
                last.then_inc(pt_kept, 1)

            def batch_scale(i, k):
                b = k % 2
                dve.wait_ge(pv_done, 6 * i + k + 1)
                if k == 5:
                    last = TS(on[:, 1, 0:HD], B3[:, 0:HD], sm[:, 1, 24:25], None, ALU.mult)
                else:
                    n = P if k < 4 else META
                    r = sm[0:n, b, 24:28].unsqueeze(2).broadcast_to([n, GRP, HD])
                    last = TT(bank4(on[0:n, b, :], HD), bank4(B3[0:n], HD), r, ALU.mult)
                last.then_inc(on_ready, 1)

            def batch_gate(i, k):
                dve.wait_ge(ot_done, 6 * i + k + 1)
                if k < 5:
                    n = P if k < 4 else META
                    cols = COLS[k] if k < 4 else slice(SEQ + SMP, TOK)
                    o = O[:, ds(2 * i, 2), cols]
                    STT(out=o, in0=B3[:, 0:2 * n].rearrange("p (u n) -> p u n", u=2), scalar=0.5, in1=o, op0=ALU.mult,
                        op1=ALU.mult).then_inc(b_gated, 1)
                else:
                    x = B3[0:HD, 0:P].rearrange("p (s r t) -> p s r t", r=GRP, t=DT)
                    for r in range(GRP):
                        a = HD * (r % 2)
                        o = tile(O, 2 * i + r // 2)[a:a + HD, SEQ:SEQ + SMP].rearrange("p (s t) -> p s t", t=DT)
                        STT(out=o, in0=x[:, :, r, :], scalar=0.5, in1=o, op0=ALU.mult, op1=ALU.mult).then_inc(b_gated, 1)

            def group_step(i, g):
                att_, proj = i is not None, g is not None

                def unit(j):
                    if proj:
                        gate(tile(O, 2 * g + j), THb, j, (thb_ready, 2 * g + j + 1))

                def run(*steps):
                    if att_:
                        for f, k in steps:
                            f(i, k)

                if att_:
                    for b in range(2):
                        dve.wait_ge(pp_free[b], 8 + SWA // 2 + 2 * i + 1)
                    spread_q(i)
                A_, B_, C_, D_ = batch_max, batch_keep, batch_scale, batch_gate
                unit(0)
                run((A_, 0))
                unit(1)
                run((A_, 1), (B_, 0), (C_, 0))
                for k in range(1, 5):
                    run((A_, k + 1), (D_, k - 1), (B_, k), (C_, k))
                run((D_, 4), (B_, 5), (C_, 5), (D_, 5))

            group_step(None, 0)
            with dve.Fori(0, KV - 1) as i:
                group_step(i, i + 1)
            group_step(KV - 1, None)

            with dve.Fori(0, NK // 4) as i:
                def keep_rows(j):
                    n4 = 4 * i + j
                    dve.wait_ge(yt_done, n4 + 1)
                    a, b = ((B0, B2), (B1, B3))[j % 2]
                    V.tensor_copy(YR[:, 0:NT, ds(n4 * P, P)], bank4(a)).then_inc(y_kept, 1)
                    V.tensor_copy(YR[0:EXT, NT, ds(n4 * P, P)], b[0:EXT, 0:P]).then_inc(y_kept, 1)

                for j in range(4):
                    dve.wait_ge(proj_done, NK + OUT_B + 4 * i + j + 1)
                    dve.wait_ge(xs_in[j], 16 * (NK // 4 + i + 1))
                    if j >= 2:
                        dve.wait_ge(xg_ready, 4 * i + j - 1)
                    TT(halves(x2[:, j % 2, :]), PV(j), halves(xs[:, j, :]), ALU.add).then_inc(pp_free[j % 2], 1)
                    if j:
                        keep_rows(j - 1)
                keep_rows(3)
                dve.wait_ge(xg_ready, 4 * i + 4)
            dve.wait_ge(ms_done, 2)
            TS(ms_c[:, 0:NT], B0[:, 0:2 * NT:2], 1.0 / DM, EPS, ALU.mult, ALU.add)
            cn.link(dve, TS(ms_c[0:EXT, NT:NT + 1], B0[0:EXT, 2 * NT:2 * NT + 1], 1.0 / DM, EPS, ALU.mult, ALU.add))
            dve.wait_ge(n_act, 6)
            newton(rs_c, ms_c, nt_c, cn)
            dve.wait_ge(y_kept, 2 * NK)
            for t in (0, 2, 4):
                n = WID[t]
                TS(YR[0:n, t, :], YR[0:n, t, :], rs_c[0:n, t:t + 1], None, ALU.mult).then_inc(y_scaled_v, 1)

        @block.gpsimd
        def _(pool):
            G = nc.gpsimd
            G.memset(acc[:], 0.0).then_inc(acc_zero, 1)
            gk = I["w_gk2_a"][0]
            G.dma_start(gk2[0:RANK, :], gk[:, 0:DK]).then_inc(gk2_in, 16)

            def load_state(h, s):
                src = I["state_gla"][0, s].rearrange("h (k p) v -> h p k v", p=P)
                src = src[h] if isinstance(h, int) else src[ds(h, 1)].rearrange("h p k v -> (h p) k v")
                alone(pool)
                G.dma_start(S0[:, s % SR, :, :], src).then_inc(s0_in[s % SR], 16)

            def store_state(h, s):
                dst = OUTS[3][0, s].rearrange("h (k p) v -> h p k v", p=P)
                dst = dst[h] if isinstance(h, int) else dst[ds(h, 1)].rearrange("h p k v -> (h p) k v")
                alone(pool)
                G.dma_start(dst, S0[:, s % SR, :, :]).then_inc(s0_out[s % SR], 16)

            for s in range(SR):
                load_state(0, s)
            for n in range(NK):
                pool.wait_ge(pp_free[n % 2], n // 2 + 1)
                alone(pool)
                G.dma_start(x0T[n], xt[:, n % 2, :]).then_inc(x0_out[n % 2], 16)
            for b in range(2):
                pool.wait_ge(x0_out[b], 8 * NK)

            def square(i, t):
                pool.wait_ge(o_kept, 5 * i + t + 1)
                if t:
                    pool.wait_ge(o_gated, 5 * i + t)
                n = VT * WID[t]
                x = o_sb[:, t % 2, 0:n]
                G.tensor_tensor(sq[:, 0:n], x, x, ALU.mult).then_inc(sq_ready, 1)

            def own_keys(i, s):
                if s >= 2:
                    pool.wait_ge(smp_u, 2 * DB * i + 2 * s - 2)
                alone(pool)
                G.tensor_scalar(kdm[0:SMP, s % 2, :], kdX[0:SMP, :], C("seq_of", 0, SMP)[:, s:s + 1], None,
                                ALU.mult).then_inc(kdm_ready, 1)

            def head_step(i, more):
                if more:
                    pool.wait_ge(proj_done, NK + USES * i + 10)
                    alone(pool)
                    G.dma_start(gk2[0:RANK, :], gk[:, ds(DK * (i + 1), DK)]).then_inc(gk2_in, 16)
                pool.wait_ge(vn_kept, 4 * i + 4)
                alone(pool)
                G.tensor_copy(Vs[0:SMP, :], Vx[0:SMP, :]).then_inc(vs_ready, 1)
                pool.wait_ge(kdt_ready, 3 * i + 3)
                own_keys(i, 0)
                own_keys(i, 1)
                for t in range(NT):
                    square(i, t)
                pool.wait_ge(s_ready, 10 * i + 10)
                dst = OUTS[2][0, 0].rearrange("h (k p) v -> h p k v", p=P)
                dst = dst[i] if isinstance(i, int) else dst[ds(i, 1)].rearrange("h p k v -> (h p) k v")
                alone(pool)
                G.dma_start(dst, S[:, :, :]).then_inc(state_out, 16)
                for s in range(DB):
                    if s >= 2:
                        own_keys(i, s)
                    pool.wait_ge(smp_new, 2 * DB * i + 2 * s + 2)
                    store_state(i, s)
                    if 1 <= s <= SR:
                        pool.wait_ge(s0_out[s - 1], 16 * (2 * i + 1))
                        load_state(i, s - 1 + SR)
                square(i, NT)
                for s in range(SR):
                    pool.wait_ge(s0_out[s], 16 * (2 * i + 2))
                    if more:
                        load_state(i + 1, s)

            with pool.Fori(0, HEADS - 1) as i:
                head_step(i, True)
            head_step(HEADS - 1, False)

            pool.wait_ge(acc_zero, 1)
            pool.wait_ge(o_gated, 5 * HEADS)
            pool.wait_ge(state_out, 16 * HEADS)

            def residual(base, src, dst, half):
                for j in range(4):
                    alone(pool)
                    G.dma_start(xs[:, j, :], src[j]).then_inc(xs_in[j], 16)

                def body(i, more):
                    for j in range(4):
                        n = 4 * i + j
                        pool.wait_ge(pp_free[j % 2], 8 + half + 2 * i + j // 2 + 1)
                        if more:
                            s_ = src[ds(n + 4, 1)].rearrange("a p n -> (a p) n")
                            alone(pool)
                            G.dma_start(xs[:, j, :], s_).then_inc(xs_in[j], 16)
                        if dst is not None:
                            d_ = dst[ds(n, 1)].rearrange("a p n -> (a p) n") if more else dst[n]
                            alone(pool)
                            G.dma_start(d_, tile(H, n)).then_inc(x1_out[j], 16)
                        pool.wait_ge(sq_a, base + n + 1)
                        if j or not more or base:
                            pool.wait_ge(acc_done, base + n) if not (isinstance(n, int) and base + n == 0) else None
                        else:
                            pool.wait_ge(acc_zero, 1)
                        G.tensor_tensor(acc[:], acc[:], sqa[:, j % 2, :], ALU.add).then_inc(acc_done, 1)
                    pool.wait_ge(acc_done, base + 4 * i + 4)

                with pool.Fori(0, NK // 4 - 1) as i:
                    body(i, True)
                body(NK // 4 - 1, False)

            residual(0, x0T, x1T, OUT_A // 2)
            pool.wait_ge(rb_ready, 2)
            G.memset(acc[:], 0.0).then_inc(acc_zero, 1)
            pool.wait_ge(acc_zero, 2)

            w = OUTS[6], OUTS[7]
            for c_, name in enumerate(("cache_k_win", "cache_v_win")):
                alone(pool)
                G.dma_start(w[c_][:, 0:P - DT], I[name][:, DT:P]).then_inc(win_out, 16)
            pool.wait_ge(vn_kept, 4 * HEADS + 4)
            pool.wait_ge(setup, 3)
            G.dma_start(Wm[P - META:P, :], Wx[SMP:EXT, :]).then_inc(vm_in, 16)
            G.dma_start(OUTS[5][0].rearrange("w k d -> w (k d)"), Wn[:, NT - 1, :]).then_inc(win_out, 16)
            for s in range(DB):
                alone(pool)
                G.dma_start(w[1][s, P - DT:P].rearrange("t k d -> t (k d)"),
                            Wx[DT * s:DT * (s + 1), :]).then_inc(win_out, 16)
            pool.wait_ge(kw_kept, 2)
            G.dma_start(OUTS[4][0].rearrange("w k d -> w (k d)"), kwin).then_inc(win_out, 16)
            for s in range(DB):
                alone(pool)
                G.dma_start(w[0][s, P - DT:P].rearrange("t k d -> t (k d)"),
                            kwx[DT * s:DT * (s + 1), :]).then_inc(win_out, 16)
            pool.wait_ge(vm_in, 16)

            def load_cache(g):
                for c_, (name, buf) in enumerate((("cache_k_win", Kc), ("cache_v_win", Vc))):
                    src = I[name].rearrange("b w k d -> w b k d")
                    if isinstance(g, int):
                        src = src[:, :, g, :]
                    else:
                        src = src[:, :, ds(g, 1), :].rearrange("w b k d -> w b (k d)")
                    alone(pool)
                    G.dma_start(buf[:, 0, :].rearrange("p (b d) -> p b d", b=DB), src).then_inc(kc_in[c_], 16)

            load_cache(0)

            def group_step(i, more):
                for b in range(2):
                    pool.wait_ge(pp_free[b], 8 + SWA // 2 + 2 * i + 2)
                alone(pool)
                G.tensor_copy(qB[:].rearrange("p a b -> p (a b)"), qN[:].rearrange("p a b -> p (a b)")).then_inc(q_copied, 1)
                alone(pool)
                G.tensor_copy(kg, tile(kdup, i)).then_inc(stage_step, 1)
                alone(pool)
                G.memset(bank4(Cc[:, 0, :])[:, :, 0:P - META], NEG).then_inc(c_fill, 1)
                alone(pool)
                G.tensor_copy(vg, Wn[:, :, ds(HD * i, HD)]).then_inc(stage_step, 1)
                pool.wait_ge(stage_step, 3 * i + 2)
                alone(pool)
                G.tensor_copy(vxg[0:EXT, :], Wx[0:EXT, ds(HD * i, HD)])
                alone(pool)
                G.tensor_copy(vmg[96:P, :], Wm[96:P, ds(HD * i, HD)]).then_inc(stage_step, 1)
                pool.wait_ge(stage_step, 3 * i + 3)
                src = tile(kdup, i)[0:HD, SEQ:SEQ + SMP].rearrange("p (s t) -> p s t", t=DT)
                alone(pool)
                G.tensor_copy(kcat[0:HD, :, P:P + DT], src).then_inc(staged, 1)
                pool.wait_ge(pv_done, 6 * i + 6)
                if more:
                    load_cache(i + 1)

            with pool.Fori(0, KV - 1) as i:
                group_step(i, True)
            group_step(KV - 1, False)
            pool.wait_ge(b_gated, 9 * KV)
            pool.wait_ge(win_out, 16 * (2 + 1 + DB + 1 + DB))
            residual(NK, x1T, None, OUT_B // 2)
            for t, s_ in ((0, (y_scaled_v, 1)), (1, (y_scaled, 1)), (2, (y_scaled_v, 2)), (3, (y_scaled, 2))):
                pool.wait_ge(*s_)
                alone(pool)
                G.dma_start(OUTS[0][0, t * P:(t + 1) * P, :], YR[:, t, :]).then_inc(y_out, 16)
            pool.wait_ge(y_scaled_v, 3)
            G.dma_start(OUTS[1].rearrange("b t d -> (b t) d"), YR[0:SMP, NT, :]).then_inc(y_out, 16)
            pool.wait_ge(y_out, 80)


_INS = ['x_prompt', 'x_sample', 'state_gla', 'cache_k_win', 'cache_v_win', 'meta_tokens', 'norm_a', 'w_in_a', 'w_gk2_a',
        'b_gk2_a', 'onorm_a', 'w_out_a', 'norm_kv', 'w_kv', 'norm_b', 'w_in_b', 'sinks_b', 'w_out_b', 'norm_f']
_OUTS = [(1, SEQ, DM), (DB, DT, DM), (1, 1, HEADS, DK, DV), (1, DB, HEADS, DK, DV), (1, P, KV, HD), (1, P, KV, HD),
         (DB, P, KV, HD), (DB, P, KV, HD)]


def kernel(**inputs):
    import concourse.bacc as bacc
    from concourse.bass_utils import run_bass_kernel_spmd

    nc = bacc.Bacc("TRN2", target_bir_lowering=False, num_devices=1)
    arrays, ins = {}, {}
    for name in _INS:
        a = np.ascontiguousarray(inputs[name])
        arrays[f"in_{name}"] = a
        ins[name] = nc.dram_tensor(f"in_{name}", a.shape, mybir.dt.from_np(a.dtype), kind="ExternalInput").ap()
    table, _ = consts_array()
    arrays["in_consts"] = table
    ins["consts"] = nc.dram_tensor("in_consts", table.shape, FP32, kind="ExternalInput").ap()
    outs = [nc.dram_tensor(f"out_{n}", shape, FP32, kind="ExternalOutput").ap() for n, shape in enumerate(_OUTS)]
    yoco_kernel(nc, ins, outs)
    r = run_bass_kernel_spmd(nc, [arrays], core_ids=[0])
    return tuple(r.results[0][f"out_{n}"] for n in range(len(_OUTS)))
```

```python
import numpy as np
import concourse.bass as bass
from concourse import mybir
from contextlib import ExitStack

FP32 = mybir.dt.float32
I32 = mybir.dt.int32
ALU = mybir.AluOpType
ACT = mybir.ActivationFunctionType
AX = mybir.AxisListType

P = 128
DM = 2048
NK = DM // P
SEQ, META, DB, DT = 512, 16, 8, 4
SMP = DB * DT
EXT = SMP + META
TOK = SEQ + EXT
HALF = TOK // 2
NT = SEQ // P
HEADS, DK, DV = 4, 256, 512
KT, VT = DK // P, DV // P
RANK = 16
GN = 16.0
KV = 8
GRP = 4
HD = 64
EPS = 1e-6
NEG = -1e30
LEVELS = [64, 32, 16, 8, 4, 2, 1]
NL = len(LEVELS) + 1
NLX = 5
WR = 4
SR = 4
USES = 14
OUT_A = USES * HEADS
K_A = NK - VT
OUT_A2 = OUT_A + NK
KVP = OUT_A2 + NK
SWA = KVP + 8
OUT_B = SWA + 4 * KV
W_OUT_A = 12 * HEADS
W_KV = W_OUT_A + NK + WR
W_SWA = W_KV + 8
W_OUT_B = W_SWA + 4 * KV


def consts_array():
    parts, where, at = [], {}, 0

    def put(name, a):
        nonlocal at
        full = np.zeros((P, a.shape[1]), np.float32)
        full[:a.shape[0]] = a
        parts.append(full)
        where[name] = (at, at + a.shape[1])
        at += a.shape[1]

    i = np.arange(P)
    put("ident", np.eye(P))
    for h in LEVELS:
        put(f"level{h}", (i[:, None] // (2 * h) == i[None] // (2 * h)) & (i[:, None] % (2 * h) < h)
            & (i[None] % (2 * h) >= h))
    put("level0", np.eye(P))
    e = np.arange(EXT)
    for h in LEVELS[-4:]:
        m = (e[:, None] // (2 * h) == e[None] // (2 * h)) & (e[:, None] % (2 * h) < h) & (e[None] % (2 * h) >= h)
        if 2 * h > DT:
            m &= (e[:, None] >= SMP) & (e[None] >= SMP)
        put(f"ext{h}", m)
    put("ext0", np.eye(EXT))
    put("causal", i[None] <= i[:, None])
    put("causalT", i[:, None] <= i[None])
    put("prevT", i[:, None] > i[None])
    m = np.arange(META)
    put("meta_neg", np.where(m[None] > m[:, None], NEG, 0.0))
    keep = np.ones((P, TOK))
    keep[:, 0:SEQ:P] = 0
    keep[:, SEQ:SEQ + SMP:DT] = 0
    keep[:, SEQ + SMP] = 0
    put("keep", keep)
    row_t, row_s = i % DT, i // (GRP * DT)
    u = np.arange(DT)
    put("new_ok", u[None] <= row_t[:, None])
    put("old_ok", u[None] > row_t[:, None])
    c = np.arange(SMP)
    put("new_block", (c[None] // DT == row_s[:, None]) & (c[None] % DT <= row_t[:, None]))
    put("seq_of", (c[:, None] // DT == np.arange(DB)[None]))
    return np.ascontiguousarray(np.concatenate(parts, 1).astype(np.float32)), where


class Tally:

    def __init__(self, sem, base=0):
        self.sem, self.base, self.n = sem, base, 0

    def inc(self, ins):
        ins.then_inc(self.sem, 1)
        self.n += 1

    @property
    def value(self):
        return self.base + self.n

    def link(self, eng, ins):
        self.inc(ins)
        eng.wait_ge(self.sem, self.value)


def yoco_kernel(nc, I, OUTS):
    ctx = ExitStack()
    _, where = consts_array()
    with ctx:
        def sb(name, shape, dt=FP32):
            return ctx.enter_context(nc.sbuf_tensor(name, shape, dt))

        def sem(name):
            return ctx.enter_context(nc.semaphore(name))

        def sems(name, n):
            return [sem(f"{name}{k}") for k in range(n)]

        H = sb("H", [P, NK, TOK])
        O = sb("O", [P, NK, TOK])
        W = sb("W", [P, WR, NK, P])
        CST = sb("CST", [P, max(b for _, b in where.values())])
        ones = sb("ones", [P, P])
        RB = sb("RB", [P, TOK])
        GV = sb("GV", [P, 76])
        SK = sb("SK", [P, 4 * KV])
        SKR = sb("SKR", [P, KV])
        small = sb("small", [P, 96])
        acc = sb("acc", [P, TOK])

        def C(name, p0=0, p1=P):
            a, b = where[name]
            return CST[p0:p1, a:b]

        ident = C("ident")
        G_A, G_KV, G_B, G_F, B_GK, G_O = 0, 16, 32, 48, 64, 72

        AR = sb("AR", [P, 22700])
        top = [0]

        def take(shape):
            n = int(np.prod(shape))
            v = AR[:, top[0]:top[0] + n]
            top[0] += n
            assert top[0] <= 22700, top
            if len(shape) == 2:
                v = v.rearrange("p (a b) -> p a b", a=shape[0])
            if len(shape) == 3:
                v = v.rearrange("p (a b c) -> p a b c", a=shape[0], b=shape[1])
            return v

        XR = take([5, DM])
        junk = take([DM])
        xt = take([2, TOK])
        NV = take([P])
        diag = take([5, P])
        sx = take([P])
        top[0] = 0
        Dd = take([2, KT * TOK])
        Dd = [Dd[:, n, :].rearrange("p (a b) -> p a b", a=KT) for n in range(2)]
        Tt = take([2, KT * TOK])
        Tt = [Tt[:, n, :].rearrange("p (a b) -> p a b", a=KT) for n in range(2)]
        qT, kT, bT = take([KT, TOK]), take([KT, TOK]), take([KT, TOK])
        kd, qe = Dd[1], Tt[1]
        kdT, kdX = take([NT, DK]), take([DK])
        Vn, Vx, Vs = take([NT, DV]), take([DV]), take([DV])
        TH = take([2, TOK])
        att, attx = take([NT, P]), take([EXT])
        S = take([KT, DV])
        S0 = take([SR, KT, DV])
        o_sb = take([2, VT * P])
        sq = take([VT * P])
        rr, ra, rv, rl = take([P]), take([P]), take([P]), take([P])
        kdm = take([2, DK])
        glr = take([TOK])
        gk2 = take([DK])
        wglr = take([NK, RANK])
        el = take([KT, NT + DB + 1])
        top[0] = 10240
        xs = take([4, TOK])
        sqa = take([2, TOK])
        x2 = take([2, TOK])
        xg = take([2, TOK])
        top[0] = 0
        YR = take([5, DM])
        top[0] = 0
        kdup = take([KV, TOK])
        Wn, Wx, Wm = take([NT, KV * HD]), take([KV * HD]), take([KV * HD])
        THb = take([2, TOK])
        qB = take([2, TOK])
        Cc, Pp = take([2, GRP * P]), take([2, GRP * P])
        PTc, PTp = take([2, GRP * P]), take([2, GRP * P])
        on = take([2, GRP * HD])
        Kc, Vc = take([1, DB * HD]), take([1, DB * HD])
        kcat = take([DB, P + DT])
        kg, vg, vxg, vmg = take([TOK]), take([NT, HD]), take([HD]), take([HD])
        sm = take([2, 32])
        Qz, Pz = take([DB, P]), take([DB, P])
        Pn, PnT = take([SMP]), take([P])
        kwin, kwx = take([KV * HD]), take([KV * HD])

        PP = [ctx.enter_context(nc.psum_tensor(f"PP{n}", [P, 2, 512], FP32)) for n in range(2)]
        BS = ctx.enter_context(nc.psum_tensor("BS", [P, 2, 512], FP32))
        B0, B1 = BS[:, 0, :], BS[:, 1, :]
        B2, B3 = [ctx.enter_context(nc.psum_tensor(f"B{n}", [P, 512], FP32)) for n in (2, 3)]

        x0T = nc.dram_tensor("x0T", (NK, P, TOK), FP32, kind="Internal").ap()
        x1T = nc.dram_tensor("x1T", (NK, P, TOK), FP32, kind="Internal").ap()

        cst_in, x_in, vec_in = sem("cst_in"), sems("x_in", 5), sem("vec_in")
        w_in = sems("w_in", WR)
        wglr_in, gk2_in = sem("wglr_in"), sem("gk2_in")
        proj_done, pp_free = sem("proj_done"), sems("pp_free", 2)
        setup, sink_rows, passed, stage_step = sem("setup"), sem("sink_rows"), sem("passed"), sem("stage_step")
        vecs_done, vecs_kept = sem("vecs_done"), sem("vecs_kept")
        row_ss, rs_act, rs_dve = sem("row_ss"), sem("rs_act"), sem("rs_dve")
        diag_ready, bc_done, rb_ready = sem("diag_ready"), sem("bc_done"), sem("rb_ready")
        h_ready, x0_out, glr_done, glr_kept = sem("h_ready"), sems("x0_out", 2), sem("glr_done"), sem("glr_kept")
        th_ready, vtr_done, vn_kept = sem("th_ready"), sem("vtr_done"), sem("vn_kept")
        g_act, decay_exp = sem("g_act"), sem("decay_exp")
        d_ready, e_ready, t_ready = sem("d_ready"), sem("e_ready"), sem("t_ready")
        scores_done, scores_kept, attx_ready = sem("scores_done"), sem("scores_kept"), sem("attx_ready")
        kde_ready, kd_ready, qe_ready = sem("kde_ready"), sem("kd_ready"), sem("qe_ready")
        kdtr_done, kdt_ready = sem("kdtr_done"), sem("kdt_ready")
        o_done, o_kept, u_done, s_ready = sem("o_done"), sem("o_kept"), sem("u_done"), sem("s_ready")
        sq_ready, ss_done, r_act, r_dve, o_gated = (sem("sq_ready"), sem("ss_done"), sem("r_act"), sem("r_dve"),
                                                    sem("o_gated"))
        state_out = sem("state_out")
        s0_in, s0_out = sems("s0_in", SR), sems("s0_out", SR)
        extbase, vs_ready, kdm_ready = sem("extbase"), sem("vs_ready"), sem("kdm_ready")
        smp_u, smp_new = sem("smp_u"), sem("smp_new")
        h_in = sems("h_in", 4)
        xs_in, sq_a, acc_done, x1_out, acc_zero = (sems("xs_in", 4), sem("sq_a"), sem("acc_done"), sems("x1_out", 4),
                                                   sem("acc_zero"))
        ms_done, n_act, n_dve = sem("ms_done"), sem("n_act"), sem("n_dve")
        kw_done, kw_kept, win_out, vm_in = sem("kw_done"), sem("kw_kept"), sem("win_out"), sem("vm_in")
        thb_ready = sem("thb_ready")
        sc_done, comb, comb_ok, sm_dve, sm_act = sem("sc_done"), sem("comb"), sem("comb_ok"), sem("sm_dve"), sem("sm_act")
        p_ready, pt_done, pt_kept, pv_done, on_ready = (sem("p_ready"), sem("pt_done"), sem("pt_kept"), sem("pv_done"),
                                                        sem("on_ready"))
        ot_done, b_gated = sem("ot_done"), sem("b_gated")
        kc_in, kct_done, kcat_ready, qz_ready, c_fill = (sems("kc_in", 2), sem("kct_done"), sem("kcat_ready"),
                                                         sem("qz_ready"), sem("c_fill"))
        staged, o_stat = sem("staged"), sem("o_stat")
        b_step, den_ready, y_scaled_v = sem("b_step"), sem("den_ready"), sem("y_scaled_v")
        xg_ready, yt_done, y_kept, y_scaled, y_out = (sem("xg_ready"), sem("yt_done"),
                                                                sem("y_kept"), sem("y_scaled"), sem("y_out"))

        ds = bass.ds
        COLS = [slice(t * P, (t + 1) * P) for t in range(NT)] + [slice(SEQ, TOK)]
        WID = [P] * NT + [EXT]

        def halves(ap):
            return ap.rearrange("p (c n) -> p c n", c=2)

        def PV(k):
            return PP[k % 2][:, :, 0:HALF]

        def tile(buf, n):
            return buf[:, n, :] if isinstance(n, int) else buf[:, ds(n, 1), :].rearrange("p a n -> p (a n)")

        def bank4(b, w=P):
            return b[:, 0:4 * w].rearrange("p (a n) -> p a n", a=4)

        def own_scores(n=P, w=P):
            return BS[0:n].rearrange("p b (h x) -> p h b x", h=2)[:, :, :, 0:w]

        def old_scores(a=0):
            return BS[:].rearrange("p b (h x) -> p h b x", h=2)[:, :, :, P + a:2 * P]

        def by_head(ap, w=P):
            return ap.rearrange("p (h b n) -> p h b n", h=2, b=2)[:, :, :, 0:w]

        def over(ap, n, axis=1):
            shape = list(ap.shape)
            shape.insert(axis, n)
            return ap.unsqueeze(axis).broadcast_to(shape)

        def right(ap, l):
            h = LEVELS[l]
            return ap.rearrange("p (b c) -> p b c", c=2 * h)[:, :, h:2 * h]

        def alone(eng):
            eng.sem_inc(passed, 1)

        ss_c, ms_c, lg_c, rs_c, nt_c = (small[:, 40 + 5 * k:45 + 5 * k] for k in range(5))
        eps_c = small[:, 65:66]

        block = ctx.enter_context(nc.Block())

        @block.sync
        def _(sp):
            sp.dma_start(CST[:], I["consts"]).then_inc(cst_in, 16)
            for t in range(NT):
                sp.dma_start(XR[:, t, :], I["x_prompt"][0, t * P:(t + 1) * P, :]).then_inc(x_in[t], 16)
            sp.dma_start(XR[0:SMP, NT, :], I["x_sample"].rearrange("b t d -> (b t) d")).then_inc(x_in[NT], 16)
            sp.dma_start(XR[SMP:EXT, NT, :], I["meta_tokens"]).then_inc(x_in[NT], 16)
            rows = ((G_A, "norm_a", NK), (G_B, "norm_b", NK), (B_GK, "b_gk2_a", KT * HEADS), (G_O, "onorm_a", VT))
            for at, name, n in rows:
                sp.dma_start(NV[at:at + n, :], I[name].rearrange("a (n p) -> (a n) p", p=P)).then_inc(vec_in, 16)
            for at, name in ((G_KV, "norm_kv"), (G_F, "norm_f")):
                sp.dma_start(NV[at:at + NK, :], I[name].rearrange("(n p) -> n p", p=P)).then_inc(vec_in, 16)
            sp.dma_start(small[0:1, 0:32], I["sinks_b"]).then_inc(vec_in, 16)
            sp.dma_start(small[0:KV, 32:36], I["sinks_b"].rearrange("a (g r) -> (a g) r", r=GRP)).then_inc(vec_in, 16)
            w_in_a = I["w_in_a"][0].rearrange("(k p) n -> p k n", p=P)
            sp.dma_start(wglr, w_in_a[:, :, 6144:6144 + RANK]).then_inc(wglr_in, 16)

            def weights(j, src, col, freed):
                if freed is not None:
                    sp.wait_ge(proj_done, NK + freed)
                alone(sp)
                sp.dma_start(W[:, j % WR, :, :], src[:, :, ds(col, P)]).then_inc(w_in[j % WR], 16)

            def head_weights(h):
                kinds = [4096 + h * DV, 4096 + h * DV + P, 4096 + h * DV + 2 * P, 4096 + h * DV + 3 * P,
                         2048 + h * DV, 2048 + h * DV + P, 2048 + h * DV + 2 * P, 2048 + h * DV + 3 * P,
                         1024 + h * DK, 1024 + h * DK + P, h * DK, h * DK + P]
                for j, col in enumerate(kinds):
                    first = isinstance(h, int) and j < WR
                    weights(j, w_in_a, col, None if first else USES * h + (j - 3) + (j == 11))

            head_weights(0)
            with sp.Fori(1, HEADS) as h:
                head_weights(h)
            w_out_a = I["w_out_a"][0].rearrange("(k p) n -> p k n", p=P)
            with sp.Fori(0, NK // 4) as i:
                for j in range(4):
                    sp.wait_ge(proj_done, NK + OUT_A + 4 * i + j - 3)
                    alone(sp)
                    sp.dma_start(W[:, j, 0:K_A, :], w_out_a[:, 0:K_A, ds((4 * i + j) * P, P)]).then_inc(w_in[j], 16)
            for j in range(WR):
                sp.wait_ge(proj_done, NK + OUT_A + 12 + j + 1)
                sp.dma_start(W[:, j].rearrange("p (k u) n -> p k (u n)", k=VT),
                             w_out_a[:, K_A:NK, j * 4 * P:(j + 1) * 4 * P]).then_inc(w_in[j], 16)
            w_kv = I["w_kv"].rearrange("(k p) n -> p k n", p=P)
            for j in range(8):
                weights(j, w_kv, j * P, KVP + j - 3 if j >= WR else OUT_A2 + 4 * (j + 1))
            w_in_b = I["w_in_b"][0].rearrange("(k p) n -> p k n", p=P)
            with sp.Fori(0, KV) as g:
                for j, col in enumerate((2048, 2048 + P, 0, P)):
                    weights(j, w_in_b, g * (GRP * HD) + col, SWA + 4 * g + j - 3)
            w_out_b = I["w_out_b"][0].rearrange("(k p) n -> p k n", p=P)
            with sp.Fori(0, NK // 4) as i:
                for j in range(4):
                    weights(j, w_out_b, (4 * i + j) * P, OUT_B + 4 * i + j - 3)

        @block.tensor
        def _(pe):
            mm = nc.tensor.matmul

            def transpose(out, in_):
                k = in_.shape[0]
                b = in_.start_partition() if callable(in_.start_partition) else in_.start_partition
                return nc.tensor.transpose(out, in_, CST[b:b + k, b:b + k])

            pe.wait_ge(cst_in, 16)
            pe.wait_ge(vec_in, 128)
            pe.wait_ge(setup, 1)
            transpose(B2[:, 0:76], NV[0:76, :])
            mm(B3[:, 0:32], ones[0:1, :], small[0:1, 0:32], start=True, stop=True)
            pe.wait_ge(sink_rows, 1)
            mm(B3[:, 32:40], sx[0:KV, :], ident[0:KV, 0:KV], start=True, stop=True).then_inc(vecs_done, 1)

            def x_tile(n):
                if n >= 2:
                    pe.wait_ge(pp_free[n % 2], n // 2)
                for t in range(NT):
                    if n == 0:
                        pe.wait_ge(x_in[t], 16)
                    transpose(PP[n % 2][:, 0, COLS[t]], XR[:, t, n * P:(n + 1) * P])
                if n == 0:
                    pe.wait_ge(x_in[NT], 32)
                transpose(PP[n % 2][:, 1, 0:EXT], XR[0:EXT, NT, n * P:(n + 1) * P]).then_inc(proj_done, 0 + 1)

            x_tile(0)
            x_tile(1)
            pe.wait_ge(diag_ready, 5)
            for t in range(NT):
                mm(B0[:, COLS[t]], ones[:], diag[:, t, :], start=True, stop=True)
            mm(B1[:, 0:EXT], ones[0:EXT, :], diag[0:EXT, NT, 0:EXT], start=True, stop=True).then_inc(bc_done, 1)
            for n in range(2, NK):
                x_tile(n)
            pe.wait_ge(wglr_in, 16)
            pe.wait_ge(vecs_kept, 2)
            for k in range(NK):
                pe.wait_ge(h_ready, k + 1)
                for c, b in enumerate((B2, B3)):
                    last = mm(b[0:RANK, 0:HALF], wglr[:, k, :], H[:, k, c * HALF:(c + 1) * HALF], start=(k == 0),
                              stop=(k == NK - 1))
            last.then_inc(glr_done, 1)

            def project(lap, jw, half, j, src, fresh=None, ks=(0, NK)):
                if ks[0] == 0:
                    pe.wait_ge(w_in[jw % WR], 16 * (lap + jw // WR + 1))
                    pe.wait_ge(pp_free[j % 2], 8 + half + j // 2)
                for k in range(*ks):
                    if fresh is not None:
                        pe.wait_ge(h_ready, fresh + k + 1)
                    for c in range(2):
                        last = mm(PP[j % 2][:, c, 0:HALF], W[:, jw % WR, k, :], src[:, k, c * HALF:(c + 1) * HALF],
                                  start=(k == 0), stop=(k == NK - 1))
                if ks[1] == NK:
                    last.then_inc(proj_done, 1)

            def head_unit(h, jw, ks):
                project(3 * h, jw, 7 * h, jw if jw < 8 else jw + 2, H, ks=ks)

            def decay(h, kt):
                pe.wait_ge(pp_free[kt], 8 + 7 * h + 4)
                if kt == 0:
                    pe.wait_ge(gk2_in, 16 * (h + 1))
                    pe.wait_ge(glr_kept, 1)
                for c in range(2):
                    last = mm(PP[kt][:, c, 0:HALF], gk2[0:RANK, kt * P:(kt + 1) * P],
                              glr[0:RANK, c * HALF:(c + 1) * HALF], start=True, stop=True)
                last.then_inc(proj_done, 1)

            def v_rows(h, j, after=None):
                pe.wait_ge(pp_free[j % 2], 8 + 7 * h + (4 + j) // 2 + 1)
                if j == 0 and after is not None:
                    pe.wait_ge(o_gated, 5 * after + 4)
                    pe.wait_ge(s_ready, 10 * after + 10)
                elif j:
                    pe.wait_ge(vn_kept, 4 * h + j)
                for t in range(NT):
                    transpose(B1[:, COLS[t]], TH[:, j % 2, COLS[t]])
                transpose(B3[0:EXT, 0:P], TH[:, j % 2, SEQ:TOK]).then_inc(vtr_done, 1)

            def scores(i, l):
                a = b = Tt[l % 2]
                if l < NL - 1:
                    pe.wait_ge(t_ready, (NL - 1) * i + l + 1)
                else:
                    a, b = kT, qT
                if l >= 2:
                    pe.wait_ge(scores_kept, NL * i + l - 1)
                bank = (B0, B1)[l % 2]

                def queries(kt, cols):
                    return b[:, kt, cols] if l == NL - 1 else right(b[:, kt, cols], l)

                w = P if l == NL - 1 else P // 2
                for t in range(NT):
                    for kt in range(KT):
                        last = mm(bank[:, t * w:(t + 1) * w], a[:, kt, COLS[t]], queries(kt, COLS[t]), start=(kt == 0),
                                  stop=(kt == KT - 1))
                x = l - (NL - NLX)
                if x >= 0:
                    w = EXT if l == NL - 1 else EXT // 2
                    for kt in range(KT):
                        last = mm(B2[0:EXT, x * EXT:x * EXT + w], a[:, kt, SEQ:TOK], queries(kt, slice(SEQ, TOK)),
                                  start=(kt == 0), stop=(kt == KT - 1))
                last.then_inc(scores_done, 1)

            def kd_rows(i):
                pe.wait_ge(kd_ready, i + 1)
                for kt, bank in enumerate((B3, B0)):
                    if kt:
                        pe.wait_ge(scores_kept, NL * i + NL - 1)
                    for t in range(NT):
                        last = transpose(bank[:, COLS[t]], kd[:, kt, COLS[t]])
                    last.then_inc(kdtr_done, 1)
                pe.wait_ge(scores_kept, NL * i + NL)
                alone(pe)
                for kt in range(KT):
                    last = transpose(B1[0:EXT, kt * P:(kt + 1) * P], kd[:, kt, SEQ:TOK])
                last.then_inc(kdtr_done, 1)

            def update(i, t):
                for kt, bank in enumerate((B2, B3)):
                    if t < 0:
                        last = mm(bank[:], kdX[SMP:EXT, kt * P:(kt + 1) * P], Vx[SMP:EXT, :], start=True, stop=True)
                    else:
                        last = mm(bank[:], kdT[:, t, kt * P:(kt + 1) * P], Vn[:, t, :], start=True, stop=True)
                    last.then_inc(u_done, 1)

            def meta_update(i):
                pe.wait_ge(kdt_ready, 3 * i + 3)
                pe.wait_ge(vn_kept, 4 * i + 4)
                pe.wait_ge(attx_ready, NLX * i + NLX)
                alone(pe)
                update(i, -1)

            def sumsq(i, t):
                pe.wait_ge(sq_ready, 5 * i + t + 1)
                if t:
                    pe.wait_ge(o_gated, 5 * i + t)
                w = WID[t]
                for v in range(VT):
                    last = mm(B1[:, 0:w], ones[:], sq[:, v * w:(v + 1) * w], start=(v == 0), stop=(v == VT - 1))
                last.then_inc(ss_done, 1)

            def tile_step(i, t):
                pe.wait_ge(s_ready, 10 * i + 2 * (t + 1))
                if t == 0:
                    pe.wait_ge(qe_ready, i + 1)
                else:
                    pe.wait_ge(o_kept, 5 * i + t)
                for v in range(VT):
                    out = B0[:, v * P:(v + 1) * P]
                    mm(out, Vn[:, t, v * P:(v + 1) * P], att[:, t, :], start=True, stop=False)
                    for kt in range(KT):
                        last = mm(out, S[:, kt, v * P:(v + 1) * P], qe[:, kt, COLS[t]], start=False, stop=(kt == KT - 1))
                last.then_inc(o_done, 1)
                if t:
                    sumsq(i, t - 1)
                update(i, t)

            def ext_base(i):
                pe.wait_ge(o_kept, 5 * i + 4)
                for v in range(VT):
                    last = mm(B0[:, v * EXT:(v + 1) * EXT], Vx[0:EXT, v * P:(v + 1) * P], attx[0:EXT, :],
                              start=(v == 0), stop=False, skip_group_check=True)
                last.then_inc(extbase, 1)

            def seq_state(i, s, kt):
                if kt == 0:
                    pe.wait_ge(s0_in[s % SR], 16 * (2 * i + s // SR + 1))
                    for v in range(VT):
                        for k2 in range(KT):
                            a = v * EXT + DT * s
                            last = mm(B0[:, a:a + DT], S0[:, s % SR, k2, v * P:(v + 1) * P],
                                      qe[:, k2, SEQ + DT * s:SEQ + DT * (s + 1)], start=False,
                                      stop=(s == DB - 1 and v == VT - 1 and k2 == KT - 1), skip_group_check=True)
                    if s == DB - 1:
                        last.then_inc(o_done, 1)
                    pe.wait_ge(kdm_ready, DB * i + s + 1)
                    if s == 0:
                        pe.wait_ge(vs_ready, i + 1)
                        pe.wait_ge(s_ready, 10 * i + 10)
                    else:
                        pe.wait_ge(smp_new, 2 * DB * i + 2 * s)
                else:
                    pe.wait_ge(smp_new, 2 * DB * i + 2 * s + 1)
                mm(B2[:], kdm[0:SMP, s % 2, kt * P:(kt + 1) * P], Vs[0:SMP, :], start=True, stop=True).then_inc(smp_u, 1)

            def out_early(a, b):
                for f in range(a, b):
                    n, k = divmod(f, K_A)
                    if k == 0:
                        pe.wait_ge(w_in[n % WR], 16 * ((W_OUT_A + n) // WR + 1))
                        pe.wait_ge(pp_free[n % 2], 8 + (OUT_A + n) // 2)
                    if f == 0:
                        pe.wait_ge(o_gated, 5 * (HEADS - 1))
                    for c in range(2):
                        last = mm(PP[n % 2][:, c, 0:HALF], W[:, n % WR, k, :], O[:, k, c * HALF:(c + 1) * HALF],
                                  start=(k == 0), stop=(k == K_A - 1))
                    if k == K_A - 1:
                        last.then_inc(proj_done, 1)

            def head_step(i, h):
                rec, proj = i is not None, h is not None

                def piece(n, parts):
                    a, b = n * (NK // parts), (n + 1) * (NK // parts)
                    if proj:
                        head_unit(h, a // NK, (a % NK, (b - 1) % NK + 1))
                    else:
                        out_early(a, b)

                for n in range(8):
                    piece(n, 2)
                    if rec and n < 7:
                        scores(i, n)
                        n == 6 and scores(i, 7)
                    elif rec:
                        kd_rows(i)
                        meta_update(i)
                for t in range(NT):
                    piece(8 + t, 2)
                    rec and tile_step(i, t)
                for q in range(24):
                    piece(24 + q, 4)
                    if rec:
                        if q == 0:
                            sumsq(i, NT - 1)
                            ext_base(i)
                        elif q <= 2 * DB:
                            seq_state(i, (q - 1) // 2, (q - 1) % 2)
                        elif q == 18:
                            if proj:
                                pe.wait_ge(vn_kept, 4 * h + 4)
                            sumsq(i, NT)
                    if proj:
                        if q in (3, 5, 7, 9):
                            v_rows(h, (q - 3) // 2, i)
                        if q in (6, 10):
                            decay(h, (q - 6) // 4)

            head_step(None, 0)
            with pe.Fori(0, HEADS - 1) as i:
                head_step(i, i + 1)
            head_step(HEADS - 1, None)

            def mean_square():
                for c, b in enumerate((B0, B1)):
                    last = mm(b[:, 0:HALF], ones[:], acc[:, c * HALF:(c + 1) * HALF], start=True, stop=True)
                last.then_inc(ms_done, 1)

            pe.wait_ge(o_gated, 5 * HEADS)
            for n in range(NK):
                m, u = divmod(n, 4)
                if u == 0:
                    pe.wait_ge(w_in[m], 16 * (W_OUT_A // WR + 4 + 1))
                pe.wait_ge(pp_free[n % 2], 8 + (OUT_A2 + n) // 2)
                for k in range(VT):
                    for c in range(2):
                        last = mm(PP[n % 2][:, c, 0:HALF], W[:, m, 4 * k + u, :], O[:, K_A + k, c * HALF:(c + 1) * HALF],
                                  start=(k == 0), stop=(k == VT - 1))
                last.then_inc(proj_done, 1)
            pe.wait_ge(acc_done, NK)
            mean_square()

            for j in range(8):
                project(W_KV // 4, j, KVP // 2, j, O, fresh=NK if j == 0 else None)
                if j >= 5:
                    kv_rows = j - 5
                    v_rows_kv = kv_rows
                    pe.wait_ge(pp_free[v_rows_kv % 2], 8 + KVP // 2 + (4 + v_rows_kv) // 2 + 1)
                    if v_rows_kv:
                        pe.wait_ge(vn_kept, 4 * HEADS + v_rows_kv)
                    else:
                        pe.wait_ge(rb_ready, 2)
                    for t in range(NT):
                        transpose(B1[:, COLS[t]], THb[:, v_rows_kv % 2, COLS[t]])
                    transpose(B3[0:EXT, 0:P], THb[:, v_rows_kv % 2, SEQ:TOK]).then_inc(vtr_done, 1)
            pe.wait_ge(pp_free[1], 8 + KVP // 2 + 4)
            pe.wait_ge(vn_kept, 4 * HEADS + 3)
            for t in range(NT):
                transpose(B1[:, COLS[t]], THb[:, 1, COLS[t]])
            transpose(B3[0:EXT, 0:P], THb[:, 1, SEQ:TOK]).then_inc(vtr_done, 1)
            for g in range(KV):
                last = transpose(B2[:, g * HD:(g + 1) * HD], kdup[0:HD, g, SEQ - P:SEQ])
            last.then_inc(kw_done, 1)
            for g in range(KV):
                last = transpose(B0[0:SMP, g * HD:(g + 1) * HD], kdup[0:HD, g, SEQ:SEQ + SMP])
            last.then_inc(kw_done, 1)
            pe.wait_ge(kw_kept, 2)
            pe.wait_ge(vn_kept, 4 * HEADS + 4)

            def batch_scores(i, k):
                if k == 0:
                    pe.wait_ge(staged, i + 1)
                    for b in range(2):
                        pe.wait_ge(pp_free[b], 8 + SWA // 2 + 2 * i + 2)
                elif k < 5:
                    pe.wait_ge(comb_ok, 6 * i + k)
                alone(pe)
                for r in range(GRP):
                    a = HD * (r % 2)
                    q = qB[a:a + HD, r // 2, :]
                    key = kg[a:a + HD, :]
                    bank, c = (B0, B1)[r % 2], 2 * P * (r // 2)
                    if k < 4:
                        mm(bank[:, c:c + P], q[:, COLS[k]], key[:, COLS[k]], start=True, stop=True)
                        if k:
                            last = mm(bank[:, c + P:c + 2 * P], q[:, COLS[k]], key[:, COLS[k - 1]], start=True, stop=True)
                        else:
                            last = mm(bank[:, c + 2 * P - META:c + 2 * P], q[:, COLS[0]], key[:, SEQ + SMP:TOK],
                                      start=True, stop=True)
                    elif k == 4:
                        last = mm(bank[0:META, c:c + META], q[:, SEQ + SMP:TOK], key[:, SEQ + SMP:TOK],
                                  start=True, stop=True)
                if k == 5:
                    pe.wait_ge(kcat_ready, 2 * i + 2)
                    pe.wait_ge(qz_ready, 4 * i + 4)
                    for s in range(DB):
                        last = mm(B0[:, 0:P + DT], Qz[0:HD, s, :], kcat[0:HD, s, :], start=(s == 0), stop=(s == DB - 1))
                last.then_inc(sc_done, 1)

            def cache_keys(i):
                pe.wait_ge(kc_in[0], 16 * (i + 1))
                pe.wait_ge(comb_ok, 6 * i + 5)
                alone(pe)
                for s in range(DB):
                    last = transpose((B0, B1)[s // 4][0:HD, (s % 4) * P:(s % 4 + 1) * P], Kc[:, 0, s * HD:(s + 1) * HD])
                last.then_inc(kct_done, 1)

            def batch_pt(i, k):
                pe.wait_ge(p_ready, 6 * i + k + 1)
                alone(pe)
                if k < 4:
                    for r in range(GRP):
                        last = transpose(B2[:, r * P:(r + 1) * P], Pp[:, k % 2, r * P:(r + 1) * P])
                elif k == 4:
                    for r in range(GRP):
                        last = transpose(B2[0:META, r * META:(r + 1) * META], Pp[0:META, 0, r * META:(r + 1) * META])
                else:
                    pe.wait_ge(o_stat, 2 * i + 2)
                    alone(pe)
                    transpose(B2[:, 0:P], Pp[:, 1, 0:P])
                    last = transpose(B2[0:SMP, P:2 * P], Pn[:, 0:SMP])
                last.then_inc(pt_done, 1)

            def batch_pv(i, k):
                pe.wait_ge(pt_kept, 6 * i + k + 1)
                if k:
                    pe.wait_ge(b_gated, 9 * i + k)
                if k == 5:
                    pe.wait_ge(kc_in[1], 16 * (i + 1))
                alone(pe)
                if k < 4:
                    for r in range(GRP):
                        out = B3[:, r * HD:(r + 1) * HD]
                        mm(out, PTc[:, k % 2, r * P:(r + 1) * P], vg[:, k, :], start=True, stop=False)
                        if k:
                            last = mm(out, PTp[:, k % 2, r * P:(r + 1) * P], vg[:, k - 1, :], start=False, stop=True)
                        else:
                            last = mm(out, PTp[96:P, 0, r * P:(r + 1) * P], vmg[96:P, :], start=False, stop=True)
                elif k == 4:
                    for r in range(GRP):
                        last = mm(B3[0:META, r * HD:(r + 1) * HD], PTc[SMP:EXT, 0, r * META:(r + 1) * META],
                                  vxg[SMP:EXT, :], start=True, stop=True)
                else:
                    mm(B3[:, 0:HD], PnT[0:SMP, :], vxg[0:SMP, :], start=True, stop=False)
                    for s in range(DB):
                        last = mm(B3[:, 0:HD], Pz[:, s, :], Vc[:, 0, s * HD:(s + 1) * HD], start=False, stop=(s == DB - 1))
                last.then_inc(pv_done, 1)

            def batch_ot(i, k):
                pe.wait_ge(on_ready, 6 * i + k + 1)
                alone(pe)
                if k < 5:
                    n = P if k < 4 else META
                    for u in range(2):
                        last = transpose(B3[:, u * n:(u + 1) * n], on[0:n, k % 2, u * P:(u + 1) * P])
                else:
                    last = transpose(B3[0:HD, 0:P], on[:, 1, 0:HD])
                last.then_inc(ot_done, 1)

            def group_step(i, g):
                att_, proj = i is not None, g is not None

                def piece(j, a, b):
                    if proj:
                        fresh = 2 * NK if isinstance(g, int) and j == 0 else None
                        project(W_SWA // 4 + g, j, SWA // 2 + 2 * g, j, H, fresh, (a, b))

                for n in range(8):
                    a = NK // 2 * (n % 2)
                    piece(n // 2, a, a + NK // 4)
                    if att_:
                        if n >= 3:
                            batch_ot(i, n - 3)
                        if n < 6:
                            batch_scores(i, n)
                    if n < 7:
                        piece(n // 2, a + NK // 4, a + NK // 2)
                        if att_ and n >= 2:
                            batch_pv(i, n - 2)
                        if att_ and n >= 1:
                            batch_pt(i, n - 1)
                        if att_ and n == 4:
                            cache_keys(i)
                    else:
                        piece(3, NK - NK // 4, NK - NK // 8)
                        att_ and batch_pv(i, 5)
                        piece(3, NK - NK // 8, NK)
                        att_ and batch_ot(i, 5)

            group_step(None, 0)
            with pe.Fori(0, KV - 1) as i:
                group_step(i, i + 1)
            group_step(KV - 1, None)

            def y_rows(i, j):
                n4 = 4 * i + j
                pe.wait_ge(xg_ready, n4 + 1)
                a, b = ((B0, B2), (B1, B3))[j % 2]
                if j >= 2:
                    pe.wait_ge(y_kept, 2 * (n4 - 1))
                for t in range(NT):
                    transpose(a[:, COLS[t]], xg[:, j % 2, COLS[t]])
                transpose(b[0:EXT, 0:P], xg[:, j % 2, SEQ:TOK]).then_inc(yt_done, 1)

            pe.wait_ge(b_gated, 9 * KV)
            with pe.Fori(0, NK // 4) as i:
                for j in range(4):
                    project(W_OUT_B // 4 + i, j, OUT_B // 2 + 2 * i, j, O)
                    if j:
                        y_rows(i, j - 1)
                y_rows(i, 3)
                pe.wait_ge(y_kept, 8 * i + 8)
            pe.wait_ge(acc_done, 2 * NK)
            for t in range(NT + 1):
                n = WID[t]
                last = mm(B0[0:n, 2 * t:2 * t + 2], acc[:, COLS[t]], ones[:, 0:2], start=True, stop=True)
            last.then_inc(ms_done, 1)

        @block.scalar
        def _(act):
            A = nc.scalar.activation
            act.wait_ge(setup, 1)
            for t in range(NT + 1):
                n = WID[t]
                act.wait_ge(x_in[t], 16 if t < NT else 32)
                if t:
                    act.wait_ge(row_ss, t)
                A(junk[0:n, :], XR[0:n, t, :], ACT.Square, accum_out=ss_c[0:n, t:t + 1]).then_inc(row_ss, 1)
            act.wait_ge(rs_dve, 1)
            A(lg_c, ms_c, ACT.Ln).then_inc(rs_act, 1)
            act.wait_ge(rs_act, 1)
            A(rs_c, lg_c, ACT.Exp, scale=-0.5).then_inc(rs_act, 1)
            act.wait_ge(vecs_done, 1)
            A(SK[:], B3[:, 0:32], ACT.Copy, scale=-1.0).then_inc(vecs_kept, 1)
            A(SKR[:], B3[:, 32:40], ACT.Copy, scale=-1.0).then_inc(vecs_kept, 1)
            for n in range(NK):
                act.wait_ge(proj_done, n + 1)
                if n >= 2:
                    act.wait_ge(h_ready, n - 1)
                    act.wait_ge(x0_out[n % 2], 16 * (n // 2))
                nc.scalar.copy(xt[:, n % 2, 0:SEQ], PP[n % 2][:, 0, :])
                nc.scalar.copy(xt[:, n % 2, SEQ:TOK], PP[n % 2][:, 1, 0:EXT]).then_inc(pp_free[n % 2], 1)
            act.wait_ge(glr_done, 1)
            for b in range(2):
                act.wait_ge(x0_out[b], 8 * NK)
            nc.scalar.copy(glr[0:RANK, 0:HALF], B2[0:RANK, 0:HALF]).then_inc(g_act, 1)
            nc.scalar.copy(glr[0:RANK, HALF:TOK], B3[0:RANK, 0:HALF]).then_inc(glr_kept, 1)
            G0 = 1

            def gate(h, j, th, half, done, after=None):
                act.wait_ge(proj_done, NK + done)
                if after is not None:
                    act.wait_ge(*after)
                A(halves(th[:, j % 2, :]), PV(j), ACT.Tanh, scale=0.5).then_inc(th_ready, 1)

            def head_gate(h, j):
                if j >= 2:
                    gate(h, j, TH, 7 * h, USES * h + j + 1, (pp_free[j % 2], 8 + 7 * h + j // 2))
                elif isinstance(h, int):
                    gate(h, j, TH, 7 * h, USES * h + j + 1)
                else:
                    gate(h, j, TH, 7 * h, USES * h + j + 1, (vtr_done, 4 * h))

            def v_tile(h, j):
                act.wait_ge(proj_done, NK + USES * h + 5 + j + (j == 3))
                if j >= 2:
                    act.wait_ge(vtr_done, 4 * h + j - 1)
                else:
                    act.wait_ge(pp_free[j % 2], 8 + 7 * h + (j + 2) // 2 + 1)
                nc.scalar.copy(halves(TH[:, j % 2, :]), PV(j)).then_inc(pp_free[j % 2], 1)

            def decay_logit(h, kt):
                act.wait_ge(proj_done, NK + USES * h + 8 + 2 * kt)
                if kt == 0:
                    act.wait_ge(vn_kept, 4 * h + 1)
                bias = GV[:, ds(B_GK + 2 * h + kt, 1)]
                A(halves(Dd[0][:, kt, :]), PV(kt), ACT.Identity, bias=bias).then_inc(g_act, 1)
                A(halves(Dd[1][:, kt, :]), PV(kt), ACT.Abs, bias=bias).then_inc(pp_free[kt], 1)

            def decay_log(h):
                for kt in range(KT):
                    act.wait_ge(pp_free[kt], 8 + 7 * h + 5)
                    A(Dd[1][:, kt, :], Dd[1][:, kt, :], ACT.Exp, scale=-1.0).then_inc(g_act, 1)
                for kt in range(KT):
                    act.wait_ge(g_act, G0 + 6 * h + 3 + kt)
                    A(Dd[1][:, kt, :], Dd[1][:, kt, :], ACT.Ln, bias=1.0).then_inc(g_act, 1)

            def q_tile(h, j):
                act.wait_ge(proj_done, NK + USES * h + 13 + j)
                if j == 0:
                    act.wait_ge(pp_free[0], 8 + 7 * h + 6)
                A(halves(qT[:, j, :]), PV(j), ACT.Copy, scale=DK ** -0.5).then_inc(pp_free[j % 2], 1)

            def level_decay(i, l):
                act.wait_ge(d_ready, (NL - 1) * i + l + 1)
                h = LEVELS[l]
                w = SEQ if l < NL - NLX else TOK
                v = Dd[l % 2][:, :, 0:w].rearrange("p k (b c) -> p k b c", c=2 * h)
                A(v[:, :, :, h:2 * h], v[:, :, :, h:2 * h], ACT.Exp, scale=1.0 / GN).then_inc(e_ready, 1)
                A(v[:, :, :, 0:h], v[:, :, :, 0:h], ACT.Exp, scale=-1.0 / GN).then_inc(e_ready, 1)

            def end_decay(i):
                act.wait_ge(kde_ready, 3 * i + 3)
                A(kd, kd, ACT.Exp, scale=-1.0 / GN).then_inc(decay_exp, 1)
                act.wait_ge(scores_done, NL * i + 6)
                A(qe, bT, ACT.Exp, scale=1.0 / GN).then_inc(decay_exp, 1)
                A(el[:, :, 0:NT], bT[:, :, P - 1:SEQ:P], ACT.Exp, scale=1.0 / GN).then_inc(decay_exp, 1)
                A(el[:, :, NT:NT + DB], bT[:, :, SEQ + DT - 1:SEQ + SMP:DT], ACT.Exp, scale=1.0 / GN).then_inc(decay_exp, 1)

            def kd_keep(i):
                act.wait_ge(kdtr_done, 3 * i + 1)
                nc.scalar.copy(kdT[:, :, 0:P], bank4(B3)).then_inc(kdt_ready, 1)
                act.wait_ge(kdtr_done, 3 * i + 2)
                nc.scalar.copy(kdT[:, :, P:DK], bank4(B0)).then_inc(kdt_ready, 1)
                act.wait_ge(kdtr_done, 3 * i + 3)
                nc.scalar.copy(kdX[0:EXT, :], B1[0:EXT, 0:DK]).then_inc(kdt_ready, 1)

            def o_keep(i, t):
                act.wait_ge(o_done, 5 * i + t + 1)
                if t >= 2:
                    act.wait_ge(o_gated, 5 * i + t - 1)
                n = VT * WID[t]
                nc.scalar.copy(o_sb[:, t % 2, 0:n], B0[:, 0:n]).then_inc(o_kept, 1)

            def head_norm(i, t):
                act.wait_ge(ss_done, 5 * i + t + 1)
                w = WID[t]
                A(rl[:, 0:w], B1[:, 0:w], ACT.Ln, bias=eps_c, scale=1.0 / DV).then_inc(r_act, 1)
                act.wait_ge(r_act, 10 * i + 2 * t + 1)
                A(rr[:, 0:w], rl[:, 0:w], ACT.Exp, scale=-0.5).then_inc(r_act, 1)

            def head_step(i, h):
                rec, proj = i is not None, h is not None
                if rec:
                    for l in range(4):
                        level_decay(i, l)
                for n in range(8):
                    if rec:
                        if n < 3:
                            level_decay(i, n + 4)
                        elif n == 5:
                            end_decay(i)
                        elif n == 7:
                            kd_keep(i)
                    if proj and n % 2:
                        head_gate(h, n // 2)
                for t in range(NT):
                    if rec:
                        o_keep(i, t)
                        if t:
                            head_norm(i, t - 1)
                    if proj and t % 2:
                        v_tile(h, t // 2)
                rec and head_norm(i, NT - 1)
                if proj:
                    v_tile(h, 2)
                    decay_logit(h, 0)
                    v_tile(h, 3)
                    decay_logit(h, 1)
                    decay_log(h)
                if rec:
                    o_keep(i, NT)
                    head_norm(i, NT)
                if proj:
                    q_tile(h, 0)
                    q_tile(h, 1)

            head_step(None, 0)
            with act.Fori(0, HEADS - 1) as i:
                head_step(i, i + 1)
            head_step(HEADS - 1, None)

            def squares(half, base):
                with act.Fori(0, NK // 4) as i:
                    for j in range(4):
                        act.wait_ge(pp_free[j % 2], 8 + half + 2 * i + j // 2 + 1)
                        if j >= 2:
                            act.wait_ge(acc_done, base + 4 * i + j - 1)
                        A(sqa[:, j % 2, :], tile(H, 4 * i + j), ACT.Square).then_inc(sq_a, 1)
                    act.wait_ge(acc_done, base + 4 * i + 4)

            squares(OUT_A2 // 2, 0)

            def root(n):
                for c, b in enumerate((B0, B1)):
                    s = slice(c * HALF, (c + 1) * HALF)
                    act.wait_ge(n_dve, n + c + 1)
                    A(RB[:, s], acc[:, s], ACT.Ln).then_inc(n_act, 1)
                    act.wait_ge(n_act, 2 * (n + c) + 1)
                    A(RB[:, s], RB[:, s], ACT.Exp, scale=-0.5).then_inc(n_act, 1)

            root(0)
            for j in range(4):
                act.wait_ge(proj_done, NK + KVP + j + 1)
                nc.scalar.copy(halves(kdup[0:HD, 2 * j, :]), PV(j)[0:HD]).then_inc(th_ready, 1)
                nc.scalar.copy(halves(kdup[HD:P, 2 * j, :]), PV(j)[0:HD]).then_inc(th_ready, 1)
            TK = 4 * HEADS + 8
            for j in range(4):
                act.wait_ge(proj_done, NK + KVP + 5 + j)
                if j >= 2:
                    act.wait_ge(vtr_done, 4 * HEADS + j - 1)
                nc.scalar.copy(halves(THb[:, j % 2, :]), PV(j)).then_inc(pp_free[j % 2], 1)
            act.wait_ge(kw_done, 1)
            nc.scalar.copy(kwin, B2[:]).then_inc(kw_kept, 1)
            act.wait_ge(kw_done, 2)
            nc.scalar.copy(kwx[0:SMP, :], B0[0:SMP, :]).then_inc(kw_kept, 1)

            def group_gate(g, j):
                act.wait_ge(proj_done, NK + SWA + 4 * g + j + 1)
                if isinstance(g, int):
                    if j == 0:
                        act.wait_ge(vtr_done, 4 * HEADS + 4)
                else:
                    act.wait_ge(pp_free[j % 2], 8 + SWA // 2 + 2 * g - 1)
                A(halves(THb[:, j % 2, :]), PV(j), ACT.Tanh, scale=0.5).then_inc(thb_ready, 1)

            def group_q(g, j):
                act.wait_ge(proj_done, NK + SWA + 4 * g + 3 + j)
                if not isinstance(g, int):
                    act.wait_ge(sc_done, 6 * g)
                nc.scalar.copy(halves(qB[:, j, :]), PV(j)).then_inc(pp_free[j % 2], 1)

            def batch_comb(i, k):
                if k == 4:
                    return
                act.wait_ge(sc_done, 6 * i + k + 1)
                if k == 0:
                    act.wait_ge(c_fill, i + 1)
                    nc.scalar.copy(by_head(Cc[:, 0, :])[:, :, :, P - META:P], old_scores(P - META)).then_inc(comb, 1)
                elif k < 4:
                    if k >= 2:
                        act.wait_ge(p_ready, 6 * i + k - 1)
                    nc.scalar.copy(by_head(Cc[:, k % 2, :]), old_scores()).then_inc(comb, 1)
                else:
                    act.wait_ge(p_ready, 6 * i + 4)
                    nc.scalar.copy(Cc[:, 1, 0:P], B0[:, 0:P]).then_inc(comb, 1)

            def batch_exp(i, k):
                b = k % 2
                act.wait_ge(sm_dve, 18 * i + 3 * k + 3)
                if k >= 2:
                    act.wait_ge(pt_done, 6 * i + k - 1)
                n, w, heads = ((P, P, GRP), (META, META, GRP), (P, P, 1))[max(k - 3, 0)]
                for r in range(heads):
                    A(Pp[0:n, b, r * w:(r + 1) * w], Cc[0:n, b, r * w:(r + 1) * w], ACT.Exp, scale=HD ** -0.5,
                      bias=sm[0:n, b, 4 + r:5 + r], accum_out=sm[0:n, b, 16 + r:17 + r]).then_inc(sm_act, 1)
                A(sm[0:n, b, 12:12 + heads], sm[0:n, b, 8:8 + heads], ACT.Exp).then_inc(p_ready, 1)

            def group_step(i, g):
                att_, proj = i is not None, g is not None

                def batch(k):
                    if att_:
                        if k == 5:
                            act.wait_ge(kct_done, i + 1)
                            for c, b in enumerate((B0, B1)):
                                nc.scalar.copy(kcat[0:HD, 4 * c:4 * c + 4, 0:P], bank4(b)[0:HD]).then_inc(kcat_ready, 1)
                        batch_comb(i, k)
                        batch_exp(i, k)

                for n in range(8):
                    if n < 6:
                        batch(n)
                    if n % 2 and proj:
                        group_gate(g, n // 2) if n < 4 else group_q(g, n // 2 - 2)

            group_step(None, 0)
            with act.Fori(0, KV - 1) as i:
                group_step(i, i + 1)
            group_step(KV - 1, None)

            with act.Fori(0, NK // 4) as i:
                for j in range(4):
                    act.wait_ge(pp_free[j % 2], 8 + OUT_B // 2 + 2 * i + j // 2 + 1)
                    if j >= 2:
                        act.wait_ge(acc_done, NK + 4 * i + j - 1)
                        act.wait_ge(yt_done, 4 * i + j - 1)
                    A(sqa[:, j % 2, :], x2[:, j % 2, :], ACT.Square).then_inc(sq_a, 1)
                    A(xg[:, j % 2, :], x2[:, j % 2, :], ACT.Copy, scale=GV[:, ds(G_F + 4 * i + j, 1)]).then_inc(xg_ready, 1)
                act.wait_ge(acc_done, NK + 4 * i + 4)
                act.wait_ge(yt_done, 4 * i + 4)
            act.wait_ge(n_dve, 3)
            A(lg_c, ms_c, ACT.Ln).then_inc(n_act, 1)
            act.wait_ge(n_act, 5)
            A(rs_c, lg_c, ACT.Exp, scale=-0.5).then_inc(n_act, 1)
            for t in (1, 3):
                act.wait_ge(n_dve, 7)
                A(YR[:, t, :], YR[:, t, :], ACT.Copy, scale=rs_c[:, t:t + 1]).then_inc(y_scaled, 1)

        @block.vector
        def _(dve):
            V = nc.vector
            TT, TS, STT = V.tensor_tensor, V.tensor_scalar, V.scalar_tensor_tensor

            V.memset(ones[:], 1.0)
            V.memset(eps_c, EPS)
            V.memset(small[:, 40:65], 1.0).then_inc(setup, 1)
            dve.wait_ge(setup, 1)

            def newton(y, x, tmp, tally):
                tally.link(dve, TT(tmp, y, y, ALU.mult))
                tally.link(dve, TT(tmp, tmp, x, ALU.mult))
                tally.link(dve, TS(tmp, tmp, -0.5, 1.5, ALU.mult, ALU.add))
                tally.link(dve, TT(y, y, tmp, ALU.mult))

            dve.wait_ge(vec_in, 128)
            V.tensor_copy(sx[0:KV, :].rearrange("p (s r t) -> p s r t", r=GRP, t=DT),
                          small[0:KV, 32:36].unsqueeze(1).unsqueeze(3).broadcast_to([KV, DB, GRP, DT])).then_inc(sink_rows, 1)

            dve.wait_ge(row_ss, NT + 1)
            c = Tally(rs_dve)
            c.link(dve, TS(ms_c, ss_c, 1.0 / DM, EPS, ALU.mult, ALU.add))
            dve.wait_ge(rs_act, 2)
            newton(rs_c, ms_c, nt_c, c)
            dve.wait_ge(cst_in, 16)
            for t in range(NT + 1):
                TS(diag[:, t, :], ident, rs_c[:, t:t + 1], None, ALU.mult).then_inc(diag_ready, 1)
            dve.wait_ge(vecs_done, 1)
            c.link(dve, V.tensor_copy(GV[:], B2[:, 0:76]))
            c.link(dve, TS(GV[:, G_O:G_O + VT], GV[:, G_O:G_O + VT], 0.5, None, ALU.mult))
            dve.wait_ge(bc_done, 1)
            V.tensor_copy(RB[:, 0:SEQ], B0[:])
            V.tensor_copy(RB[:, SEQ:TOK], B1[:, 0:EXT]).then_inc(rb_ready, 1)
            dve.wait_ge(rb_ready, 1)
            for n in range(NK):
                dve.wait_ge(pp_free[n % 2], n // 2 + 1)
                STT(out=H[:, n, :], in0=xt[:, n % 2, :], scalar=GV[:, G_A + n:G_A + n + 1], in1=RB[:], op0=ALU.mult,
                    op1=ALU.mult).then_inc(h_ready, 1)
            for b in range(2):
                dve.wait_ge(x0_out[b], 8 * NK)
            dve.wait_ge(h_ready, NK)
            V.memset(att[:, :, :].rearrange("p t n -> p (t n)"), 0.0)
            V.memset(attx, 0.0).then_inc(setup, 1)
            dve.wait_ge(setup, 2)

            def gate(O_tile, th, j, ready):
                dve.wait_ge(*ready)
                STT(out=halves(O_tile), in0=halves(th[:, j % 2, :]), scalar=1.0, in1=PV(j), op0=ALU.add,
                    op1=ALU.mult).then_inc(pp_free[j % 2], 1)

            def head_gate(h, j):
                gate(tile(O, VT * h + j), TH, j, (th_ready, 4 * h + j + 1))

            def v_keep(base, j, rows, ext, after=None):
                dve.wait_ge(vtr_done, base + j + 1)
                if j == 0 and after is not None:
                    dve.wait_ge(extbase, after + 1)
                    dve.wait_ge(vs_ready, after + 1)
                V.tensor_copy(rows[:, :, j * P:(j + 1) * P], bank4(B1))
                V.tensor_copy(ext[0:EXT, j * P:(j + 1) * P], B3[0:EXT, 0:P]).then_inc(vn_kept, 1)

            def decay_sum(h, kt):
                dve.wait_ge(g_act, 1 + 6 * h + 5 + kt)
                STT(out=Dd[0][:, kt, :], in0=Dd[0][:, kt, :], scalar=0.0, in1=Dd[1][:, kt, :], op0=ALU.min,
                    op1=ALU.subtract).then_inc(b_step, 1)
                dve.wait_ge(b_step, 4 * h + 2 * kt + 1)
                V.tensor_tensor_scan(bT[:, kt, :], C("keep"), Dd[0][:, kt, :], 0.0, ALU.mult, ALU.add).then_inc(b_step, 1)

            def k_tile(h, j):
                dve.wait_ge(proj_done, NK + USES * h + 11 + j)
                V.tensor_copy(halves(kT[:, j, :]), PV(j)).then_inc(pp_free[j % 2], 1)

            def blocks(buf, l):
                w = SEQ if l < NL - NLX else TOK
                return buf[:, :, 0:w].rearrange("p k (b c) -> p k b c", c=2 * LEVELS[l])

            def distance(i, l):
                if l == 0:
                    dve.wait_ge(b_step, 4 * i + 4)
                if l >= 2:
                    dve.wait_ge(t_ready, (NL - 1) * i + l - 1)
                b, h = blocks(bT, l), LEVELS[l]
                ref = b[:, :, :, h - 1:h].broadcast_to(list(b.shape))
                TT(blocks(Dd[l % 2], l), b, ref, ALU.subtract).then_inc(d_ready, 1)

            def level_qk(i, l):
                dve.wait_ge(e_ready, 2 * (NL - 1) * i + 2 * l + 2)
                if l == 0:
                    for b in range(2):
                        dve.wait_ge(pp_free[b], 8 + 7 * i + 7)
                if l >= 2:
                    dve.wait_ge(scores_done, NL * i + l - 1)
                h = LEVELS[l]
                T_, D_, q, k = (blocks(x, l) for x in (Tt[l % 2], Dd[l % 2], qT, kT))
                TT(T_[:, :, :, h:2 * h], q[:, :, :, h:2 * h], D_[:, :, :, h:2 * h], ALU.mult)
                TT(T_[:, :, :, 0:h], k[:, :, :, 0:h], D_[:, :, :, 0:h], ALU.mult).then_inc(t_ready, 1)

            def take_scores(i, l):
                dve.wait_ge(scores_done, NL * i + l + 1)
                if l:
                    dve.wait_ge(scores_kept, NL * i + l)
                else:
                    dve.wait_ge(t_ready, (NL - 1) * i + 1)
                bank = (B0, B1)[l % 2]
                alone(dve)
                if l == NL - 1:
                    V.copy_predicated(att, over(C("level0").bitcast(I32), NT), bank4(bank)).then_inc(scores_kept, 1)
                else:
                    mask = right(C(f"level{LEVELS[l]}").bitcast(I32), l)
                    dst = att.rearrange("p t (b c) -> p t b c", c=2 * LEVELS[l])[:, :, :, LEVELS[l]:2 * LEVELS[l]]
                    src = bank4(bank, P // 2).rearrange("p t (b c) -> p t b c", c=LEVELS[l])
                    V.copy_predicated(dst, over(mask, NT), src).then_inc(scores_kept, 1)

            def take_ext(i):
                for x in range(NLX):
                    if x:
                        dve.wait_ge(attx_ready, NLX * i + x)
                    alone(dve)
                    if x == NLX - 1:
                        V.copy_predicated(attx[0:EXT, :], C("ext0", 0, EXT).bitcast(I32),
                                          B2[0:EXT, x * EXT:(x + 1) * EXT]).then_inc(attx_ready, 1)
                    else:
                        l = NL - NLX + x
                        src = B2[0:EXT, x * EXT:x * EXT + EXT // 2].rearrange("p (b c) -> p b c", c=LEVELS[l])
                        V.copy_predicated(right(attx[0:EXT, :], l), right(C(f"ext{LEVELS[l]}", 0, EXT).bitcast(I32), l),
                                          src).then_inc(attx_ready, 1)

            def end_distance(i):
                dve.wait_ge(t_ready, (NL - 1) * i + 6)
                for a, b, n in ((0, SEQ, P), (SEQ, SEQ + SMP, DT), (SEQ + SMP, TOK, META)):
                    v = bT[:, :, a:b].rearrange("p k (b c) -> p k b c", c=n)
                    last = v[:, :, :, n - 1:n].broadcast_to(list(v.shape))
                    TT(kd[:, :, a:b].rearrange("p k (b c) -> p k b c", c=n), v, last, ALU.subtract).then_inc(kde_ready, 1)

            def end_qk(i):
                dve.wait_ge(decay_exp, 4 * i + 1)
                TT(kd, kd, kT, ALU.mult).then_inc(kd_ready, 1)
                dve.wait_ge(decay_exp, 4 * i + 2)
                TT(qe, qe, qT, ALU.mult).then_inc(qe_ready, 1)

            def meta_state(i):
                for kt, bank in enumerate((B2, B3)):
                    dve.wait_ge(u_done, 10 * i + kt + 1)
                    V.tensor_copy(S[:, kt, :], bank[:]).then_inc(s_ready, 1)

            def state(i, t):
                if t == 0:
                    dve.wait_ge(decay_exp, 4 * i + 4)
                for kt, bank in enumerate((B2, B3)):
                    dve.wait_ge(u_done, 10 * i + 2 * (t + 1) + kt + 1)
                    dve.wait_ge(s_ready, 10 * i + 2 * t + kt + 1)
                    STT(out=S[:, kt, :], in0=S[:, kt, :], scalar=el[:, kt, t:t + 1], in1=bank[:], op0=ALU.mult,
                        op1=ALU.add).then_inc(s_ready, 1)

            def head_norm(i, t):
                w = WID[t]
                c = Tally(r_dve, 30 * i + 6 * t)
                dve.wait_ge(r_act, 10 * i + 2 * t + 2)
                if t == 0:
                    for b in range(2):
                        dve.wait_ge(pp_free[b], 8 + 7 * i + 2)
                c.link(dve, TS(rv[:, 0:w], B1[:, 0:w], 1.0 / DV, EPS, ALU.mult, ALU.add))
                newton(rr[:, 0:w], rv[:, 0:w], ra[:, 0:w], c)
                x = sq[:, 0:VT * w].rearrange("p (v n) -> p v n", v=VT)
                c.link(dve, TT(x, o_sb[:, t % 2, 0:VT * w].rearrange("p (v n) -> p v n", v=VT), over(rr[:, 0:w], VT),
                               ALU.mult))
                for v in range(VT):
                    o = tile(O, VT * i + v)[:, COLS[t]]
                    last = STT(out=o, in0=x[:, v, :], scalar=GV[:, G_O + v:G_O + v + 1], in1=o, op0=ALU.mult, op1=ALU.mult)
                last.then_inc(o_gated, 1)

            def seq_state(i, s, kt):
                dve.wait_ge(smp_u, 2 * DB * i + 2 * s + kt + 1)
                x = S0[:, s % SR, kt, :]
                STT(out=x, in0=x, scalar=el[:, kt, NT + s:NT + s + 1], in1=B2[:], op0=ALU.mult,
                    op1=ALU.add).then_inc(smp_new, 1)

            def out_early(n):
                dve.wait_ge(proj_done, NK + OUT_A + n + 1)
                dve.wait_ge(h_in[n // 4], 16)
                TT(halves(H[:, n, :]), PV(n), halves(H[:, n, :]), ALU.add).then_inc(pp_free[n % 2], 1)

            def head_step(i, h):
                rec, proj = i is not None, h is not None

                def early(a, b):
                    if not proj:
                        for n in range(a // K_A, b // K_A):
                            out_early(n)

                if rec:
                    distance(i, 0)
                    distance(i, 1)
                    level_qk(i, 0)
                    distance(i, 2)
                    level_qk(i, 1)
                    distance(i, 3)
                for n in range(8):
                    if rec:
                        if n < 7:
                            take_scores(i, n)
                        if n < 5:
                            level_qk(i, n + 2)
                        if n < 3:
                            distance(i, n + 4)
                        elif n == 3:
                            end_distance(i)
                        elif n == 5:
                            end_qk(i)
                        elif n == 6:
                            take_scores(i, 7)
                            take_ext(i)
                        elif n == 7:
                            meta_state(i)
                    if proj and n % 2:
                        head_gate(h, n // 2)
                    early(8 * n, 8 * n + 8)
                if rec:
                    for t in range(NT):
                        state(i, t)
                        if t:
                            head_norm(i, t - 1)
                        early(64 + 8 * t, 72 + 8 * t)
                    head_norm(i, NT - 1)
                for q in range(24):
                    if rec:
                        if 1 <= q <= 2 * DB:
                            seq_state(i, (q - 1) // 2, (q - 1) % 2)
                        if q == 18:
                            head_norm(i, NT)
                    if proj:
                        if q in (3, 5, 7, 9):
                            v_keep(4 * h, (q - 3) // 2, Vn, Vx, i)
                        if q in (11, 15):
                            k_tile(h, (q - 11) // 4)
                        if q in (13, 14):
                            decay_sum(h, q - 13)
                    early(96 + 4 * q, 100 + 4 * q)
                if rec:
                    dve.wait_ge(state_out, 16 * (i + 1))

            head_step(None, 0)
            with dve.Fori(0, HEADS - 1) as i:
                head_step(i, i + 1)
            head_step(HEADS - 1, None)

            with dve.Fori(0, NK // 4) as i:
                for j in range(4):
                    dve.wait_ge(proj_done, NK + OUT_A2 + 4 * i + j + 1)
                    h_ = halves(tile(H, 4 * i + j))
                    TT(h_, PV(j), h_, ALU.add).then_inc(pp_free[j % 2], 1)
            dve.wait_ge(ms_done, 1)
            cn = Tally(n_dve)
            for c_, b in enumerate((B0, B1)):
                cn.link(dve, TS(acc[:, c_ * HALF:(c_ + 1) * HALF], b[:, 0:HALF], 1.0 / DM, EPS, ALU.mult, ALU.add))
            cr = Tally(rs_dve, c.value)
            dve.wait_ge(n_act, 4)
            newton(RB[:], acc[:], x2[:, 0, :], cr)
            V.tensor_copy(small[:, 90:91], eps_c).then_inc(rb_ready, 1)

            def normed(dst, g, n):
                STT(out=dst[:, n, :], in0=H[:, n, :], scalar=GV[:, g + n:g + n + 1], in1=RB[:], op0=ALU.mult,
                    op1=ALU.mult).then_inc(h_ready, 1)

            for b in range(2):
                dve.wait_ge(pp_free[b], 8 + KVP // 2)
            for n in range(NK):
                normed(O, G_KV, n)
            for q in range(4):
                dve.wait_ge(x1_out[q], 4 * 16)
            dve.wait_ge(h_ready, 2 * NK)
            for n in range(NK):
                normed(H, G_B, n)
            for j in range(4):
                dve.wait_ge(th_ready, 4 * HEADS + 2 * j + 2)
                V.tensor_copy(halves(kdup[0:HD, 2 * j + 1, :]), PV(j)[HD:P])
                V.tensor_copy(halves(kdup[HD:P, 2 * j + 1, :]), PV(j)[HD:P]).then_inc(pp_free[j % 2], 1)
            dve.wait_ge(h_ready, 3 * NK)
            V.memset(Wm[96:P, :], 0.0).then_inc(setup, 1)
            V.memset(Qz[0:HD].rearrange("p s n -> p (s n)"), 0.0)
            V.memset(Pz.rearrange("p s n -> p (s n)"), 0.0).then_inc(setup, 1)
            for j in range(4):
                v_keep(4 * HEADS, j, Wn, Wx)
            dve.wait_ge(setup, 4)

            def z_blocks(buf):
                full = buf.rearrange("p s n -> p (s n)")
                return full

            def spread_q(i):
                for r in range(GRP):
                    a = HD * (r % 2)
                    src = qB[a:a + HD, r // 2, SEQ:SEQ + SMP].rearrange("p (s t) -> p s t", t=DT)
                    V.tensor_copy(diag_view(Qz, DT * r, DT)[0:HD], src).then_inc(qz_ready, 1)

            def diag_view(buf, off, n):
                flat = buf.rearrange("p s n -> p (s n)")
                w = GRP * DT
                a = flat[:, 0:(P + w) * (DB - 1) + w]
                pad = flat[:, 0:DB * P]
                v = bass.AP(tensor=a.tensor, offset=a.offset + off, ap=[list(a.ap[0]), [P + w, DB], [1, n]])
                return v

            def batch_max(i, k):
                b = k % 2
                if k < 4:
                    dve.wait_ge(comb, 5 * i + k + 1)
                    x = bank4(Cc[:, b, :])
                    alone(dve)
                    V.copy_predicated(by_head(Cc[:, b, :]), over(over(C("causal").bitcast(I32), 2), 2),
                                      own_scores()).then_inc(comb_ok, 1)
                    n, g = P, GRP
                elif k == 4:
                    dve.wait_ge(sc_done, 6 * i + 5)
                    dve.wait_ge(p_ready, 6 * i + 3)
                    n, g = META, GRP
                    x = bank4(Cc[0:META, 0, :], META)
                    TT(x.rearrange("p (h b) n -> p h b n", h=2), own_scores(META, META),
                       over(over(C("meta_neg", 0, META), 2), 2), ALU.add).then_inc(comb_ok, 1)
                else:
                    dve.wait_ge(comb, 5 * i + 5)
                    n, g = P, 1
                    alone(dve)
                    V.copy_predicated(Cc[:, 1, 0:DT], C("new_ok").bitcast(I32), B0[:, P:P + DT]).then_inc(comb_ok, 1)
                    x = Cc[:, 1, 0:P].unsqueeze(1)
                dve.wait_ge(comb_ok, 6 * i + k + 1)
                nsink = SK[0:n, ds(GRP * i, GRP)] if k < 5 else SKR[:, ds(i, 1)]
                t = Tally(sm_dve, 18 * i + 3 * k)
                m, nm, d = (sm[0:n, b, 4 * q:4 * q + g] for q in range(3))
                t.link(dve, V.tensor_reduce(m, x, AX.X, ALU.max, negate=True))
                t.link(dve, STT(out=nm, in0=m, scalar=HD ** -0.5, in1=nsink, op0=ALU.mult, op1=ALU.min))
                t.link(dve, TT(d, nm, nsink, ALU.subtract))

            def batch_keep(i, k):
                b = k % 2
                dve.wait_ge(p_ready, 6 * i + k + 1)
                n, g = ((P, GRP), (META, GRP), (P, 1))[max(k - 3, 0)]
                es, rs, den, rinv = (sm[0:n, b, 4 * q:4 * q + g] for q in (3, 4, 5, 6))
                if k >= 2:
                    dve.wait_ge(on_ready, 6 * i + k - 1)
                t = Tally(den_ready, 12 * i + 2 * k)
                t.link(dve, TT(den, es, rs, ALU.add))
                t.link(dve, V.reciprocal(rinv, den))
                if k == 5:
                    TT(Pn.rearrange("p (s u) -> p s u", u=DT), over(Pp[:, 1, 0:DT], DB),
                       C("new_block").rearrange("p (s u) -> p s u", u=DT), ALU.mult).then_inc(o_stat, 1)
                    dve.wait_ge(o_stat, 2 * i + 1)
                    TT(Pp[:, 1, 0:DT], Pp[:, 1, 0:DT], C("old_ok"), ALU.mult).then_inc(o_stat, 1)
                dve.wait_ge(pt_done, 6 * i + k + 1)
                if k >= 2:
                    dve.wait_ge(pv_done, 6 * i + k - 1)
                if k < 4:
                    TT(bank4(PTc[:, b, :]), bank4(B2), over(C("causalT"), GRP), ALU.mult)
                    last = TT(bank4(PTp[:, b, :]), bank4(B2), over(C("prevT"), GRP), ALU.mult)
                elif k == 4:
                    last = V.tensor_copy(PTc[SMP:EXT, 0, 0:GRP * META], B2[0:META, 0:GRP * META])
                else:
                    V.tensor_copy(diag_view(Pz, 0, GRP * DT), B2[:, 0:P].rearrange("p (s n) -> p s n", s=DB))
                    last = V.tensor_copy(PnT[0:SMP, :], B2[0:SMP, P:2 * P])
                last.then_inc(pt_kept, 1)

            def batch_scale(i, k):
                b = k % 2
                dve.wait_ge(pv_done, 6 * i + k + 1)
                if k == 5:
                    last = TS(on[:, 1, 0:HD], B3[:, 0:HD], sm[:, 1, 24:25], None, ALU.mult)
                else:
                    n = P if k < 4 else META
                    r = sm[0:n, b, 24:28].unsqueeze(2).broadcast_to([n, GRP, HD])
                    last = TT(bank4(on[0:n, b, :], HD), bank4(B3[0:n], HD), r, ALU.mult)
                last.then_inc(on_ready, 1)

            def batch_gate(i, k):
                dve.wait_ge(ot_done, 6 * i + k + 1)
                if k < 5:
                    n = P if k < 4 else META
                    cols = COLS[k] if k < 4 else slice(SEQ + SMP, TOK)
                    o = O[:, ds(2 * i, 2), cols]
                    STT(out=o, in0=B3[:, 0:2 * n].rearrange("p (u n) -> p u n", u=2), scalar=0.5, in1=o, op0=ALU.mult,
                        op1=ALU.mult).then_inc(b_gated, 1)
                else:
                    x = B3[0:HD, 0:P].rearrange("p (s r t) -> p s r t", r=GRP, t=DT)
                    for r in range(GRP):
                        a = HD * (r % 2)
                        o = tile(O, 2 * i + r // 2)[a:a + HD, SEQ:SEQ + SMP].rearrange("p (s t) -> p s t", t=DT)
                        STT(out=o, in0=x[:, :, r, :], scalar=0.5, in1=o, op0=ALU.mult, op1=ALU.mult).then_inc(b_gated, 1)

            def group_step(i, g):
                att_, proj = i is not None, g is not None

                def unit(j):
                    if proj:
                        gate(tile(O, 2 * g + j), THb, j, (thb_ready, 2 * g + j + 1))

                def run(*steps):
                    if att_:
                        for f, k in steps:
                            f(i, k)

                if att_:
                    for b in range(2):
                        dve.wait_ge(pp_free[b], 8 + SWA // 2 + 2 * i + 2)
                    spread_q(i)
                for n in range(9):
                    if n >= 3:
                        run((batch_gate, n - 3))
                    if n < 6:
                        run((batch_max, n))
                    if n in (1, 3):
                        unit(n // 2)
                    if 2 <= n < 8:
                        run((batch_scale, n - 2))
                    if 1 <= n < 7:
                        run((batch_keep, n - 1))

            group_step(None, 0)
            with dve.Fori(0, KV - 1) as i:
                group_step(i, i + 1)
            group_step(KV - 1, None)

            with dve.Fori(0, NK // 4) as i:
                def keep_rows(j):
                    n4 = 4 * i + j
                    dve.wait_ge(yt_done, n4 + 1)
                    a, b = ((B0, B2), (B1, B3))[j % 2]
                    V.tensor_copy(YR[:, 0:NT, ds(n4 * P, P)], bank4(a)).then_inc(y_kept, 1)
                    V.tensor_copy(YR[0:EXT, NT, ds(n4 * P, P)], b[0:EXT, 0:P]).then_inc(y_kept, 1)

                for j in range(4):
                    dve.wait_ge(proj_done, NK + OUT_B + 4 * i + j + 1)
                    dve.wait_ge(xs_in[j], 16 * (i + 1))
                    if j >= 2:
                        dve.wait_ge(xg_ready, 4 * i + j - 1)
                    TT(halves(x2[:, j % 2, :]), PV(j), halves(xs[:, j, :]), ALU.add).then_inc(pp_free[j % 2], 1)
                    if j:
                        keep_rows(j - 1)
                keep_rows(3)
                dve.wait_ge(xg_ready, 4 * i + 4)
            dve.wait_ge(ms_done, 2)
            TS(ms_c[:, 0:NT], B0[:, 0:2 * NT:2], 1.0 / DM, EPS, ALU.mult, ALU.add)
            cn.link(dve, TS(ms_c[0:EXT, NT:NT + 1], B0[0:EXT, 2 * NT:2 * NT + 1], 1.0 / DM, EPS, ALU.mult, ALU.add))
            dve.wait_ge(n_act, 6)
            newton(rs_c, ms_c, nt_c, cn)
            dve.wait_ge(y_kept, 2 * NK)
            for t in (0, 2, 4):
                n = WID[t]
                TS(YR[0:n, t, :], YR[0:n, t, :], rs_c[0:n, t:t + 1], None, ALU.mult).then_inc(y_scaled_v, 1)

        @block.gpsimd
        def _(pool):
            G = nc.gpsimd
            G.memset(acc[:], 0.0).then_inc(acc_zero, 1)
            gk = I["w_gk2_a"][0]
            G.dma_start(gk2[0:RANK, :], gk[:, 0:DK]).then_inc(gk2_in, 16)

            def load_state(h, s):
                src = I["state_gla"][0, s].rearrange("h (k p) v -> h p k v", p=P)
                src = src[h] if isinstance(h, int) else src[ds(h, 1)].rearrange("h p k v -> (h p) k v")
                alone(pool)
                G.dma_start(S0[:, s % SR, :, :], src).then_inc(s0_in[s % SR], 16)

            def store_state(h, s):
                dst = OUTS[3][0, s].rearrange("h (k p) v -> h p k v", p=P)
                dst = dst[h] if isinstance(h, int) else dst[ds(h, 1)].rearrange("h p k v -> (h p) k v")
                alone(pool)
                G.dma_start(dst, S0[:, s % SR, :, :]).then_inc(s0_out[s % SR], 16)

            for s in range(SR):
                load_state(0, s)
            for n in range(NK):
                pool.wait_ge(pp_free[n % 2], n // 2 + 1)
                alone(pool)
                G.dma_start(x0T[n], xt[:, n % 2, :]).then_inc(x0_out[n % 2], 16)
            for b in range(2):
                pool.wait_ge(x0_out[b], 8 * NK)

            def square(i, t):
                pool.wait_ge(o_kept, 5 * i + t + 1)
                if t:
                    pool.wait_ge(o_gated, 5 * i + t)
                n = VT * WID[t]
                x = o_sb[:, t % 2, 0:n]
                G.tensor_tensor(sq[:, 0:n], x, x, ALU.mult).then_inc(sq_ready, 1)

            def own_keys(i, s):
                if s >= 2:
                    pool.wait_ge(smp_u, 2 * DB * i + 2 * s - 2)
                alone(pool)
                G.tensor_scalar(kdm[0:SMP, s % 2, :], kdX[0:SMP, :], C("seq_of", 0, SMP)[:, s:s + 1], None,
                                ALU.mult).then_inc(kdm_ready, 1)

            def head_step(i, more):
                if more:
                    pool.wait_ge(proj_done, NK + USES * i + 10)
                    alone(pool)
                    G.dma_start(gk2[0:RANK, :], gk[:, ds(DK * (i + 1), DK)]).then_inc(gk2_in, 16)
                pool.wait_ge(vn_kept, 4 * i + 4)
                alone(pool)
                G.tensor_copy(Vs[0:SMP, :], Vx[0:SMP, :]).then_inc(vs_ready, 1)
                pool.wait_ge(kdt_ready, 3 * i + 3)
                own_keys(i, 0)
                own_keys(i, 1)
                for t in range(NT):
                    square(i, t)
                pool.wait_ge(s_ready, 10 * i + 10)
                dst = OUTS[2][0, 0].rearrange("h (k p) v -> h p k v", p=P)
                dst = dst[i] if isinstance(i, int) else dst[ds(i, 1)].rearrange("h p k v -> (h p) k v")
                alone(pool)
                G.dma_start(dst, S[:, :, :]).then_inc(state_out, 16)
                for s in range(DB):
                    if s >= 2:
                        own_keys(i, s)
                    pool.wait_ge(smp_new, 2 * DB * i + 2 * s + 2)
                    store_state(i, s)
                    if 1 <= s <= SR:
                        pool.wait_ge(s0_out[s - 1], 16 * (2 * i + 1))
                        load_state(i, s - 1 + SR)
                square(i, NT)
                for s in range(SR):
                    pool.wait_ge(s0_out[s], 16 * (2 * i + 2))
                    if more:
                        load_state(i + 1, s)

            with pool.Fori(0, HEADS - 1) as i:
                head_step(i, True)
            pool.wait_ge(proj_done, NK + OUT_A)
            for m in range(4):
                G.dma_start(H[:, 4 * m:4 * m + 4, :], x0T[4 * m:4 * m + 4].rearrange("n p t -> p n t")).then_inc(h_in[m], 16)
            head_step(HEADS - 1, False)

            pool.wait_ge(acc_zero, 1)
            pool.wait_ge(o_gated, 5 * HEADS)
            pool.wait_ge(state_out, 16 * HEADS)

            def residual(base, src, dst, half):
                if src is not None:
                    for j in range(4):
                        alone(pool)
                        G.dma_start(xs[:, j, :], src[j]).then_inc(xs_in[j], 16)

                def body(i, more):
                    for j in range(4):
                        n = 4 * i + j
                        pool.wait_ge(pp_free[j % 2], 8 + half + 2 * i + j // 2 + 1)
                        if more and src is not None:
                            s_ = src[ds(n + 4, 1)].rearrange("a p n -> (a p) n")
                            alone(pool)
                            G.dma_start(xs[:, j, :], s_).then_inc(xs_in[j], 16)
                        if dst is not None:
                            d_ = dst[ds(n, 1)].rearrange("a p n -> (a p) n") if more else dst[n]
                            alone(pool)
                            G.dma_start(d_, tile(H, n)).then_inc(x1_out[j], 16)
                        pool.wait_ge(sq_a, base + n + 1)
                        if j or not more or base:
                            pool.wait_ge(acc_done, base + n) if not (isinstance(n, int) and base + n == 0) else None
                        else:
                            pool.wait_ge(acc_zero, 1)
                        G.tensor_tensor(acc[:], acc[:], sqa[:, j % 2, :], ALU.add).then_inc(acc_done, 1)
                    pool.wait_ge(acc_done, base + 4 * i + 4)

                with pool.Fori(0, NK // 4 - 1) as i:
                    body(i, True)
                body(NK // 4 - 1, False)

            residual(0, None, x1T, OUT_A2 // 2)
            pool.wait_ge(rb_ready, 2)
            G.memset(acc[:], 0.0).then_inc(acc_zero, 1)
            pool.wait_ge(acc_zero, 2)

            w = OUTS[6], OUTS[7]
            for c_, name in enumerate(("cache_k_win", "cache_v_win")):
                alone(pool)
                G.dma_start(w[c_][:, 0:P - DT], I[name][:, DT:P]).then_inc(win_out, 16)
            pool.wait_ge(vn_kept, 4 * HEADS + 4)
            pool.wait_ge(setup, 3)
            G.dma_start(Wm[P - META:P, :], Wx[SMP:EXT, :]).then_inc(vm_in, 16)
            G.dma_start(OUTS[5][0].rearrange("w k d -> w (k d)"), Wn[:, NT - 1, :]).then_inc(win_out, 16)
            for s in range(DB):
                alone(pool)
                G.dma_start(w[1][s, P - DT:P].rearrange("t k d -> t (k d)"),
                            Wx[DT * s:DT * (s + 1), :]).then_inc(win_out, 16)
            pool.wait_ge(kw_kept, 2)
            G.dma_start(OUTS[4][0].rearrange("w k d -> w (k d)"), kwin).then_inc(win_out, 16)
            for s in range(DB):
                alone(pool)
                G.dma_start(w[0][s, P - DT:P].rearrange("t k d -> t (k d)"),
                            kwx[DT * s:DT * (s + 1), :]).then_inc(win_out, 16)
            pool.wait_ge(vm_in, 16)

            def load_cache(g):
                for c_, (name, buf) in enumerate((("cache_k_win", Kc), ("cache_v_win", Vc))):
                    src = I[name].rearrange("b w k d -> w b k d")
                    if isinstance(g, int):
                        src = src[:, :, g, :]
                    else:
                        src = src[:, :, ds(g, 1), :].rearrange("w b k d -> w b (k d)")
                    alone(pool)
                    G.dma_start(buf[:, 0, :].rearrange("p (b d) -> p b d", b=DB), src).then_inc(kc_in[c_], 16)

            def stage(i):
                load_cache(i)
                alone(pool)
                G.tensor_copy(kg, tile(kdup, i)).then_inc(stage_step, 1)
                alone(pool)
                G.memset(bank4(Cc[:, 0, :])[:, :, 0:P - META], NEG).then_inc(c_fill, 1)
                alone(pool)
                G.tensor_copy(vg, Wn[:, :, ds(HD * i, HD)]).then_inc(stage_step, 1)
                pool.wait_ge(stage_step, 3 * i + 2)
                alone(pool)
                G.tensor_copy(vxg[0:EXT, :], Wx[0:EXT, ds(HD * i, HD)])
                alone(pool)
                G.tensor_copy(vmg[96:P, :], Wm[96:P, ds(HD * i, HD)]).then_inc(stage_step, 1)
                pool.wait_ge(stage_step, 3 * i + 3)
                src = tile(kdup, i)[0:HD, SEQ:SEQ + SMP].rearrange("p (s t) -> p s t", t=DT)
                alone(pool)
                G.tensor_copy(kcat[0:HD, :, P:P + DT], src).then_inc(staged, 1)

            stage(0)
            with pool.Fori(1, KV) as i:
                pool.wait_ge(pv_done, 6 * i)
                stage(i)
            pool.wait_ge(pv_done, 6 * KV)
            pool.wait_ge(b_gated, 9 * KV)
            pool.wait_ge(win_out, 16 * (2 + 1 + DB + 1 + DB))
            residual(NK, x1T, None, OUT_B // 2)
            for t, s_ in ((0, (y_scaled_v, 1)), (1, (y_scaled, 1)), (2, (y_scaled_v, 2)), (3, (y_scaled, 2))):
                pool.wait_ge(*s_)
                alone(pool)
                G.dma_start(OUTS[0][0, t * P:(t + 1) * P, :], YR[:, t, :]).then_inc(y_out, 16)
            pool.wait_ge(y_scaled_v, 3)
            G.dma_start(OUTS[1].rearrange("b t d -> (b t) d"), YR[0:SMP, NT, :]).then_inc(y_out, 16)
            pool.wait_ge(y_out, 80)


_INS = ['x_prompt', 'x_sample', 'state_gla', 'cache_k_win', 'cache_v_win', 'meta_tokens', 'norm_a', 'w_in_a', 'w_gk2_a',
        'b_gk2_a', 'onorm_a', 'w_out_a', 'norm_kv', 'w_kv', 'norm_b', 'w_in_b', 'sinks_b', 'w_out_b', 'norm_f']
_OUTS = [(1, SEQ, DM), (DB, DT, DM), (1, 1, HEADS, DK, DV), (1, DB, HEADS, DK, DV), (1, P, KV, HD), (1, P, KV, HD),
         (DB, P, KV, HD), (DB, P, KV, HD)]


def kernel(**inputs):
    import concourse.bacc as bacc
    from concourse.bass_utils import run_bass_kernel_spmd

    nc = bacc.Bacc("TRN2", target_bir_lowering=False, num_devices=1)
    arrays, ins = {}, {}
    for name in _INS:
        a = np.ascontiguousarray(inputs[name])
        arrays[f"in_{name}"] = a
        ins[name] = nc.dram_tensor(f"in_{name}", a.shape, mybir.dt.from_np(a.dtype), kind="ExternalInput").ap()
    table, _ = consts_array()
    arrays["in_consts"] = table
    ins["consts"] = nc.dram_tensor("in_consts", table.shape, FP32, kind="ExternalInput").ap()
    outs = [nc.dram_tensor(f"out_{n}", shape, FP32, kind="ExternalOutput").ap() for n, shape in enumerate(_OUTS)]
    yoco_kernel(nc, ins, outs)
    r = run_bass_kernel_spmd(nc, [arrays], core_ids=[0])
    return tuple(r.results[0][f"out_{n}"] for n in range(len(_OUTS)))
```

```python
import numpy as np
import concourse.bass as bass
from concourse import mybir
from contextlib import ExitStack

FP32 = mybir.dt.float32
FP16 = mybir.dt.float16
I32 = mybir.dt.int32
ALU = mybir.AluOpType
ACT = mybir.ActivationFunctionType
AX = mybir.AxisListType

P = 128
DM = 2048
NK = DM // P
SEQ, META, DB, DT = 512, 16, 8, 4
SMP = DB * DT
EXT = SMP + META
TOK = SEQ + EXT
HALF = TOK // 2
NT = SEQ // P
HEADS, DK, DV = 4, 256, 512
KT, VT = DK // P, DV // P
RANK = 16
GN = 16.0
KV = 8
NORM_STEPS = 16
AR_WORDS = 22320
GRP = 4
HD = 64
EPS = 1e-6
NEG = -1e30
LEVELS = [64, 32, 16, 8, 4, 2, 1]
NL = len(LEVELS) + 1
NLX = 5
WR = 4
SR = 4
USES = 14
OUT_A = USES * HEADS
K_A = NK - VT
OUT_A2 = OUT_A + NK
KVP = OUT_A2 + NK
SWA = KVP + 8
OUT_B = SWA + 4 * KV
U_HEAD = 12
U_KV = U_HEAD * HEADS
U_SWA = U_KV + 8
U_OUT = U_SWA + 4 * KV
MAGIC = 0x5F3759DF
HI_EXP = 0x7F800000
X_MAX = 2.0 ** 10
W_MAX = 2.0 ** 15


def first(x):
    return isinstance(x, int) and x == 0


def head_unit_at(h, j):
    k = j - 2
    return U_HEAD * h + j, U_HEAD // 2 * h + j // 2, USES * h + k + 1 + (0 if k < 7 else 1 if k == 7 else 2)


def kv_unit_at(j):
    return U_KV + j, U_KV // 2 + j // 2, KVP + max(j - 1, 0)


def out_unit_at(i, j):
    return U_OUT + 4 * i + j, U_OUT // 2 + 2 * i + j // 2, OUT_B + 4 * i + j - 1


def group_unit_at(g, j):
    return U_SWA + 4 * g + j, U_SWA // 2 + 2 * g + j // 2, SWA + 4 * g + j - 1


def consts_array():
    parts, where, at = [], {}, 0

    def put(name, a):
        nonlocal at
        full = np.zeros((P, a.shape[1]), np.float32)
        full[:a.shape[0]] = a
        parts.append(full)
        where[name] = (at, at + a.shape[1])
        at += a.shape[1]

    i = np.arange(P)
    put("ident", np.eye(P))
    for h in LEVELS:
        put(f"level{h}", (i[:, None] // (2 * h) == i[None] // (2 * h)) & (i[:, None] % (2 * h) < h)
            & (i[None] % (2 * h) >= h))
    e = np.arange(EXT)
    for h in LEVELS[-4:]:
        m = (e[:, None] // (2 * h) == e[None] // (2 * h)) & (e[:, None] % (2 * h) < h) & (e[None] % (2 * h) >= h)
        if 2 * h > DT:
            m &= (e[:, None] >= SMP) & (e[None] >= SMP)
        put(f"ext{h}", m)
    put("causal", i[None] <= i[:, None])
    put("causalT", i[:, None] <= i[None])
    put("prevT", i[:, None] > i[None])
    m = np.arange(META)
    put("meta_neg", np.where(m[None] > m[:, None], NEG, 0.0))
    keep = np.ones((P, TOK))
    keep[:, 0:SEQ:P] = 0
    keep[:, SEQ:SEQ + SMP:DT] = 0
    keep[:, SEQ + SMP] = 0
    put("keep", keep)
    row_t, row_s = i % DT, i // (GRP * DT)
    u = np.arange(DT)
    put("new_ok", u[None] <= row_t[:, None])
    put("old_ok", u[None] > row_t[:, None])
    c = np.arange(SMP)
    put("new_block", (c[None] // DT == row_s[:, None]) & (c[None] % DT <= row_t[:, None]))
    put("seq_of", (c[:, None] // DT == np.arange(DB)[None]))
    return np.ascontiguousarray(np.concatenate(parts, 1).astype(np.float32)), where


class Tally:

    def __init__(self, sem, base=0):
        self.sem, self.base, self.n = sem, base, 0

    def inc(self, ins):
        ins.then_inc(self.sem, 1)
        self.n += 1

    @property
    def value(self):
        return self.base + self.n

    def link(self, eng, ins):
        self.inc(ins)
        eng.wait_ge(self.sem, self.value)


def yoco_kernel(nc, I, OUTS):
    ctx = ExitStack()
    _, where = consts_array()
    with ctx:
        def sb(name, shape, dt=FP32):
            return ctx.enter_context(nc.sbuf_tensor(name, shape, dt))

        def sem(name):
            return ctx.enter_context(nc.semaphore(name))

        def sems(name, n):
            return [sem(f"{name}{k}") for k in range(n)]

        H = sb("H", [P, NK, TOK])
        O = sb("O", [P, NK, TOK])
        W = sb("W", [P, WR, NK, P])
        CST = sb("CST", [P, max(b for _, b in where.values())])
        ones = sb("ones", [P, P])
        RB = sb("RB", [P, TOK])
        GV = sb("GV", [P, 76])
        SK = sb("SK", [P, 4 * KV])
        SKR = sb("SKR", [P, KV])
        small = sb("small", [P, 72])
        wjunk = sb("wjunk", [P, DM], mybir.dt.bfloat16)[:]
        acc = sb("acc", [P, TOK])
        SCL = sb("SCL", [P, 4, 4])
        WSUM = sb("WSUM", [P, 2])
        undo = sb("undo", [P, 3, 4])
        GS = sb("GS", [P, 3])
        OS = sb("OS", [P, KV])
        out_fix = sb("out_fix", [P, 4])
        step = sb("step", [P, 3, 3])

        def C(name, p0=0, p1=P):
            a, b = where[name]
            return CST[p0:p1, a:b]

        ident = C("ident")
        G_A, G_KV, G_B, G_F, B_GK, G_O = 0, 16, 32, 48, 64, 72

        AR = sb("AR", [P, AR_WORDS])
        top = [0]

        def take(shape):
            n = int(np.prod(shape))
            v = AR[:, top[0]:top[0] + n]
            top[0] += n
            assert top[0] <= AR_WORDS, top
            if len(shape) == 2:
                v = v.rearrange("p (a b) -> p a b", a=shape[0])
            if len(shape) == 3:
                v = v.rearrange("p (a b c) -> p a b c", a=shape[0], b=shape[1])
            return v

        XR = take([5, DM])
        junk = take([DM])
        tn = junk[:, 0:3 * TOK].rearrange("p (a b) -> p a b", a=3)
        xt = take([2, TOK])
        NV = take([P])
        nv_sq = take([3 * NK])
        diag = take([5, P])
        sx = take([P])
        top[0] = 0
        Dd = take([2, KT * TOK])
        Dd = [Dd[:, n, :].rearrange("p (a b) -> p a b", a=KT) for n in range(2)]
        Tt = take([2, KT * TOK])
        Tt = [Tt[:, n, :].rearrange("p (a b) -> p a b", a=KT) for n in range(2)]
        qT, kT, bT = take([KT, TOK]), take([KT, TOK]), take([KT, TOK])
        kd, qe = Dd[1], Tt[1]
        kdT, kdX = take([NT, DK]), take([DK])
        Vn, Vx, Vs = take([NT, DV]), take([DV]), take([DV])
        TH = take([2, TOK])
        att, attx = take([NT, P]), take([EXT])
        S = take([KT, DV])
        S0 = take([SR, KT, DV])
        o_sb = take([2, VT * P])
        wglr = o_sb[:, 0, 0:NK * RANK].rearrange("p (a b) -> p a b", a=NK)
        sq = take([VT * P])
        rr, ra, rv = take([P]), take([P]), take([P])
        kdm = take([2, DK])
        glr = take([TOK])
        gk2 = take([DK])
        el = take([KT, NT + DB + 1])
        top[0] = 10240
        xs = take([4, TOK])
        sqa = take([2, TOK])
        x2 = take([2, TOK])
        xg = take([2, TOK])
        top[0] = 0
        YR = take([5, DM])
        top[0] = 0
        to = take([4, TOK])
        top[0] = 0
        kdup = take([KV, TOK])
        Wn, Wx, Wm = take([NT, KV * HD]), take([KV * HD]), take([KV * HD])
        THb = take([2, TOK])
        qB = take([2, TOK])
        Cc, Pp = take([2, GRP * P]), take([2, GRP * P])
        PTc, PTp = take([2, GRP * P]), take([2, GRP * P])
        on = take([2, GRP * HD])
        Kc, Vc = take([1, DB * HD]), take([1, DB * HD])
        kcat = take([DB, P + DT])
        kg, vg, vxg, vmg = take([TOK]), take([NT, HD]), take([HD]), take([HD])
        sm = take([2, 32])
        Qz, Pz = take([DB, P]), take([DB, P])
        Pn, PnT = take([SMP]), take([P])
        kwin, kwx = take([KV * HD]), take([KV * HD])

        PP = [ctx.enter_context(nc.psum_tensor(f"PP{n}", [P, 2, 512], FP32)) for n in range(2)]
        BS = ctx.enter_context(nc.psum_tensor("BS", [P, 2, 512], FP32))
        B0, B1 = BS[:, 0, :], BS[:, 1, :]
        B2, B3 = [ctx.enter_context(nc.psum_tensor(f"B{n}", [P, 512], FP32)) for n in (2, 3)]

        x0T = nc.dram_tensor("x0T", (NK, P, TOK), FP32, kind="Internal").ap()
        x1T = nc.dram_tensor("x1T", (NK, P, TOK), FP32, kind="Internal").ap()

        cst_in, x_in, vec_in = sem("cst_in"), sems("x_in", 5), sem("vec_in")
        w_in, w_staged = sems("w_in", WR), sems("w_staged", 2)
        w_summed, block_summed, w_step = sem("w_summed"), sem("block_summed"), sem("w_step")
        w_hi, w_ready = sem("w_hi"), sem("w_ready")
        o_summed, os_ready, os_done, os_step = sem("o_summed"), sem("os_ready"), sem("os_done"), sem("os_step")
        gs_ready, gs_done, gs_step = sem("gs_ready"), sem("gs_done"), sem("gs_step")
        t_ready_x, x_hi, glr_step, gate_done = sem("t_ready_x"), sem("x_hi"), sem("glr_step"), sem("gate_done")
        wglr_in, gk2_in = sem("wglr_in"), sem("gk2_in")
        proj_done, pp_free = sem("proj_done"), sems("pp_free", 2)
        setup, sink_rows, passed, stage_step = sem("setup"), sem("sink_rows"), sem("passed"), sem("stage_step")
        vecs_done, vecs_kept = sem("vecs_done"), sem("vecs_kept")
        row_ss, rs_act, rs_dve = sem("row_ss"), sem("rs_act"), sem("rs_dve")
        diag_ready, bc_done, rb_ready = sem("diag_ready"), sem("bc_done"), sem("rb_ready")
        h_ready, x0_out, glr_kept = sem("h_ready"), sems("x0_out", 2), sem("glr_kept")
        th_ready, vtr_done, vn_kept = sem("th_ready"), sem("vtr_done"), sem("vn_kept")
        g_act, decay_exp = sem("g_act"), sem("decay_exp")
        d_ready, e_ready, t_ready = sem("d_ready"), sem("e_ready"), sem("t_ready")
        scores_done, scores_kept, attx_ready = sem("scores_done"), sem("scores_kept"), sem("attx_ready")
        kde_ready, kd_ready, qe_ready = sem("kde_ready"), sem("kd_ready"), sem("qe_ready")
        kdtr_done, kdt_ready = sem("kdtr_done"), sem("kdt_ready")
        o_done, o_kept, u_done, s_ready = sem("o_done"), sem("o_kept"), sem("u_done"), sem("s_ready")
        sq_ready, ss_done, r_dve, o_gated = sem("sq_ready"), sem("ss_done"), sem("r_dve"), sem("o_gated")
        state_out = sem("state_out")
        s0_in, s0_out = sems("s0_in", SR), sems("s0_out", SR)
        extbase, vs_ready, kdm_ready = sem("extbase"), sem("vs_ready"), sem("kdm_ready")
        smp_u, smp_new = sem("smp_u"), sem("smp_new")
        h_in = sems("h_in", 4)
        xs_in, sq_a, acc_done, x1_out, acc_zero = (sems("xs_in", 4), sem("sq_a"), sem("acc_done"), sems("x1_out", 4),
                                                   sem("acc_zero"))
        ms_done, n_act, n_dve = sem("ms_done"), sem("n_act"), sem("n_dve")
        kw_done, kw_kept, win_out, vm_in = sem("kw_done"), sem("kw_kept"), sem("win_out"), sem("vm_in")
        sc_done, comb, comb_ok, sm_dve, sm_act = sem("sc_done"), sem("comb"), sem("comb_ok"), sem("sm_dve"), sem("sm_act")
        p_ready, pt_done, pt_kept, pv_done, on_ready = (sem("p_ready"), sem("pt_done"), sem("pt_kept"), sem("pv_done"),
                                                        sem("on_ready"))
        ot_done, b_gated = sem("ot_done"), sem("b_gated")
        kc_in, kct_done, kcat_ready, qz_ready, c_fill = (sems("kc_in", 2), sem("kct_done"), sem("kcat_ready"),
                                                         sem("qz_ready"), sem("c_fill"))
        kg_ready, staged, o_stat = sem("kg_ready"), sem("staged"), sem("o_stat")
        b_step, den_ready, y_scaled_v = sem("b_step"), sem("den_ready"), sem("y_scaled_v")
        xg_ready, yt_done, y_kept, y_scaled, y_out = (sem("xg_ready"), sem("yt_done"),
                                                                sem("y_kept"), sem("y_scaled"), sem("y_out"))

        ds = bass.ds
        COLS = [slice(t * P, (t + 1) * P) for t in range(NT)] + [slice(SEQ, TOK)]
        WID = [P] * NT + [EXT]

        def halves(ap):
            return ap.rearrange("p (c n) -> p c n", c=2)

        def PV(k):
            return PP[k % 2][:, :, 0:HALF]

        def tile(buf, n):
            return buf[:, n, :] if isinstance(n, int) else buf[:, ds(n, 1), :].rearrange("p a n -> p (a n)")

        def bank4(b, w=P):
            return b[:, 0:4 * w].rearrange("p (a n) -> p a n", a=4)

        def own_scores(n=P, w=P):
            return BS[0:n].rearrange("p b (h x) -> p h b x", h=2)[:, :, :, 0:w]

        def old_scores(a=0):
            return BS[:].rearrange("p b (h x) -> p h b x", h=2)[:, :, :, P + a:2 * P]

        def by_head(ap, w=P):
            return ap.rearrange("p (h b n) -> p h b n", h=2, b=2)[:, :, :, 0:w]

        def over(ap, n, axis=1):
            shape = list(ap.shape)
            shape.insert(axis, n)
            return ap.unsqueeze(axis).broadcast_to(shape)

        def right(ap, l):
            h = LEVELS[l]
            return ap.rearrange("p (b c) -> p b c", c=2 * h)[:, :, h:2 * h]

        def parts(buf, n):
            v = buf[:, n, :].bitcast(FP16)
            return v[:, 0:TOK], v[:, TOK:2 * TOK]

        def w_parts(b):
            v = W[:, 2 + b].rearrange("p k n -> p (k n)").bitcast(FP16)
            v = v.rearrange("p (s k n) -> p s k n", s=2, k=NK)
            return v[:, 0], v[:, 1]

        def unscale(j, kind=1):
            return SCL[:, j % 4, kind:kind + 1]

        def alone(eng):
            eng.sem_inc(passed, 1)

        ss_c, ms_c, lg_c, rs_c, nt_c = (small[:, 40 + 5 * k:45 + 5 * k] for k in range(5))
        eps_c = small[:, 65:66]

        block = ctx.enter_context(nc.Block())

        @block.sync
        def _(sp):
            sp.dma_start(CST[:], I["consts"]).then_inc(cst_in, 16)
            for t in range(NT):
                sp.dma_start(XR[:, t, :], I["x_prompt"][0, t * P:(t + 1) * P, :]).then_inc(x_in[t], 16)
            sp.dma_start(XR[0:SMP, NT, :], I["x_sample"].rearrange("b t d -> (b t) d")).then_inc(x_in[NT], 16)
            sp.dma_start(XR[SMP:EXT, NT, :], I["meta_tokens"]).then_inc(x_in[NT], 16)
            rows = ((G_A, "norm_a", NK), (G_B, "norm_b", NK), (B_GK, "b_gk2_a", KT * HEADS), (G_O, "onorm_a", VT))
            for at, name, n in rows:
                sp.dma_start(NV[at:at + n, :], I[name].rearrange("a (n p) -> (a n) p", p=P)).then_inc(vec_in, 16)
            for at, name in ((G_KV, "norm_kv"), (G_F, "norm_f")):
                sp.dma_start(NV[at:at + NK, :], I[name].rearrange("(n p) -> n p", p=P)).then_inc(vec_in, 16)
            sp.dma_start(small[0:1, 0:32], I["sinks_b"]).then_inc(vec_in, 16)
            sp.dma_start(small[0:KV, 32:36], I["sinks_b"].rearrange("a (g r) -> (a g) r", r=GRP)).then_inc(vec_in, 16)
            w_in_a = I["w_in_a"][0].rearrange("(k p) n -> p k n", p=P)
            sp.dma_start(wglr, w_in_a[:, :, 6144:6144 + RANK]).then_inc(wglr_in, 16)

            def weights(u, j, src, col, whole=None):
                if whole is not None:
                    sp.wait_ge(proj_done, NK + whole)
                elif not (isinstance(u, int) and u < 2):
                    sp.wait_ge(w_ready, 2 * u - 2)
                alone(sp)
                sp.dma_start(W[:, j % 2, :, :], src[:, :, ds(col, P)]).then_inc(w_staged[j % 2], 16)

            def head_weights(h):
                kinds = [4096 + h * DV, 4096 + h * DV + P, 4096 + h * DV + 2 * P, 4096 + h * DV + 3 * P,
                         2048 + h * DV, 2048 + h * DV + P, 2048 + h * DV + 2 * P, 2048 + h * DV + 3 * P,
                         1024 + h * DK, 1024 + h * DK + P, h * DK, h * DK + P]
                for j, col in enumerate(kinds):
                    weights(head_unit_at(h, j)[0], j, w_in_a, col)

            head_weights(0)
            with sp.Fori(1, HEADS) as h:
                head_weights(h)
            w_out_a = I["w_out_a"][0].rearrange("(k p) n -> p k n", p=P)
            for n in range(NK):
                if n < 2:
                    sp.wait_ge(w_ready, 2 * (U_KV - 2 + n) + 2)
                elif n < 4:
                    sp.wait_ge(proj_done, NK + OUT_A - 3 + n)
                else:
                    sp.wait_ge(proj_done, NK + OUT_A + n - 3)
                sp.dma_start(W[:, n % WR, 0:K_A, :], w_out_a[:, 0:K_A, n * P:(n + 1) * P]).then_inc(w_in[n % WR], 16)
            for j in range(WR):
                sp.wait_ge(proj_done, NK + OUT_A + 12 + j + 1)
                sp.dma_start(W[:, j].rearrange("p (k u) n -> p k (u n)", k=VT),
                             w_out_a[:, K_A:NK, j * 4 * P:(j + 1) * 4 * P]).then_inc(w_in[j], 16)
            w_kv = I["w_kv"].rearrange("(k p) n -> p k n", p=P)
            for j in range(8):
                weights(U_KV + j, j, w_kv, j * P, OUT_A2 + 4 * (j + 1) if j < 2 else None)
            w_in_b = I["w_in_b"][0].rearrange("(k p) n -> p k n", p=P)
            with sp.Fori(0, KV) as g:
                for j, col in enumerate((2048, 2048 + P, 0, P)):
                    weights(group_unit_at(g, j)[0], j, w_in_b, g * (GRP * HD) + col)
            w_out_b = I["w_out_b"][0].rearrange("(k p) n -> p k n", p=P)

            with sp.Fori(0, NK // 4) as i:
                for j in range(4):
                    weights(out_unit_at(i, j)[0], j, w_out_b, (4 * i + j) * P)

        @block.tensor
        def _(pe):
            mm = nc.tensor.matmul

            def transpose(out, in_):
                k = in_.shape[0]
                b = in_.start_partition() if callable(in_.start_partition) else in_.start_partition
                return nc.tensor.transpose(out, in_, CST[b:b + k, b:b + k])

            pe.wait_ge(cst_in, 16)
            pe.wait_ge(vec_in, 128)
            pe.wait_ge(setup, 1)
            transpose(B2[:, 0:76], NV[0:76, :])
            mm(B3[:, 0:32], ones[0:1, :], small[0:1, 0:32], start=True, stop=True)
            pe.wait_ge(sink_rows, 1)
            mm(B3[:, 32:40], sx[0:KV, :], ident[0:KV, 0:KV], start=True, stop=True).then_inc(vecs_done, 1)

            def x_tile(n):
                if n >= 2:
                    pe.wait_ge(pp_free[n % 2], n // 2)
                for t in range(NT):
                    if n == 0:
                        pe.wait_ge(x_in[t], 16)
                    transpose(PP[n % 2][:, 0, COLS[t]], XR[:, t, n * P:(n + 1) * P])
                if n == 0:
                    pe.wait_ge(x_in[NT], 32)
                transpose(PP[n % 2][:, 1, 0:EXT], XR[0:EXT, NT, n * P:(n + 1) * P]).then_inc(proj_done, 0 + 1)

            def block_sum(u, j, out, freed=None):
                pe.wait_ge(w_summed, u + 1)
                if freed is not None:
                    pe.wait_ge(pp_free[j % 2], freed)
                alone(pe)
                mm(out, ones[:], WSUM[:, j % 2:j % 2 + 1], start=True, stop=True).then_inc(block_summed, 1)

            def low_rank(k):
                pe.wait_ge(t_ready_x, k + 1)
                for c, b in enumerate((B2, B3)):
                    last = mm(b[0:RANK, 0:HALF], wglr[:, k, :], tn[:, k % 3, c * HALF:(c + 1) * HALF], start=(k == 0),
                              stop=(k == NK - 1))
                last.then_inc(glr_step, 1)

            pe.wait_ge(vecs_kept, 2)
            pe.wait_ge(gs_ready, 2)
            mm(B3[:, 64:67], ones[:], GS[:], start=True, stop=True).then_inc(gs_done, 1)
            x_tile(0)
            x_tile(1)
            pe.wait_ge(diag_ready, 5)
            for t in range(NT):
                mm(B0[:, COLS[t]], ones[:], diag[:, t, :], start=True, stop=True)
            mm(B1[:, 0:EXT], ones[0:EXT, :], diag[0:EXT, NT, 0:EXT], start=True, stop=True).then_inc(bc_done, 1)
            pe.wait_ge(wglr_in, 16)
            for n in range(2, NK):
                x_tile(n)
                low_rank(n - 2)
                if n == 6:
                    pe.wait_ge(rb_ready, 1)
                    block_sum(0, 0, B0[:, 0:1])
            low_rank(NK - 2)
            low_rank(NK - 1)

            def project(at, j, use, half, src, fresh=None, ks=(0, NK), after=None):
                u = at[0]
                w_high, w_low = w_parts(j % 2)
                for k in range(*ks):
                    if k % (NK // 2) == 0:
                        pe.wait_ge(w_ready, 2 * u + 1 + 2 * k // NK)
                    if k == 0:
                        pe.wait_ge(pp_free[j % 2], 8 + half + use // 2)
                    if k == 4 and after is not None:
                        v, freed = after
                        block_sum(v, j + 1, PP[(j + 1) % 2][:, 1, 300:301], freed)
                    if fresh is not None:
                        pe.wait_ge(h_ready, fresh + k + 1)
                    high, low = parts(src, k)
                    for w, x, s_, e in ((w_high, high, k == 0, False), (w_high, low, False, False),
                                        (w_low, high, False, k == NK - 1)):
                        for c in range(2):
                            last = mm(PP[j % 2][:, c, 0:HALF], w[:, k, :], x[:, c * HALF:(c + 1) * HALF], start=s_, stop=e)
                if ks[1] == NK:
                    last.then_inc(proj_done, 1)

            def use_of(j):
                return j if j < 8 else j + 2

            def head_unit(h, j, ks, more):
                after = None
                if j < U_HEAD - 1 or more:
                    freed = 4 if j + 1 in (8, 9) else use_of(j + 1) // 2
                    after = head_unit_at(h, j + 1)[0], 8 + 7 * h + freed
                project(head_unit_at(h, j), j, use_of(j), 7 * h, H, fresh=0 if first(h) and j == 0 else None, ks=ks, after=after)

            def decay(h, kt):
                pe.wait_ge(pp_free[kt], 8 + 7 * h + 4)
                pe.wait_ge(w_step, 6 * head_unit_at(h, 8 + kt)[0] + 1)
                if kt == 0:
                    pe.wait_ge(gk2_in, 16 * (h + 1))
                    pe.wait_ge(glr_kept, 1)
                for c in range(2):
                    last = mm(PP[kt][:, c, 0:HALF], gk2[0:RANK, kt * P:(kt + 1) * P],
                              glr[0:RANK, c * HALF:(c + 1) * HALF], start=True, stop=True)
                last.then_inc(proj_done, 1)

            def v_rows(h, j, after=None):
                pe.wait_ge(pp_free[j % 2], 8 + 7 * h + (4 + j) // 2 + 1)
                if j == 0 and after is not None:
                    pe.wait_ge(r_dve, NORM_STEPS * (5 * after + 3) + 1)
                    pe.wait_ge(s_ready, 10 * after + 10)
                elif j:
                    pe.wait_ge(vn_kept, 4 * h + j)
                for t in range(NT):
                    transpose(B1[:, COLS[t]], TH[:, j % 2, COLS[t]])
                transpose(B3[0:EXT, 0:P], TH[:, j % 2, SEQ:TOK]).then_inc(vtr_done, 1)

            def scores(i, l):
                a = b = Tt[l % 2]
                if l < NL - 1:
                    pe.wait_ge(t_ready, (NL - 1) * i + l + 1)
                else:
                    a, b = kT, qT
                if l >= 2:
                    pe.wait_ge(scores_kept, NL * i + l - 1)
                bank = (B0, B1)[l % 2]

                def queries(kt, cols):
                    return b[:, kt, cols] if l == NL - 1 else right(b[:, kt, cols], l)

                w = P if l == NL - 1 else P // 2
                for t in range(NT):
                    for kt in range(KT):
                        last = mm(bank[:, t * w:(t + 1) * w], a[:, kt, COLS[t]], queries(kt, COLS[t]), start=(kt == 0),
                                  stop=(kt == KT - 1))
                x = l - (NL - NLX)
                if x >= 0:
                    w = EXT if l == NL - 1 else EXT // 2
                    for kt in range(KT):
                        last = mm(B2[0:EXT, x * EXT:x * EXT + w], a[:, kt, SEQ:TOK], queries(kt, slice(SEQ, TOK)),
                                  start=(kt == 0), stop=(kt == KT - 1))
                last.then_inc(scores_done, 1)

            def kd_rows(i):
                pe.wait_ge(kd_ready, i + 1)
                for kt, bank in enumerate((B3, B0)):
                    if kt:
                        pe.wait_ge(scores_kept, NL * i + NL - 1)
                    for t in range(NT):
                        last = transpose(bank[:, COLS[t]], kd[:, kt, COLS[t]])
                    last.then_inc(kdtr_done, 1)
                pe.wait_ge(scores_kept, NL * i + NL)
                alone(pe)
                for kt in range(KT):
                    last = transpose(B1[0:EXT, kt * P:(kt + 1) * P], kd[:, kt, SEQ:TOK])
                last.then_inc(kdtr_done, 1)

            def update(i, t):
                for kt, bank in enumerate((B2, B3)):
                    if t < 0:
                        last = mm(bank[:], kdX[SMP:EXT, kt * P:(kt + 1) * P], Vx[SMP:EXT, :], start=True, stop=True)
                    else:
                        last = mm(bank[:], kdT[:, t, kt * P:(kt + 1) * P], Vn[:, t, :], start=True, stop=True)
                    last.then_inc(u_done, 1)

            def meta_update(i):
                pe.wait_ge(kdt_ready, 3 * i + 3)
                pe.wait_ge(vn_kept, 4 * i + 4)
                pe.wait_ge(attx_ready, NLX * i + NLX)
                alone(pe)
                update(i, -1)

            def sumsq(i, t):
                pe.wait_ge(sq_ready, 5 * i + t + 1)
                if t:
                    pe.wait_ge(r_dve, NORM_STEPS * (5 * i + t - 1) + 1)
                w = WID[t]
                for v in range(VT):
                    last = mm(B1[:, 0:w], ones[:], sq[:, v * w:(v + 1) * w], start=(v == 0), stop=(v == VT - 1))
                last.then_inc(ss_done, 1)

            def tile_step(i, t):
                pe.wait_ge(s_ready, 10 * i + 2 * (t + 1))
                if t == 0:
                    pe.wait_ge(qe_ready, i + 1)
                else:
                    pe.wait_ge(o_kept, 5 * i + t)
                for v in range(VT):
                    out = B0[:, v * P:(v + 1) * P]
                    mm(out, Vn[:, t, v * P:(v + 1) * P], att[:, t, :], start=True, stop=False)
                    for kt in range(KT):
                        last = mm(out, S[:, kt, v * P:(v + 1) * P], qe[:, kt, COLS[t]], start=False, stop=(kt == KT - 1))
                last.then_inc(o_done, 1)
                if t:
                    sumsq(i, t - 1)
                update(i, t)

            def ext_base(i):
                pe.wait_ge(o_kept, 5 * i + 4)
                for v in range(VT):
                    last = mm(B0[:, v * EXT:(v + 1) * EXT], Vx[0:EXT, v * P:(v + 1) * P], attx[0:EXT, :],
                              start=(v == 0), stop=False, skip_group_check=True)
                last.then_inc(extbase, 1)

            def seq_state(i, s, kt):
                if kt == 0:
                    pe.wait_ge(s0_in[s % SR], 16 * (2 * i + s // SR + 1))
                    for v in range(VT):
                        for k2 in range(KT):
                            a = v * EXT + DT * s
                            last = mm(B0[:, a:a + DT], S0[:, s % SR, k2, v * P:(v + 1) * P],
                                      qe[:, k2, SEQ + DT * s:SEQ + DT * (s + 1)], start=False,
                                      stop=(s == DB - 1 and v == VT - 1 and k2 == KT - 1), skip_group_check=True)
                    if s == DB - 1:
                        last.then_inc(o_done, 1)
                    pe.wait_ge(kdm_ready, DB * i + s + 1)
                    if s == 0:
                        pe.wait_ge(vs_ready, i + 1)
                        pe.wait_ge(s_ready, 10 * i + 10)
                    else:
                        pe.wait_ge(smp_new, 2 * DB * i + 2 * s)
                else:
                    pe.wait_ge(smp_new, 2 * DB * i + 2 * s + 1)
                mm(B2[:], kdm[0:SMP, s % 2, kt * P:(kt + 1) * P], Vs[0:SMP, :], start=True, stop=True).then_inc(smp_u, 1)

            def out_early(a, b):
                for f in range(a, b):
                    n, k = divmod(f, K_A)
                    if k == 0:
                        pe.wait_ge(w_in[n % WR], 16 * (n // WR + 1))
                        pe.wait_ge(pp_free[n % 2], 8 + (OUT_A + n) // 2)
                    if f == 0:
                        pe.wait_ge(o_gated, 5 * (HEADS - 1))
                    for c in range(2):
                        last = mm(PP[n % 2][:, c, 0:HALF], W[:, n % WR, k, :], O[:, k, c * HALF:(c + 1) * HALF],
                                  start=(k == 0), stop=(k == K_A - 1))
                    if k == K_A - 1:
                        last.then_inc(proj_done, 1)

            def head_step(i, h, more):
                rec, proj = i is not None, h is not None

                def piece(n, parts):
                    a, b = n * (NK // parts), (n + 1) * (NK // parts)
                    if proj:
                        head_unit(h, a // NK, (a % NK, (b - 1) % NK + 1), more)
                    else:
                        out_early(a, b)

                for n in range(8):
                    piece(n, 2)
                    if rec and n < 7:
                        scores(i, n)
                        n == 6 and scores(i, 7)
                    elif rec:
                        kd_rows(i)
                        meta_update(i)
                for t in range(NT):
                    piece(8 + t, 2)
                    rec and tile_step(i, t)
                for q in range(24):
                    piece(24 + q, 4)
                    if rec:
                        if q == 0:
                            sumsq(i, NT - 1)
                            ext_base(i)
                        elif q <= 2 * DB:
                            seq_state(i, (q - 1) // 2, (q - 1) % 2)
                        elif q == 18:
                            if proj:
                                pe.wait_ge(vn_kept, 4 * h + 4)
                            sumsq(i, NT)
                    if proj:
                        if q in (3, 5, 7, 9):
                            v_rows(h, (q - 3) // 2, i)
                        if q in (6, 10):
                            decay(h, (q - 6) // 4)

            head_step(None, 0, True)
            with pe.Fori(0, HEADS - 2) as i:
                head_step(i, i + 1, True)
            head_step(HEADS - 2, HEADS - 1, False)
            head_step(HEADS - 1, None, False)

            def mean_square():
                for c, b in enumerate((B0, B1)):
                    last = mm(b[:, 0:HALF], ones[:], acc[:, c * HALF:(c + 1) * HALF], start=True, stop=True)
                last.then_inc(ms_done, 1)

            pe.wait_ge(o_gated, 5 * HEADS)
            for n in range(NK):
                m, u = divmod(n, 4)
                if u == 0:
                    pe.wait_ge(w_in[m], 16 * (NK // WR + 1))
                pe.wait_ge(pp_free[n % 2], 8 + (OUT_A2 + n) // 2)
                for k in range(VT):
                    for c in range(2):
                        last = mm(PP[n % 2][:, c, 0:HALF], W[:, m, 4 * k + u, :], O[:, K_A + k, c * HALF:(c + 1) * HALF],
                                  start=(k == 0), stop=(k == VT - 1))
                last.then_inc(proj_done, 1)
            pe.wait_ge(acc_done, NK)
            mean_square()

            block_sum(U_KV, 0, PP[0][:, 1, 300:301], 8 + KVP // 2)
            for j in range(8):
                project(kv_unit_at(j), j, j, KVP // 2, O, fresh=NK if j == 0 else None,
                        after=(U_KV + j + 1, 8 + KVP // 2 + (j + 1) // 2))
                if j >= 5:
                    v = j - 5
                    pe.wait_ge(pp_free[v % 2], 8 + KVP // 2 + (4 + v) // 2 + 1)
                    if v:
                        pe.wait_ge(vn_kept, 4 * HEADS + v)
                    else:
                        pe.wait_ge(rb_ready, 2)
                    for t in range(NT):
                        transpose(B1[:, COLS[t]], THb[:, v % 2, COLS[t]])
                    transpose(B3[0:EXT, 0:P], THb[:, v % 2, SEQ:TOK]).then_inc(vtr_done, 1)
            pe.wait_ge(pp_free[1], 8 + KVP // 2 + 4)
            pe.wait_ge(vn_kept, 4 * HEADS + 3)
            for t in range(NT):
                transpose(B1[:, COLS[t]], THb[:, 1, COLS[t]])
            transpose(B3[0:EXT, 0:P], THb[:, 1, SEQ:TOK]).then_inc(vtr_done, 1)
            for g in range(KV):
                last = transpose(B2[:, g * HD:(g + 1) * HD], kdup[0:HD, g, SEQ - P:SEQ])
            last.then_inc(kw_done, 1)
            for g in range(KV):
                last = transpose(B0[0:SMP, g * HD:(g + 1) * HD], kdup[0:HD, g, SEQ:SEQ + SMP])
            last.then_inc(kw_done, 1)
            pe.wait_ge(kw_kept, 2)
            pe.wait_ge(vn_kept, 4 * HEADS + 4)

            def batch_scores(i, k):
                if k == 0:
                    pe.wait_ge(kg_ready, i + 1)
                    for b in range(2):
                        pe.wait_ge(pp_free[b], 8 + SWA // 2 + 2 * i + 2)
                elif k < 5:
                    pe.wait_ge(comb_ok, 6 * i + k)
                alone(pe)
                for r in range(GRP):
                    a = HD * (r % 2)
                    q = qB[a:a + HD, r // 2, :]
                    key = kg[a:a + HD, :]
                    bank, c = (B0, B1)[r % 2], 2 * P * (r // 2)
                    if k < 4:
                        mm(bank[:, c:c + P], q[:, COLS[k]], key[:, COLS[k]], start=True, stop=True)
                        if k:
                            last = mm(bank[:, c + P:c + 2 * P], q[:, COLS[k]], key[:, COLS[k - 1]], start=True, stop=True)
                        else:
                            last = mm(bank[:, c + 2 * P - META:c + 2 * P], q[:, COLS[0]], key[:, SEQ + SMP:TOK],
                                      start=True, stop=True)
                    elif k == 4:
                        last = mm(bank[0:META, c:c + META], q[:, SEQ + SMP:TOK], key[:, SEQ + SMP:TOK],
                                  start=True, stop=True)
                if k == 5:
                    pe.wait_ge(kcat_ready, 2 * i + 2)
                    pe.wait_ge(qz_ready, 4 * i + 4)
                    for s in range(DB):
                        last = mm(B0[:, 0:P + DT], Qz[0:HD, s, :], kcat[0:HD, s, :], start=(s == 0), stop=(s == DB - 1))
                last.then_inc(sc_done, 1)

            def cache_keys(i):
                pe.wait_ge(kc_in[0], 16 * (i + 1))
                pe.wait_ge(comb_ok, 6 * i + 5)
                alone(pe)
                for s in range(DB):
                    last = transpose((B0, B1)[s // 4][0:HD, (s % 4) * P:(s % 4 + 1) * P], Kc[:, 0, s * HD:(s + 1) * HD])
                last.then_inc(kct_done, 1)

            def batch_pt(i, k):
                pe.wait_ge(p_ready, 6 * i + k + 1)
                alone(pe)
                if k < 4:
                    for r in range(GRP):
                        last = transpose(B2[:, r * P:(r + 1) * P], Pp[:, k % 2, r * P:(r + 1) * P])
                elif k == 4:
                    for r in range(GRP):
                        last = transpose(B2[0:META, r * META:(r + 1) * META], Pp[0:META, 0, r * META:(r + 1) * META])
                else:
                    pe.wait_ge(o_stat, 2 * i + 2)
                    alone(pe)
                    transpose(B2[:, 0:P], Pp[:, 1, 0:P])
                    last = transpose(B2[0:SMP, P:2 * P], Pn[:, 0:SMP])
                last.then_inc(pt_done, 1)

            def batch_pv(i, k):
                pe.wait_ge(pt_kept, 6 * i + k + 1)
                if k:
                    pe.wait_ge(b_gated, 9 * i + k)
                if k == 0:
                    pe.wait_ge(staged, i + 1)
                if k == 5:
                    pe.wait_ge(kc_in[1], 16 * (i + 1))
                alone(pe)
                if k < 4:
                    for r in range(GRP):
                        out = B3[:, r * HD:(r + 1) * HD]
                        mm(out, PTc[:, k % 2, r * P:(r + 1) * P], vg[:, k, :], start=True, stop=False)
                        if k:
                            last = mm(out, PTp[:, k % 2, r * P:(r + 1) * P], vg[:, k - 1, :], start=False, stop=True)
                        else:
                            last = mm(out, PTp[96:P, 0, r * P:(r + 1) * P], vmg[96:P, :], start=False, stop=True)
                elif k == 4:
                    for r in range(GRP):
                        last = mm(B3[0:META, r * HD:(r + 1) * HD], PTc[SMP:EXT, 0, r * META:(r + 1) * META],
                                  vxg[SMP:EXT, :], start=True, stop=True)
                else:
                    mm(B3[:, 0:HD], PnT[0:SMP, :], vxg[0:SMP, :], start=True, stop=False)
                    for s in range(DB):
                        last = mm(B3[:, 0:HD], Pz[:, s, :], Vc[:, 0, s * HD:(s + 1) * HD], start=False, stop=(s == DB - 1))
                last.then_inc(pv_done, 1)

            def batch_ot(i, k):
                pe.wait_ge(on_ready, 6 * i + k + 1)
                alone(pe)
                if k < 5:
                    n = P if k < 4 else META
                    for u in range(2):
                        last = transpose(B3[:, u * n:(u + 1) * n], on[0:n, k % 2, u * P:(u + 1) * P])
                else:
                    last = transpose(B3[0:HD, 0:P], on[:, 1, 0:HD])
                last.then_inc(ot_done, 1)

            def group_step(i, g):
                att_, proj = i is not None, g is not None

                def piece(j, a, b):
                    if proj:
                        fresh = 2 * NK if first(g) and j == 0 else None
                        after = group_unit_at(g, j + 1)[0], 8 + SWA // 2 + 2 * g + (j + 1) // 2
                        project(group_unit_at(g, j), j, j, SWA // 2 + 2 * g, H, fresh, (a, b), after)

                for n in range(8):
                    a = NK // 2 * (n % 2)
                    piece(n // 2, a, a + NK // 4)
                    if att_:
                        if n >= 3:
                            batch_ot(i, n - 3)
                        if n < 6:
                            batch_scores(i, n)
                    if n < 7:
                        piece(n // 2, a + NK // 4, a + NK // 2)
                        if att_ and n >= 2:
                            batch_pv(i, n - 2)
                        if att_ and n >= 1:
                            batch_pt(i, n - 1)
                        if att_ and n == 4:
                            cache_keys(i)
                    else:
                        piece(3, NK - NK // 4, NK - NK // 8)
                        att_ and batch_pv(i, 5)
                        piece(3, NK - NK // 8, NK)
                        att_ and batch_ot(i, 5)

            group_step(None, 0)
            with pe.Fori(0, KV - 1) as i:
                group_step(i, i + 1)
            group_step(KV - 1, None)

            def y_rows(i, j):
                n4 = 4 * i + j
                pe.wait_ge(xg_ready, n4 + 1)
                a, b = ((B0, B2), (B1, B3))[j % 2]
                if j >= 2 or j < 0 or not first(i):
                    pe.wait_ge(y_kept, 2 * (n4 - 1))
                for t in range(NT):
                    transpose(a[:, COLS[t]], xg[:, j % 2, COLS[t]])
                transpose(b[0:EXT, 0:P], xg[:, j % 2, SEQ:TOK]).then_inc(yt_done, 1)

            pe.wait_ge(b_gated, 9 * KV)
            def out_tiles(i, more=True):
                for j in range(4):
                    after = None
                    if j < 3 or more:
                        after = out_unit_at(i, j + 1)[0], 8 + OUT_B // 2 + 2 * i + (j + 1) // 2
                    project(out_unit_at(i, j), j, j, OUT_B // 2 + 2 * i, O, 3 * NK if j == 0 and first(i) else None,
                            after=after)
                    if j or not first(i):
                        y_rows(i, j - 1)

            pe.wait_ge(os_ready, 1)
            mm(B2[:, 0:1], ones[:], out_fix[:, 0:1], start=True, stop=True).then_inc(os_done, 1)
            out_tiles(0)
            with pe.Fori(1, NK // 4 - 1) as i:
                out_tiles(i)
            out_tiles(NK // 4 - 1, False)
            y_rows(NK // 4 - 1, 3)
            pe.wait_ge(acc_done, 2 * NK)
            pe.wait_ge(y_kept, 2 * NK)
            for t in range(NT + 1):
                n = WID[t]
                last = mm(B0[0:n, 2 * t:2 * t + 2], acc[:, COLS[t]], ones[:, 0:2], start=True, stop=True)
            last.then_inc(ms_done, 1)

        @block.scalar
        def _(act):
            A = nc.scalar.activation
            act.wait_ge(setup, 1)
            for t in range(NT + 1):
                n = WID[t]
                act.wait_ge(x_in[t], 16 if t < NT else 32)
                if t:
                    act.wait_ge(row_ss, t)
                A(junk[0:n, :], XR[0:n, t, :], ACT.Square, accum_out=ss_c[0:n, t:t + 1]).then_inc(row_ss, 1)
            act.wait_ge(rs_dve, 1)
            A(lg_c, ms_c, ACT.Ln).then_inc(rs_act, 1)
            act.wait_ge(rs_act, 1)
            A(rs_c, lg_c, ACT.Exp, scale=-0.5).then_inc(rs_act, 1)
            act.wait_ge(vecs_done, 1)
            A(SK[:], B3[:, 0:32], ACT.Copy, scale=-1.0).then_inc(vecs_kept, 1)
            A(SKR[:], B3[:, 32:40], ACT.Copy, scale=-1.0).then_inc(vecs_kept, 1)

            def unit_sum(at, j):
                act.wait_ge(w_staged[j % 2], 16 * (at[1] + 1))
                if not (isinstance(at[0], int) and at[0] < 2):
                    act.wait_ge(block_summed, at[0] - 1)
                alone(act)
                x = W[:, j % 2].rearrange("p k n -> p (k n)")
                A(wjunk, x, ACT.Square, accum_out=WSUM[:, j % 2:j % 2 + 1]).then_inc(w_summed, 1)

            def unit_high(at, j):
                act.wait_ge(w_step, 6 * at[0] + 4)
                if not first(at[0]) and not (isinstance(at[0], int) and at[0] == 1):
                    act.wait_ge(proj_done, NK + at[2])
                for c in range(2):
                    ks = slice(c * NK // 2, (c + 1) * NK // 2)
                    A(w_parts(j % 2)[0][:, ks], W[:, j % 2, ks], ACT.Copy, scale=SCL[:, j % 4, 0:1]).then_inc(w_hi, 1)

            def prepare(at_fn, base, j, last=False):
                unit_high(at_fn(*base, j), j)
                if not last:
                    unit_sum(at_fn(*base, j + 1), j + 1)

            def prepare_high(at_fn, base, j):
                unit_high(at_fn(*base, j), j)

            def prepare_sum(at_fn, base, j):
                unit_sum(at_fn(*base, j), j)

            def x_high(buf, src, n, base):
                act.wait_ge(t_ready_x, base + n + 1)
                A(parts(buf, n)[0], src, ACT.Copy).then_inc(x_hi, 1)

            for n in range(NK + 1):
                if n < NK:
                    act.wait_ge(proj_done, n + 1)
                    if n >= 2:
                        act.wait_ge(t_ready_x, n - 1)
                        act.wait_ge(x0_out[n % 2], 16 * (n // 2))
                    nc.scalar.copy(xt[:, n % 2, 0:SEQ], PP[n % 2][:, 0, :])
                    nc.scalar.copy(xt[:, n % 2, SEQ:TOK], PP[n % 2][:, 1, 0:EXT]).then_inc(pp_free[n % 2], 1)
                if n:
                    x_high(H, tn[:, (n - 1) % 3, :], n - 1, 0)
                if n == 4:
                    unit_sum(head_unit_at(0, 0), 0)
                if n == 8:
                    prepare(head_unit_at, (0,), 0)
            act.wait_ge(glr_step, NK)
            for b in range(2):
                act.wait_ge(x0_out[b], 8 * NK)
            A(glr[0:RANK, 0:HALF], B2[0:RANK, 0:HALF], ACT.Copy, scale=undo[0:RANK, 0, 1:2]).then_inc(g_act, 1)
            A(glr[0:RANK, HALF:TOK], B3[0:RANK, 0:HALF], ACT.Copy, scale=undo[0:RANK, 0, 1:2]).then_inc(glr_kept, 1)
            G0 = 1

            def gate(o, th, j, done, after=None):
                act.wait_ge(proj_done, NK + done)
                if after is not None:
                    act.wait_ge(*after)
                A(halves(o), PV(j), ACT.Copy, scale=unscale(j))
                A(halves(th[:, j % 2, :]), PV(j), ACT.Tanh, scale=unscale(j, 2)).then_inc(pp_free[j % 2], 1)

            def head_gate(h, j):
                after = None
                if j >= 2:
                    after = gate_done, 4 * h + j - 1
                elif not first(h):
                    after = vtr_done, 4 * h
                gate(tile(O, VT * h + j), TH, j, USES * h + j + 1, after)

            def v_tile(h, j):
                act.wait_ge(proj_done, NK + USES * h + 5 + j + (j == 3))
                if j >= 2:
                    act.wait_ge(vtr_done, 4 * h + j - 1)
                else:
                    act.wait_ge(gate_done, 4 * h + 3 + j)
                A(halves(TH[:, j % 2, :]), PV(j), ACT.Copy, scale=unscale(4 + j)).then_inc(pp_free[j % 2], 1)

            def decay_logit(h, kt):
                act.wait_ge(proj_done, NK + USES * h + 8 + 2 * kt)
                if kt == 0:
                    act.wait_ge(vn_kept, 4 * h + 1)
                bias = GV[:, ds(B_GK + 2 * h + kt, 1)]
                A(halves(Dd[0][:, kt, :]), PV(kt), ACT.Identity, bias=bias).then_inc(g_act, 1)
                A(halves(Dd[1][:, kt, :]), PV(kt), ACT.Abs, bias=bias).then_inc(pp_free[kt], 1)

            def decay_log(h):
                for kt in range(KT):
                    act.wait_ge(pp_free[kt], 8 + 7 * h + 5)
                    A(Dd[1][:, kt, :], Dd[1][:, kt, :], ACT.Exp, scale=-1.0).then_inc(g_act, 1)
                for kt in range(KT):
                    act.wait_ge(g_act, G0 + 6 * h + 3 + kt)
                    A(Dd[1][:, kt, :], Dd[1][:, kt, :], ACT.Ln, bias=1.0).then_inc(g_act, 1)

            def q_tile(h, j):
                act.wait_ge(proj_done, NK + USES * h + 13 + j)
                if j == 0:
                    act.wait_ge(pp_free[0], 8 + 7 * h + 6)
                A(halves(qT[:, j, :]), PV(j), ACT.Copy, scale=unscale(10 + j, 3)).then_inc(pp_free[j % 2], 1)

            def level_decay(i, l):
                act.wait_ge(d_ready, (NL - 1) * i + l + 1)
                h = LEVELS[l]
                w = SEQ if l < NL - NLX else TOK
                v = Dd[l % 2][:, :, 0:w].rearrange("p k (b c) -> p k b c", c=2 * h)
                A(v[:, :, :, h:2 * h], v[:, :, :, h:2 * h], ACT.Exp, scale=1.0 / GN).then_inc(e_ready, 1)
                A(v[:, :, :, 0:h], v[:, :, :, 0:h], ACT.Exp, scale=-1.0 / GN).then_inc(e_ready, 1)

            def end_decay(i):
                act.wait_ge(kde_ready, 3 * i + 3)
                A(kd, kd, ACT.Exp, scale=-1.0 / GN).then_inc(decay_exp, 1)
                act.wait_ge(scores_done, NL * i + 6)
                A(qe, bT, ACT.Exp, scale=1.0 / GN).then_inc(decay_exp, 1)
                A(el[:, :, 0:NT], bT[:, :, P - 1:SEQ:P], ACT.Exp, scale=1.0 / GN).then_inc(decay_exp, 1)
                A(el[:, :, NT:NT + DB], bT[:, :, SEQ + DT - 1:SEQ + SMP:DT], ACT.Exp, scale=1.0 / GN).then_inc(decay_exp, 1)

            def kd_keep(i):
                act.wait_ge(kdtr_done, 3 * i + 1)
                nc.scalar.copy(kdT[:, :, 0:P], bank4(B3)).then_inc(kdt_ready, 1)
                act.wait_ge(kdtr_done, 3 * i + 2)
                nc.scalar.copy(kdT[:, :, P:DK], bank4(B0)).then_inc(kdt_ready, 1)
                act.wait_ge(kdtr_done, 3 * i + 3)
                nc.scalar.copy(kdX[0:EXT, :], B1[0:EXT, 0:DK]).then_inc(kdt_ready, 1)

            def o_keep(i, t):
                act.wait_ge(o_done, 5 * i + t + 1)
                if t >= 2:
                    act.wait_ge(o_gated, 5 * i + t - 1)
                n = VT * WID[t]
                nc.scalar.copy(o_sb[:, t % 2, 0:n], B0[:, 0:n]).then_inc(o_kept, 1)
                act.wait_ge(o_kept, 5 * i + t + 1)
                if t:
                    act.wait_ge(ss_done, 5 * i + t)
                A(sq[:, 0:n], o_sb[:, t % 2, 0:n], ACT.Square).then_inc(sq_ready, 1)

            def head_step(i, h, more):
                rec, proj = i is not None, h is not None
                if rec:
                    for l in range(4):
                        level_decay(i, l)
                for n in range(8):
                    if proj and n in (1, 3, 5):
                        prepare_sum(head_unit_at, (h,), n // 2 + 2)
                    if proj and n == 1:
                        head_gate(h, 0)
                    if rec:
                        if n < 3:
                            level_decay(i, n + 4)
                        elif n == 5:
                            end_decay(i)
                        elif n == 7:
                            kd_keep(i)
                    if proj and n == 7:
                        prepare_sum(head_unit_at, (h,), 5)
                    if proj and n % 2 == 0:
                        prepare_high(head_unit_at, (h,), n // 2 + 1)
                    if proj and n in (3, 5, 7):
                        head_gate(h, n // 2)
                for t in range(NT):
                    if proj and t % 2:
                        prepare_sum(head_unit_at, (h,), 6 + t // 2)
                    if rec:
                        o_keep(i, t)
                    if proj and t % 2 == 0:
                        prepare_high(head_unit_at, (h,), 5 + t // 2)
                    if proj and t % 2:
                        v_tile(h, t // 2)
                if proj:
                    prepare(head_unit_at, (h,), 7)
                    v_tile(h, 2)
                    prepare(head_unit_at, (h,), 8)
                    decay_logit(h, 0)
                    v_tile(h, 3)
                    prepare(head_unit_at, (h,), 9)
                    decay_logit(h, 1)
                    decay_log(h)
                    prepare(head_unit_at, (h,), 10)
                if rec:
                    o_keep(i, NT)
                if proj:
                    prepare(head_unit_at, (h,), 11, last=not more)
                    q_tile(h, 0)
                    if more:
                        prepare(head_unit_at, (h,), 12)
                    q_tile(h, 1)

            head_step(None, 0, True)
            with act.Fori(0, HEADS - 2) as i:
                head_step(i, i + 1, True)
            head_step(HEADS - 2, HEADS - 1, False)
            head_step(HEADS - 1, None, False)

            def squares(half, base):
                with act.Fori(0, NK // 4) as i:
                    for j in range(4):
                        act.wait_ge(pp_free[j % 2], 8 + half + 2 * i + j // 2 + 1)
                        if j >= 2:
                            act.wait_ge(acc_done, base + 4 * i + j - 1)
                        A(sqa[:, j % 2, :], tile(H, 4 * i + j), ACT.Square).then_inc(sq_a, 1)
                    act.wait_ge(acc_done, base + 4 * i + 4)

            squares(OUT_A2 // 2, 0)

            def root(n):
                act.wait_ge(n_dve, n + 2)
                A(RB[:], acc[:], ACT.Ln).then_inc(n_act, 1)
                act.wait_ge(n_act, n + 1)
                A(RB[:], RB[:], ACT.Exp, scale=-0.5).then_inc(n_act, 1)

            unit_sum(kv_unit_at(0), 0)
            root(0)
            for n in range(NK):
                x_high(O, xs[:, n % 4, :], n, NK)
                if n == 1:
                    unit_high(kv_unit_at(0), 0)
            unit_sum(kv_unit_at(1), 1)
            for j in range(8):
                prepare(kv_unit_at, (), j + 1)
                for n in (2 * j, 2 * j + 1):
                    x_high(H, xs[:, n % 4, :], n, 2 * NK)
                act.wait_ge(proj_done, NK + KVP + j + 1)
                if j < 4:
                    un = unscale(j)[0:HD]
                    A(halves(kdup[0:HD, 2 * j, :]), PV(j)[0:HD], ACT.Copy, scale=un).then_inc(th_ready, 1)
                    A(halves(kdup[HD:P, 2 * j, :]), PV(j)[0:HD], ACT.Copy, scale=un).then_inc(th_ready, 1)
                else:
                    if j >= 6:
                        act.wait_ge(vtr_done, 4 * HEADS + j - 5)
                    A(halves(THb[:, j % 2, :]), PV(j), ACT.Copy, scale=unscale(j)).then_inc(pp_free[j % 2], 1)
            act.wait_ge(kw_done, 1)
            nc.scalar.copy(kwin, B2[:]).then_inc(kw_kept, 1)
            act.wait_ge(kw_done, 2)
            nc.scalar.copy(kwx[0:SMP, :], B0[0:SMP, :]).then_inc(kw_kept, 1)

            def group_gate(g, j):
                after = gate_done, 4 * HEADS + 2 * g + j - 1
                if first(g):
                    after = (vtr_done, 4 * HEADS + 4) if j == 0 else None
                gate(tile(O, 2 * g + j), THb, j, SWA + 4 * g + j + 1, after)

            def group_q(g, j):
                act.wait_ge(proj_done, NK + SWA + 4 * g + 3 + j)
                if not first(g):
                    act.wait_ge(sc_done, 6 * g)
                A(halves(qB[:, j, :]), PV(j), ACT.Copy, scale=unscale(2 + j)).then_inc(pp_free[j % 2], 1)

            def batch_comb(i, k):
                if k == 4:
                    return
                act.wait_ge(sc_done, 6 * i + k + 1)
                if k == 0:
                    act.wait_ge(c_fill, i + 1)
                    nc.scalar.copy(by_head(Cc[:, 0, :])[:, :, :, P - META:P], old_scores(P - META)).then_inc(comb, 1)
                elif k < 4:
                    if k >= 2:
                        act.wait_ge(p_ready, 6 * i + k - 1)
                    nc.scalar.copy(by_head(Cc[:, k % 2, :]), old_scores()).then_inc(comb, 1)
                else:
                    act.wait_ge(p_ready, 6 * i + 4)
                    nc.scalar.copy(Cc[:, 1, 0:P], B0[:, 0:P]).then_inc(comb, 1)

            def batch_exp(i, k):
                b = k % 2
                act.wait_ge(sm_dve, 18 * i + 3 * k + 3)
                if k >= 2:
                    act.wait_ge(pt_done, 6 * i + k - 1)
                n, w, heads = ((P, P, GRP), (META, META, GRP), (P, P, 1))[max(k - 3, 0)]
                for r in range(heads):
                    A(Pp[0:n, b, r * w:(r + 1) * w], Cc[0:n, b, r * w:(r + 1) * w], ACT.Exp, scale=HD ** -0.5,
                      bias=sm[0:n, b, 4 + r:5 + r], accum_out=sm[0:n, b, 16 + r:17 + r]).then_inc(sm_act, 1)
                A(sm[0:n, b, 12:12 + heads], sm[0:n, b, 8:8 + heads], ACT.Exp).then_inc(p_ready, 1)

            def group_step(i, g):
                att_, proj = i is not None, g is not None

                def keep_cache_keys():
                    act.wait_ge(kct_done, i + 1)
                    for c, b in enumerate((B0, B1)):
                        nc.scalar.copy(kcat[0:HD, 4 * c:4 * c + 4, 0:P], bank4(b)[0:HD]).then_inc(kcat_ready, 1)

                def batch(k):
                    if att_:
                        batch_comb(i, k)
                        batch_exp(i, k)

                for n in range(8):
                    if n < 6:
                        batch(n)
                    if n == 4 and att_:
                        keep_cache_keys()
                    if n % 2 == 0 and proj:
                        prepare_high(group_unit_at, (g,), n // 2 + 1)
                    if n % 2 and proj:
                        prepare_sum(group_unit_at, (g,), n // 2 + 2)
                        group_gate(g, n // 2) if n < 4 else group_q(g, n // 2 - 2)
                if att_:
                    act.wait_ge(b_gated, 9 * i + 9)
                    act.wait_ge(w_summed, U_SWA + 4 * i + 10 if proj else U_OUT + 2)
                    o = O[:, ds(2 * i, 2), :]
                    A(wjunk[:, 0:2 * TOK].rearrange("p (a n) -> p a n", a=2), o, ACT.Square,
                      accum_out=OS[:, ds(i, 1)]).then_inc(o_summed, 1)
                    act.wait_ge(o_summed, i + 1)

            group_step(None, 0)
            with act.Fori(0, KV - 1) as i:
                group_step(i, i + 1)
            group_step(KV - 1, None)

            for n in range(NK):
                x_high(O, to[:, n % 4, :], n, 3 * NK)

            def out_tiles(i, more=True):
                for j in range(4):
                    if j < 3 or more:
                        prepare(out_unit_at, (i,), j + 1, last=not more and j == 2)
                    act.wait_ge(pp_free[j % 2], 8 + OUT_B // 2 + 2 * i + j // 2 + 1)
                    if j >= 2 or not first(i):
                        act.wait_ge(acc_done, NK + 4 * i + j - 1)
                        act.wait_ge(yt_done, 4 * i + j - 1)
                    A(sqa[:, j % 2, :], x2[:, j % 2, :], ACT.Square).then_inc(sq_a, 1)
                    A(xg[:, j % 2, :], x2[:, j % 2, :], ACT.Copy, scale=GV[:, ds(G_F + 4 * i + j, 1)]).then_inc(xg_ready, 1)

            out_tiles(0)
            with act.Fori(1, NK // 4 - 1) as i:
                out_tiles(i)
            out_tiles(NK // 4 - 1, False)
            act.wait_ge(n_dve, 3)
            A(lg_c, ms_c, ACT.Ln).then_inc(n_act, 1)
            act.wait_ge(n_act, 3)
            A(rs_c, lg_c, ACT.Exp, scale=-0.5).then_inc(n_act, 1)
            for t in (1, 3):
                act.wait_ge(n_dve, 7)
                A(YR[:, t, :], YR[:, t, :], ACT.Copy, scale=rs_c[:, t:t + 1]).then_inc(y_scaled, 1)

        @block.vector
        def _(dve):
            V = nc.vector
            TT, TS, STT = V.tensor_tensor, V.tensor_scalar, V.scalar_tensor_tensor

            V.memset(ones[:], 1.0)
            V.memset(eps_c, EPS)
            V.memset(small[:, 40:65], 1.0).then_inc(setup, 1)
            dve.wait_ge(setup, 1)

            def newton(y, x, tmp, tally):
                tally.link(dve, TT(tmp, y, y, ALU.mult))
                tally.link(dve, TT(tmp, tmp, x, ALU.mult))
                tally.link(dve, TS(tmp, tmp, -0.5, 1.5, ALU.mult, ALU.add))
                tally.link(dve, TT(y, y, tmp, ALU.mult))

            dve.wait_ge(vec_in, 128)
            V.tensor_copy(sx[0:KV, :].rearrange("p (s r t) -> p s r t", r=GRP, t=DT),
                          small[0:KV, 32:36].unsqueeze(1).unsqueeze(3).broadcast_to([KV, DB, GRP, DT])).then_inc(sink_rows, 1)

            dve.wait_ge(row_ss, NT + 1)
            c = Tally(rs_dve)
            c.link(dve, TS(ms_c, ss_c, 1.0 / DM, EPS, ALU.mult, ALU.add))
            dve.wait_ge(rs_act, 2)
            newton(rs_c, ms_c, nt_c, c)
            dve.wait_ge(cst_in, 16)
            for t in range(NT + 1):
                TS(diag[:, t, :], ident, rs_c[:, t:t + 1], None, ALU.mult).then_inc(diag_ready, 1)
            dve.wait_ge(vecs_done, 1)
            c.link(dve, V.tensor_copy(GV[:], B2[:, 0:76]))

            def scale_of(out, total, x, half, guess, factor, tally):
                tally.link(dve, TS(x, total, factor ** -2, 1e-36, ALU.mult, ALU.max))
                tally.link(dve, TS(half.bitcast(I32), x.bitcast(I32), 1, None, ALU.logical_shift_right))
                tally.link(dve, TS(guess.bitcast(I32), half.bitcast(I32), -1, MAGIC, ALU.mult, ALU.add))
                tally.link(dve, TS(out.bitcast(I32), guess.bitcast(I32), HI_EXP, None, ALU.bitwise_and))

            gt = Tally(gs_ready)
            gt.link(dve, TT(nv_sq, GV[:, 0:3 * NK], GV[:, 0:3 * NK], ALU.mult))
            gt.link(dve, V.tensor_reduce(GS[:], nv_sq.rearrange("p (a n) -> p a n", a=3), AX.X, ALU.add))
            dve.wait_ge(vecs_kept, 2)
            dve.wait_ge(gs_done, 1)
            gt = Tally(gs_step)
            scale_of(GS[:], B3[:, 64:67], step[:, 0, :], step[:, 1, :], step[:, 2, :], X_MAX, gt)
            gt.link(dve, V.reciprocal(undo[:, :, 0], GS[:]))
            for k, f in ((1, 1.0), (2, 0.5), (3, 1 / 16)):
                gt.link(dve, TS(undo[:, :, k], undo[:, :, 0], f, None, ALU.mult))
            gt.link(dve, TT(GV[:, 0:3 * NK].rearrange("p (a n) -> p a n", a=3), GV[:, 0:3 * NK].rearrange(
                "p (a n) -> p a n", a=3), GS[:].unsqueeze(2).broadcast_to([P, 3, NK]), ALU.mult))
            c.link(dve, TS(GV[:, G_O:G_O + VT], GV[:, G_O:G_O + VT], 0.5, None, ALU.mult))
            dve.wait_ge(bc_done, 1)
            V.tensor_copy(RB[:, 0:SEQ], B0[:])
            V.tensor_copy(RB[:, SEQ:TOK], B1[:, 0:EXT]).then_inc(rb_ready, 1)
            dve.wait_ge(rb_ready, 1)

            def unit_scale(at, j, norm, total=None):
                u = at[0]
                total = PP[j % 2][:, 1, 300:301] if total is None else total
                dve.wait_ge(block_summed, u + 1)
                t = Tally(w_step, 6 * u)
                x, half, guess = (step[:, k, 0:1] for k in range(3))
                scale_of(SCL[:, j % 4, 0:1], total, x, half, guess, W_MAX, t)
                t.link(dve, V.reciprocal(x, SCL[:, j % 4, 0:1]))
                t.link(dve, TS(SCL[:, j % 4, 1:4], undo[:, norm, 1:4], x, None, ALU.mult))

            def unit_low(at, j, halves_=(0, 1)):
                for c in halves_:
                    ks = slice(c * NK // 2, (c + 1) * NK // 2)
                    high, low = w_parts(j % 2)
                    dve.wait_ge(w_hi, 2 * at[0] + c + 1)
                    STT(out=low[:, ks], in0=W[:, j % 2, ks], scalar=SCL[:, j % 4, 0:1], in1=high[:, ks], op0=ALU.mult,
                        op1=ALU.subtract).then_inc(w_ready, 1)

            def x_low(buf, src, n, base):
                dve.wait_ge(x_hi, base + n + 1)
                TT(parts(buf, n)[1], src, parts(buf, n)[0], ALU.subtract).then_inc(h_ready, 1)

            for n in range(NK + 1):
                if n < NK:
                    dve.wait_ge(pp_free[n % 2], n // 2 + 1)
                    if n >= 3:
                        dve.wait_ge(glr_step, n - 2)
                        dve.wait_ge(h_ready, n - 2)
                    STT(out=tn[:, n % 3, :], in0=xt[:, n % 2, :], scalar=GV[:, G_A + n:G_A + n + 1], in1=RB[:],
                        op0=ALU.mult, op1=ALU.mult).then_inc(t_ready_x, 1)
                if n:
                    x_low(H, tn[:, (n - 1) % 3, :], n - 1, 0)
                if n == 8:
                    unit_scale(head_unit_at(0, 0), 0, 0, B0[:, 0:1])
                if n == 9:
                    unit_low(head_unit_at(0, 0), 0)
            for b in range(2):
                dve.wait_ge(x0_out[b], 8 * NK)
            dve.wait_ge(h_ready, NK)
            V.memset(att[:, :, :].rearrange("p t n -> p (t n)"), 0.0)
            V.memset(attx, 0.0).then_inc(setup, 1)
            dve.wait_ge(setup, 2)

            def gate(o, th, j, ready):
                dve.wait_ge(*ready)
                STT(out=o, in0=th[:, j % 2, :], scalar=1.0, in1=o, op0=ALU.add, op1=ALU.mult).then_inc(gate_done, 1)

            def head_gate(h, j):
                gate(tile(O, VT * h + j), TH, j, (pp_free[j % 2], 8 + 7 * h + j // 2 + 1))

            def v_keep(base, j, rows, ext, after=None):
                dve.wait_ge(vtr_done, base + j + 1)
                if j == 0 and after is not None:
                    dve.wait_ge(extbase, after + 1)
                    dve.wait_ge(vs_ready, after + 1)
                V.tensor_copy(rows[:, :, j * P:(j + 1) * P], bank4(B1))
                V.tensor_copy(ext[0:EXT, j * P:(j + 1) * P], B3[0:EXT, 0:P]).then_inc(vn_kept, 1)

            def decay_sum(h, kt):
                dve.wait_ge(g_act, 1 + 6 * h + 5 + kt)
                STT(out=Dd[0][:, kt, :], in0=Dd[0][:, kt, :], scalar=0.0, in1=Dd[1][:, kt, :], op0=ALU.min,
                    op1=ALU.subtract).then_inc(b_step, 1)
                dve.wait_ge(b_step, 4 * h + 2 * kt + 1)
                V.tensor_tensor_scan(bT[:, kt, :], C("keep"), Dd[0][:, kt, :], 0.0, ALU.mult, ALU.add).then_inc(b_step, 1)

            def k_tile(h, j):
                dve.wait_ge(proj_done, NK + USES * h + 11 + j)
                TS(halves(kT[:, j, :]), PV(j), unscale(8 + j), None, ALU.mult).then_inc(pp_free[j % 2], 1)

            def blocks(buf, l):
                w = SEQ if l < NL - NLX else TOK
                return buf[:, :, 0:w].rearrange("p k (b c) -> p k b c", c=2 * LEVELS[l])

            def distance(i, l):
                if l == 0:
                    dve.wait_ge(b_step, 4 * i + 4)
                if l >= 2:
                    dve.wait_ge(t_ready, (NL - 1) * i + l - 1)
                b, h = blocks(bT, l), LEVELS[l]
                ref = b[:, :, :, h - 1:h].broadcast_to(list(b.shape))
                TT(blocks(Dd[l % 2], l), b, ref, ALU.subtract).then_inc(d_ready, 1)

            def level_qk(i, l):
                dve.wait_ge(e_ready, 2 * (NL - 1) * i + 2 * l + 2)
                if l == 0:
                    for b in range(2):
                        dve.wait_ge(pp_free[b], 8 + 7 * i + 7)
                if l >= 2:
                    dve.wait_ge(scores_done, NL * i + l - 1)
                h = LEVELS[l]
                T_, D_, q, k = (blocks(x, l) for x in (Tt[l % 2], Dd[l % 2], qT, kT))
                TT(T_[:, :, :, h:2 * h], q[:, :, :, h:2 * h], D_[:, :, :, h:2 * h], ALU.mult)
                TT(T_[:, :, :, 0:h], k[:, :, :, 0:h], D_[:, :, :, 0:h], ALU.mult).then_inc(t_ready, 1)

            def take_scores(i, l):
                dve.wait_ge(scores_done, NL * i + l + 1)
                if l:
                    dve.wait_ge(scores_kept, NL * i + l)
                else:
                    dve.wait_ge(t_ready, (NL - 1) * i + 1)
                bank = (B0, B1)[l % 2]
                alone(dve)
                if l == NL - 1:
                    V.copy_predicated(att, over(ident.bitcast(I32), NT), bank4(bank)).then_inc(scores_kept, 1)
                else:
                    mask = right(C(f"level{LEVELS[l]}").bitcast(I32), l)
                    dst = att.rearrange("p t (b c) -> p t b c", c=2 * LEVELS[l])[:, :, :, LEVELS[l]:2 * LEVELS[l]]
                    src = bank4(bank, P // 2).rearrange("p t (b c) -> p t b c", c=LEVELS[l])
                    V.copy_predicated(dst, over(mask, NT), src).then_inc(scores_kept, 1)

            def take_ext(i):
                for x in range(NLX):
                    if x:
                        dve.wait_ge(attx_ready, NLX * i + x)
                    alone(dve)
                    if x == NLX - 1:
                        V.copy_predicated(attx[0:EXT, :], ident[0:EXT, 0:EXT].bitcast(I32),
                                          B2[0:EXT, x * EXT:(x + 1) * EXT]).then_inc(attx_ready, 1)
                    else:
                        l = NL - NLX + x
                        src = B2[0:EXT, x * EXT:x * EXT + EXT // 2].rearrange("p (b c) -> p b c", c=LEVELS[l])
                        V.copy_predicated(right(attx[0:EXT, :], l), right(C(f"ext{LEVELS[l]}", 0, EXT).bitcast(I32), l),
                                          src).then_inc(attx_ready, 1)

            def end_distance(i):
                dve.wait_ge(t_ready, (NL - 1) * i + 6)
                for a, b, n in ((0, SEQ, P), (SEQ, SEQ + SMP, DT), (SEQ + SMP, TOK, META)):
                    v = bT[:, :, a:b].rearrange("p k (b c) -> p k b c", c=n)
                    last = v[:, :, :, n - 1:n].broadcast_to(list(v.shape))
                    TT(kd[:, :, a:b].rearrange("p k (b c) -> p k b c", c=n), v, last, ALU.subtract).then_inc(kde_ready, 1)

            def end_qk(i):
                dve.wait_ge(decay_exp, 4 * i + 1)
                TT(kd, kd, kT, ALU.mult).then_inc(kd_ready, 1)
                dve.wait_ge(decay_exp, 4 * i + 2)
                TT(qe, qe, qT, ALU.mult).then_inc(qe_ready, 1)

            def meta_state(i):
                for kt, bank in enumerate((B2, B3)):
                    dve.wait_ge(u_done, 10 * i + kt + 1)
                    V.tensor_copy(S[:, kt, :], bank[:]).then_inc(s_ready, 1)

            def state(i, t):
                if t == 0:
                    dve.wait_ge(decay_exp, 4 * i + 4)
                for kt, bank in enumerate((B2, B3)):
                    dve.wait_ge(u_done, 10 * i + 2 * (t + 1) + kt + 1)
                    dve.wait_ge(s_ready, 10 * i + 2 * t + kt + 1)
                    STT(out=S[:, kt, :], in0=S[:, kt, :], scalar=el[:, kt, t:t + 1], in1=bank[:], op0=ALU.mult,
                        op1=ALU.add).then_inc(s_ready, 1)

            def head_norm(i, t, part=None):
                if part is None:
                    for part in range(3):
                        head_norm(i, t, part)
                    return
                w = WID[t]
                c = Tally(r_dve, NORM_STEPS * (5 * i + t) + (0, 7, 15)[part])
                r, v, tmp = rr[:, 0:w], rv[:, 0:w], ra[:, 0:w]
                if part == 0:
                    dve.wait_ge(ss_done, 5 * i + t + 1)
                    if t == 0:
                        dve.wait_ge(gate_done, 4 * i + 4)
                    c.link(dve, TS(v, B1[:, 0:w], 1.0 / DV, EPS, ALU.mult, ALU.add))
                    c.link(dve, TS(tmp.bitcast(I32), v.bitcast(I32), 1, None, ALU.logical_shift_right))
                    c.link(dve, TS(r.bitcast(I32), tmp.bitcast(I32), -1, MAGIC, ALU.mult, ALU.add))
                    newton(r, v, tmp, c)
                elif part == 1:
                    newton(r, v, tmp, c)
                    newton(r, v, tmp, c)
                else:
                    x = o_sb[:, t % 2, 0:VT * w].rearrange("p (v n) -> p v n", v=VT)
                    c.link(dve, TT(x, x, over(rr[:, 0:w], VT), ALU.mult))
                    for k in range(VT):
                        o = tile(O, VT * i + k)[:, COLS[t]]
                        last = STT(out=o, in0=x[:, k, :], scalar=GV[:, G_O + k:G_O + k + 1], in1=o, op0=ALU.mult,
                                   op1=ALU.mult)
                    last.then_inc(o_gated, 1)

            def seq_state(i, s, kt):
                dve.wait_ge(smp_u, 2 * DB * i + 2 * s + kt + 1)
                x = S0[:, s % SR, kt, :]
                STT(out=x, in0=x, scalar=el[:, kt, NT + s:NT + s + 1], in1=B2[:], op0=ALU.mult,
                    op1=ALU.add).then_inc(smp_new, 1)

            def out_early(n):
                dve.wait_ge(proj_done, NK + OUT_A + n + 1)
                dve.wait_ge(h_in[n // 4], 16)
                TT(halves(H[:, n, :]), PV(n), halves(H[:, n, :]), ALU.add).then_inc(pp_free[n % 2], 1)

            def head_step(i, h, more):
                rec, proj = i is not None, h is not None

                def prepare(j, part):
                    if part == 0:
                        unit_scale(head_unit_at(h, j), j, 0)
                    unit_low(head_unit_at(h, j), j, (part,))

                def early(a, b):
                    if not proj:
                        for n in range(a // K_A, b // K_A):
                            out_early(n)

                if rec:
                    distance(i, 0)
                    distance(i, 1)
                    level_qk(i, 0)
                    distance(i, 2)
                    level_qk(i, 1)
                    distance(i, 3)
                for n in range(8):
                    if rec:
                        if n < 7:
                            take_scores(i, n)
                        if n < 5:
                            level_qk(i, n + 2)
                        if n < 3:
                            distance(i, n + 4)
                        elif n == 3:
                            end_distance(i)
                        elif n == 5:
                            end_qk(i)
                        elif n == 6:
                            take_scores(i, 7)
                            take_ext(i)
                        elif n == 7:
                            meta_state(i)
                    if proj:
                        prepare(n // 2 + 1, n % 2)
                    if proj and n % 2:
                        head_gate(h, n // 2)
                    early(8 * n, 8 * n + 8)
                for t in range(NT):
                    if rec:
                        state(i, t)
                        if t:
                            head_norm(i, t - 1)
                        early(64 + 8 * t, 72 + 8 * t)
                    if proj:
                        prepare(5 + t // 2, t % 2)
                for q in range(24):
                    if rec:
                        if 1 <= q <= 2 * DB:
                            seq_state(i, (q - 1) // 2, (q - 1) % 2)
                        if q < 3:
                            head_norm(i, NT - 1, q)
                        if q == 18:
                            head_norm(i, NT)
                    if proj and q % 4 in (1, 2) and (q < 21 or more):
                        prepare(7 + q // 4, q % 4 - 1)
                    if proj:
                        if q in (3, 5, 7, 9):
                            v_keep(4 * h, (q - 3) // 2, Vn, Vx, i)
                        if q in (11, 15):
                            k_tile(h, (q - 11) // 4)
                        if q in (13, 14):
                            decay_sum(h, q - 13)
                    early(96 + 4 * q, 100 + 4 * q)
                if rec:
                    dve.wait_ge(state_out, 16 * (i + 1))

            head_step(None, 0, True)
            with dve.Fori(0, HEADS - 2) as i:
                head_step(i, i + 1, True)
            head_step(HEADS - 2, HEADS - 1, False)
            head_step(HEADS - 1, None, False)

            with dve.Fori(0, NK // 4) as i:
                for j in range(4):
                    dve.wait_ge(proj_done, NK + OUT_A2 + 4 * i + j + 1)
                    h_ = halves(tile(H, 4 * i + j))
                    TT(h_, PV(j), h_, ALU.add).then_inc(pp_free[j % 2], 1)
            dve.wait_ge(ms_done, 1)
            cn = Tally(n_dve)
            for c_, b in enumerate((B0, B1)):
                cn.link(dve, TS(acc[:, c_ * HALF:(c_ + 1) * HALF], b[:, 0:HALF], 1.0 / DM, EPS, ALU.mult, ALU.add))
            unit_scale(kv_unit_at(0), 0, 1)
            cr = Tally(rs_dve, c.value)
            dve.wait_ge(n_act, 2)
            newton(RB[:], acc[:], x2[:, 0, :], cr)
            V.tensor_copy(small[:, 66:67], eps_c).then_inc(rb_ready, 1)

            def normed(g, n, base):
                dve.wait_ge(h_ready, base + n - 3)
                STT(out=xs[:, n % 4, :], in0=H[:, n, :], scalar=GV[:, g + n:g + n + 1], in1=RB[:], op0=ALU.mult,
                    op1=ALU.mult).then_inc(t_ready_x, 1)

            for b in range(2):
                dve.wait_ge(pp_free[b], 8 + KVP // 2)
            for n in range(NK + 1):
                if n < NK:
                    normed(G_KV, n, NK)
                if n:
                    x_low(O, xs[:, (n - 1) % 4, :], n - 1, NK)
                if n in (2, 4):
                    unit_low(kv_unit_at(0), 0, (n // 2 - 1,))
            for q in range(4):
                dve.wait_ge(x1_out[q], 4 * 16)
            for j in range(8):
                unit_scale(kv_unit_at(j + 1), j + 1, 1 if j < 7 else 2)
                unit_low(kv_unit_at(j + 1), j + 1)
                for n in (2 * j, 2 * j + 1):
                    normed(G_B, n, 2 * NK)
                for n in (2 * j, 2 * j + 1):
                    x_low(H, xs[:, n % 4, :], n, 2 * NK)
                if j < 4:
                    dve.wait_ge(th_ready, 2 * j + 2)
                    un = unscale(j)[HD:P]
                    TS(halves(kdup[0:HD, 2 * j + 1, :]), PV(j)[HD:P], un, None, ALU.mult)
                    TS(halves(kdup[HD:P, 2 * j + 1, :]), PV(j)[HD:P], un, None, ALU.mult).then_inc(pp_free[j % 2], 1)
                elif j > 4:
                    v_keep(4 * HEADS, j - 5, Wn, Wx)
            dve.wait_ge(h_ready, 3 * NK)
            V.memset(Wm[96:P, :], 0.0).then_inc(setup, 1)
            V.memset(Qz[0:HD].rearrange("p s n -> p (s n)"), 0.0)
            V.memset(Pz.rearrange("p s n -> p (s n)"), 0.0).then_inc(setup, 1)
            v_keep(4 * HEADS, 3, Wn, Wx)
            dve.wait_ge(setup, 4)

            def spread_q(i):
                for r in range(GRP):
                    a = HD * (r % 2)
                    src = qB[a:a + HD, r // 2, SEQ:SEQ + SMP].rearrange("p (s t) -> p s t", t=DT)
                    V.tensor_copy(diag_view(Qz, DT * r, DT)[0:HD], src).then_inc(qz_ready, 1)

            def diag_view(buf, off, n):
                w = GRP * DT
                a = buf.rearrange("p s n -> p (s n)")[:, 0:(P + w) * (DB - 1) + w]
                return bass.AP(tensor=a.tensor, offset=a.offset + off, ap=[list(a.ap[0]), [P + w, DB], [1, n]])

            def batch_max(i, k):
                b = k % 2
                if k < 4:
                    dve.wait_ge(comb, 5 * i + k + 1)
                    x = bank4(Cc[:, b, :])
                    alone(dve)
                    V.copy_predicated(by_head(Cc[:, b, :]), over(over(C("causal").bitcast(I32), 2), 2),
                                      own_scores()).then_inc(comb_ok, 1)
                    n, g = P, GRP
                elif k == 4:
                    dve.wait_ge(sc_done, 6 * i + 5)
                    dve.wait_ge(p_ready, 6 * i + 3)
                    n, g = META, GRP
                    x = bank4(Cc[0:META, 0, :], META)
                    TT(x.rearrange("p (h b) n -> p h b n", h=2), own_scores(META, META),
                       over(over(C("meta_neg", 0, META), 2), 2), ALU.add).then_inc(comb_ok, 1)
                else:
                    dve.wait_ge(comb, 5 * i + 5)
                    n, g = P, 1
                    alone(dve)
                    V.copy_predicated(Cc[:, 1, 0:DT], C("new_ok").bitcast(I32), B0[:, P:P + DT]).then_inc(comb_ok, 1)
                    x = Cc[:, 1, 0:P].unsqueeze(1)
                dve.wait_ge(comb_ok, 6 * i + k + 1)
                nsink = SK[0:n, ds(GRP * i, GRP)] if k < 5 else SKR[:, ds(i, 1)]
                t = Tally(sm_dve, 18 * i + 3 * k)
                m, nm, d = (sm[0:n, b, 4 * q:4 * q + g] for q in range(3))
                t.link(dve, V.tensor_reduce(m, x, AX.X, ALU.max, negate=True))
                t.link(dve, STT(out=nm, in0=m, scalar=HD ** -0.5, in1=nsink, op0=ALU.mult, op1=ALU.min))
                t.link(dve, TT(d, nm, nsink, ALU.subtract))

            def batch_keep(i, k):
                b = k % 2
                dve.wait_ge(p_ready, 6 * i + k + 1)
                n, g = ((P, GRP), (META, GRP), (P, 1))[max(k - 3, 0)]
                es, rs, den, rinv = (sm[0:n, b, 4 * q:4 * q + g] for q in (3, 4, 5, 6))
                if k >= 2:
                    dve.wait_ge(on_ready, 6 * i + k - 1)
                t = Tally(den_ready, 12 * i + 2 * k)
                t.link(dve, TT(den, es, rs, ALU.add))
                t.link(dve, V.reciprocal(rinv, den))
                if k == 5:
                    TT(Pn.rearrange("p (s u) -> p s u", u=DT), over(Pp[:, 1, 0:DT], DB),
                       C("new_block").rearrange("p (s u) -> p s u", u=DT), ALU.mult).then_inc(o_stat, 1)
                    dve.wait_ge(o_stat, 2 * i + 1)
                    TT(Pp[:, 1, 0:DT], Pp[:, 1, 0:DT], C("old_ok"), ALU.mult).then_inc(o_stat, 1)
                dve.wait_ge(pt_done, 6 * i + k + 1)
                if k >= 2:
                    dve.wait_ge(pv_done, 6 * i + k - 1)
                if k < 4:
                    TT(bank4(PTc[:, b, :]), bank4(B2), over(C("causalT"), GRP), ALU.mult)
                    last = TT(bank4(PTp[:, b, :]), bank4(B2), over(C("prevT"), GRP), ALU.mult)
                elif k == 4:
                    last = V.tensor_copy(PTc[SMP:EXT, 0, 0:GRP * META], B2[0:META, 0:GRP * META])
                else:
                    V.tensor_copy(diag_view(Pz, 0, GRP * DT), B2[:, 0:P].rearrange("p (s n) -> p s n", s=DB))
                    last = V.tensor_copy(PnT[0:SMP, :], B2[0:SMP, P:2 * P])
                last.then_inc(pt_kept, 1)

            def batch_scale(i, k):
                b = k % 2
                dve.wait_ge(pv_done, 6 * i + k + 1)
                if k == 5:
                    last = TS(on[:, 1, 0:HD], B3[:, 0:HD], sm[:, 1, 24:25], None, ALU.mult)
                else:
                    n = P if k < 4 else META
                    r = sm[0:n, b, 24:28].unsqueeze(2).broadcast_to([n, GRP, HD])
                    last = TT(bank4(on[0:n, b, :], HD), bank4(B3[0:n], HD), r, ALU.mult)
                last.then_inc(on_ready, 1)

            def batch_gate(i, k):
                dve.wait_ge(ot_done, 6 * i + k + 1)
                if k < 5:
                    n = P if k < 4 else META
                    cols = COLS[k] if k < 4 else slice(SEQ + SMP, TOK)
                    o = O[:, ds(2 * i, 2), cols]
                    STT(out=o, in0=B3[:, 0:2 * n].rearrange("p (u n) -> p u n", u=2), scalar=0.5, in1=o, op0=ALU.mult,
                        op1=ALU.mult).then_inc(b_gated, 1)
                else:
                    x = B3[0:HD, 0:P].rearrange("p (s r t) -> p s r t", r=GRP, t=DT)
                    for r in range(GRP):
                        a = HD * (r % 2)
                        o = tile(O, 2 * i + r // 2)[a:a + HD, SEQ:SEQ + SMP].rearrange("p (s t) -> p s t", t=DT)
                        STT(out=o, in0=x[:, :, r, :], scalar=0.5, in1=o, op0=ALU.mult, op1=ALU.mult).then_inc(b_gated, 1)

            def group_step(i, g):
                att_, proj = i is not None, g is not None

                def unit(j):
                    if proj:
                        gate(tile(O, 2 * g + j), THb, j, (pp_free[j % 2], 8 + SWA // 2 + 2 * g + 1))

                def run(*steps):
                    if att_:
                        for f, k in steps:
                            f(i, k)

                if att_:
                    for b in range(2):
                        dve.wait_ge(pp_free[b], 8 + SWA // 2 + 2 * i + 2)
                    dve.wait_ge(gate_done, 4 * HEADS + 2 * i + 2)
                    spread_q(i)
                for n in range(9):
                    if n >= 3:
                        run((batch_gate, n - 3))
                    if n < 6:
                        run((batch_max, n))
                    if n in (1, 3):
                        unit(n // 2)
                    if 2 <= n < 8:
                        run((batch_scale, n - 2))
                    if 1 <= n < 7:
                        run((batch_keep, n - 1))
                    if n < 8 and proj:
                        at = group_unit_at(g, n // 2 + 1)
                        if n % 2 == 0:
                            unit_scale(at, n // 2 + 1, 2)
                        unit_low(at, n // 2 + 1, (n % 2,))

            group_step(None, 0)
            with dve.Fori(0, KV - 1) as i:
                group_step(i, i + 1)
            group_step(KV - 1, None)

            def keep_rows(i, j):
                n4 = 4 * i + j
                dve.wait_ge(yt_done, n4 + 1)
                a, b = ((B0, B2), (B1, B3))[j % 2]
                V.tensor_copy(YR[:, 0:NT, ds(n4 * P, P)], bank4(a)).then_inc(y_kept, 1)
                V.tensor_copy(YR[0:EXT, NT, ds(n4 * P, P)], b[0:EXT, 0:P]).then_inc(y_kept, 1)

            dve.wait_ge(o_summed, KV)
            V.tensor_reduce(out_fix[:, 0:1], OS[:], AX.X, ALU.add).then_inc(os_ready, 1)
            dve.wait_ge(os_done, 1)
            t = Tally(os_step)
            x, half, guess = (step[:, k, 0:1] for k in range(3))
            scale_of(out_fix[:, 1:2], B2[:, 0:1], x, half, guess, W_MAX, t)
            t.link(dve, V.reciprocal(out_fix[:, 2:3], out_fix[:, 1:2]))
            t.link(dve, TS(undo[:, 0, 1:4], undo[:, 0, 1:4], 0.0, out_fix[:, 2:3], ALU.mult, ALU.add))
            t.link(dve, TT(out_fix[:, 3:4], out_fix[:, 2:3], GS[:, 2:3], ALU.mult))
            t.link(dve, TS(SCL[:, 0, 1:4], SCL[:, 0, 1:4], out_fix[:, 3:4], None, ALU.mult))
            for n in range(NK + 1):
                if n < NK:
                    dve.wait_ge(h_ready, 3 * NK + n - 3)
                    TS(to[:, n % 4, :], O[:, n, :], out_fix[:, 1:2], None, ALU.mult).then_inc(t_ready_x, 1)
                if n:
                    x_low(O, to[:, (n - 1) % 4, :], n - 1, 3 * NK)

            def out_tiles(i, more=True):
                for j in range(4):
                    if j < 3 or more:
                        unit_scale(out_unit_at(i, j + 1), j + 1, 0)
                        unit_low(out_unit_at(i, j + 1), j + 1)
                    dve.wait_ge(proj_done, NK + OUT_B + 4 * i + j + 1)
                    dve.wait_ge(xs_in[j], 16 * (i + 1))
                    if j >= 2 or not first(i):
                        dve.wait_ge(xg_ready, 4 * i + j - 1)
                    STT(out=halves(x2[:, j % 2, :]), in0=PV(j), scalar=unscale(j), in1=halves(xs[:, j, :]), op0=ALU.mult,
                        op1=ALU.add).then_inc(pp_free[j % 2], 1)
                    if j or not first(i):
                        keep_rows(i, j - 1)

            out_tiles(0)
            with dve.Fori(1, NK // 4 - 1) as i:
                out_tiles(i)
            out_tiles(NK // 4 - 1, False)
            keep_rows(NK // 4 - 1, 3)
            dve.wait_ge(ms_done, 2)
            TS(ms_c[:, 0:NT], B0[:, 0:2 * NT:2], 1.0 / DM, EPS, ALU.mult, ALU.add)
            cn.link(dve, TS(ms_c[0:EXT, NT:NT + 1], B0[0:EXT, 2 * NT:2 * NT + 1], 1.0 / DM, EPS, ALU.mult, ALU.add))
            dve.wait_ge(n_act, 4)
            newton(rs_c, ms_c, nt_c, cn)
            dve.wait_ge(y_kept, 2 * NK)
            for t in (0, 2, 4):
                n = WID[t]
                TS(YR[0:n, t, :], YR[0:n, t, :], rs_c[0:n, t:t + 1], None, ALU.mult).then_inc(y_scaled_v, 1)

        @block.gpsimd
        def _(pool):
            G = nc.gpsimd
            G.memset(acc[:], 0.0).then_inc(acc_zero, 1)
            gk = I["w_gk2_a"][0]
            G.dma_start(gk2[0:RANK, :], gk[:, 0:DK]).then_inc(gk2_in, 16)

            def load_state(h, s):
                src = I["state_gla"][0, s].rearrange("h (k p) v -> h p k v", p=P)
                src = src[h] if isinstance(h, int) else src[ds(h, 1)].rearrange("h p k v -> (h p) k v")
                alone(pool)
                G.dma_start(S0[:, s % SR, :, :], src).then_inc(s0_in[s % SR], 16)

            def store_state(h, s):
                dst = OUTS[3][0, s].rearrange("h (k p) v -> h p k v", p=P)
                dst = dst[h] if isinstance(h, int) else dst[ds(h, 1)].rearrange("h p k v -> (h p) k v")
                alone(pool)
                G.dma_start(dst, S0[:, s % SR, :, :]).then_inc(s0_out[s % SR], 16)

            for s in range(SR):
                load_state(0, s)
            for n in range(NK):
                pool.wait_ge(pp_free[n % 2], n // 2 + 1)
                alone(pool)
                G.dma_start(x0T[n], xt[:, n % 2, :]).then_inc(x0_out[n % 2], 16)
            for b in range(2):
                pool.wait_ge(x0_out[b], 8 * NK)

            def own_keys(i, s):
                if s >= 2:
                    pool.wait_ge(smp_u, 2 * DB * i + 2 * s - 2)
                alone(pool)
                G.tensor_scalar(kdm[0:SMP, s % 2, :], kdX[0:SMP, :], C("seq_of", 0, SMP)[:, s:s + 1], None,
                                ALU.mult).then_inc(kdm_ready, 1)

            def head_step(i, more):
                if more:
                    pool.wait_ge(proj_done, NK + USES * i + 10)
                    alone(pool)
                    G.dma_start(gk2[0:RANK, :], gk[:, ds(DK * (i + 1), DK)]).then_inc(gk2_in, 16)
                pool.wait_ge(vn_kept, 4 * i + 4)
                alone(pool)
                G.tensor_copy(Vs[0:SMP, :], Vx[0:SMP, :]).then_inc(vs_ready, 1)
                pool.wait_ge(kdt_ready, 3 * i + 3)
                own_keys(i, 0)
                own_keys(i, 1)
                pool.wait_ge(s_ready, 10 * i + 10)
                dst = OUTS[2][0, 0].rearrange("h (k p) v -> h p k v", p=P)
                dst = dst[i] if isinstance(i, int) else dst[ds(i, 1)].rearrange("h p k v -> (h p) k v")
                alone(pool)
                G.dma_start(dst, S[:, :, :]).then_inc(state_out, 16)
                for s in range(DB):
                    if s >= 2:
                        own_keys(i, s)
                    pool.wait_ge(smp_new, 2 * DB * i + 2 * s + 2)
                    store_state(i, s)
                    if 1 <= s <= SR:
                        pool.wait_ge(s0_out[s - 1], 16 * (2 * i + 1))
                        load_state(i, s - 1 + SR)
                for s in range(SR):
                    pool.wait_ge(s0_out[s], 16 * (2 * i + 2))
                    if more:
                        load_state(i + 1, s)

            with pool.Fori(0, HEADS - 1) as i:
                head_step(i, True)
            pool.wait_ge(proj_done, NK + OUT_A)
            for m in range(4):
                G.dma_start(H[:, 4 * m:4 * m + 4, :], x0T[4 * m:4 * m + 4].rearrange("n p t -> p n t")).then_inc(h_in[m], 16)
            head_step(HEADS - 1, False)

            pool.wait_ge(acc_zero, 1)
            pool.wait_ge(o_gated, 5 * HEADS)
            pool.wait_ge(state_out, 16 * HEADS)

            def residual(base, src, dst, half):
                if src is not None:
                    for j in range(4):
                        alone(pool)
                        G.dma_start(xs[:, j, :], src[j]).then_inc(xs_in[j], 16)

                def body(i, more):
                    for j in range(4):
                        n = 4 * i + j
                        pool.wait_ge(pp_free[j % 2], 8 + half + 2 * i + j // 2 + 1)
                        if more and src is not None:
                            s_ = src[ds(n + 4, 1)].rearrange("a p n -> (a p) n")
                            alone(pool)
                            G.dma_start(xs[:, j, :], s_).then_inc(xs_in[j], 16)
                        if dst is not None:
                            d_ = dst[ds(n, 1)].rearrange("a p n -> (a p) n") if more else dst[n]
                            alone(pool)
                            G.dma_start(d_, tile(H, n)).then_inc(x1_out[j], 16)
                        pool.wait_ge(sq_a, base + n + 1)
                        if j or not more or base:
                            pool.wait_ge(acc_done, base + n) if not (isinstance(n, int) and base + n == 0) else None
                        else:
                            pool.wait_ge(acc_zero, 1)
                        G.tensor_tensor(acc[:], acc[:], sqa[:, j % 2, :], ALU.add).then_inc(acc_done, 1)
                    pool.wait_ge(acc_done, base + 4 * i + 4)

                with pool.Fori(0, NK // 4 - 1) as i:
                    body(i, True)
                body(NK // 4 - 1, False)

            residual(0, None, x1T, OUT_A2 // 2)
            pool.wait_ge(rb_ready, 2)
            G.memset(acc[:], 0.0).then_inc(acc_zero, 1)
            pool.wait_ge(acc_zero, 2)

            w = OUTS[6], OUTS[7]
            for c_, name in enumerate(("cache_k_win", "cache_v_win")):
                alone(pool)
                G.dma_start(w[c_][:, 0:P - DT], I[name][:, DT:P]).then_inc(win_out, 16)
            pool.wait_ge(vn_kept, 4 * HEADS + 4)
            pool.wait_ge(setup, 3)
            G.dma_start(Wm[P - META:P, :], Wx[SMP:EXT, :]).then_inc(vm_in, 16)
            G.dma_start(OUTS[5][0].rearrange("w k d -> w (k d)"), Wn[:, NT - 1, :]).then_inc(win_out, 16)
            for s in range(DB):
                alone(pool)
                G.dma_start(w[1][s, P - DT:P].rearrange("t k d -> t (k d)"),
                            Wx[DT * s:DT * (s + 1), :]).then_inc(win_out, 16)
            pool.wait_ge(kw_kept, 2)
            G.dma_start(OUTS[4][0].rearrange("w k d -> w (k d)"), kwin).then_inc(win_out, 16)
            for s in range(DB):
                alone(pool)
                G.dma_start(w[0][s, P - DT:P].rearrange("t k d -> t (k d)"),
                            kwx[DT * s:DT * (s + 1), :]).then_inc(win_out, 16)
            pool.wait_ge(vm_in, 16)

            def load_cache(g):
                for c_, (name, buf) in enumerate((("cache_k_win", Kc), ("cache_v_win", Vc))):
                    src = I[name].rearrange("b w k d -> w b k d")
                    if isinstance(g, int):
                        src = src[:, :, g, :]
                    else:
                        src = src[:, :, ds(g, 1), :].rearrange("w b k d -> w b (k d)")
                    alone(pool)
                    G.dma_start(buf[:, 0, :].rearrange("p (b d) -> p b d", b=DB), src).then_inc(kc_in[c_], 16)

            def stage(i, again):
                if again:
                    pool.wait_ge(sc_done, 6 * i - 1)
                alone(pool)
                G.tensor_copy(kg, tile(kdup, i)).then_inc(kg_ready, 1)
                if again:
                    pool.wait_ge(p_ready, 6 * i - 1)
                alone(pool)
                G.memset(bank4(Cc[:, 0, :])[:, :, 0:P - META], NEG).then_inc(c_fill, 1)
                if again:
                    pool.wait_ge(pv_done, 6 * i)
                alone(pool)
                G.tensor_copy(vg, Wn[:, :, ds(HD * i, HD)]).then_inc(stage_step, 1)
                pool.wait_ge(stage_step, 2 * i + 1)
                alone(pool)
                G.tensor_copy(vxg[0:EXT, :], Wx[0:EXT, ds(HD * i, HD)])
                alone(pool)
                G.tensor_copy(vmg[96:P, :], Wm[96:P, ds(HD * i, HD)]).then_inc(stage_step, 1)
                pool.wait_ge(stage_step, 2 * i + 2)
                src = tile(kdup, i)[0:HD, SEQ:SEQ + SMP].rearrange("p (s t) -> p s t", t=DT)
                alone(pool)
                G.tensor_copy(kcat[0:HD, :, P:P + DT], src).then_inc(staged, 1)
                load_cache(i)

            pool.wait_ge(h_ready, 3 * NK)
            stage(0, False)
            with pool.Fori(1, KV) as i:
                stage(i, True)
            pool.wait_ge(pv_done, 6 * KV)
            pool.wait_ge(b_gated, 9 * KV)
            pool.wait_ge(win_out, 16 * (2 + 1 + DB + 1 + DB))
            residual(NK, x1T, None, OUT_B // 2)
            for t, s_ in ((0, (y_scaled_v, 1)), (1, (y_scaled, 1)), (2, (y_scaled_v, 2)), (3, (y_scaled, 2))):
                pool.wait_ge(*s_)
                alone(pool)
                G.dma_start(OUTS[0][0, t * P:(t + 1) * P, :], YR[:, t, :]).then_inc(y_out, 16)
            pool.wait_ge(y_scaled_v, 3)
            G.dma_start(OUTS[1].rearrange("b t d -> (b t) d"), YR[0:SMP, NT, :]).then_inc(y_out, 16)
            pool.wait_ge(y_out, 80)


_INS = ['x_prompt', 'x_sample', 'state_gla', 'cache_k_win', 'cache_v_win', 'meta_tokens', 'norm_a', 'w_in_a', 'w_gk2_a',
        'b_gk2_a', 'onorm_a', 'w_out_a', 'norm_kv', 'w_kv', 'norm_b', 'w_in_b', 'sinks_b', 'w_out_b', 'norm_f']
_OUTS = [(1, SEQ, DM), (DB, DT, DM), (1, 1, HEADS, DK, DV), (1, DB, HEADS, DK, DV), (1, P, KV, HD), (1, P, KV, HD),
         (DB, P, KV, HD), (DB, P, KV, HD)]


def kernel(**inputs):
    import concourse.bacc as bacc
    from concourse.bass_utils import run_bass_kernel_spmd

    nc = bacc.Bacc("TRN2", target_bir_lowering=False, num_devices=1)
    arrays, ins = {}, {}
    for name in _INS:
        a = np.ascontiguousarray(inputs[name])
        arrays[f"in_{name}"] = a
        ins[name] = nc.dram_tensor(f"in_{name}", a.shape, mybir.dt.from_np(a.dtype), kind="ExternalInput").ap()
    table, _ = consts_array()
    arrays["in_consts"] = table
    ins["consts"] = nc.dram_tensor("in_consts", table.shape, FP32, kind="ExternalInput").ap()
    outs = [nc.dram_tensor(f"out_{n}", shape, FP32, kind="ExternalOutput").ap() for n, shape in enumerate(_OUTS)]
    yoco_kernel(nc, ins, outs)
    r = run_bass_kernel_spmd(nc, [arrays], core_ids=[0])
    return tuple(r.results[0][f"out_{n}"] for n in range(len(_OUTS)))
```
